# Optimizing a Trainium2 kernel written in Bass

```python
import math
import jax, jax.numpy as jnp
from jax import lax
import numpy as np

D_MODEL = 2048
BATCH = 1
SEQ = 256
DEPTH = 2

CHUNK = 64
Q_BLOCK = 128

N_EVEN = (DEPTH + 1) // 2
N_ODD = DEPTH // 2

FOX_HEADS = 8
FOX_HEAD_DIM = 128
FOX_WIDTH = FOX_HEADS * FOX_HEAD_DIM

LRU_WIDTH = 1024
LRU_BLOCKS = 8
LRU_CONV = 4
LRU_C = 8.0

SWA_Q_HEADS = 16
SWA_KV_HEADS = 2
SWA_HEAD_DIM = 64
SWA_WINDOW = 128

MLA_HEADS = 8
MLA_Q_RANK = 512
MLA_KV_RANK = 256
MLA_NOPE = 128
MLA_ROPE = 64
MLA_V = 128
ROPE_THETA = 10000.0

FFN_HIDDEN = -(-8 * D_MODEL // (3 * 256)) * 256

EVEN_IN = 3 * FOX_WIDTH + FOX_HEADS + 2 * LRU_WIDTH
EVEN_MIX = FOX_WIDTH + LRU_WIDTH
ODD_IN = SWA_Q_HEADS * SWA_HEAD_DIM + 2 * SWA_KV_HEADS * SWA_HEAD_DIM + MLA_Q_RANK + MLA_KV_RANK + MLA_ROPE
ODD_MIX = SWA_Q_HEADS * SWA_HEAD_DIM + MLA_HEADS * MLA_V

DEEPNORM_ALPHA = (2 * DEPTH) ** 0.25
DEEPNORM_BETA = (8 * DEPTH) ** -0.25
LN_EPS = 1e-5
RMS_EPS = 1e-6

kernel_name = 'hybrid_fox_rglru_swasink_mla_trunk'

def layer_norm(x, g, b):
    xf = x.astype(jnp.float32)
    mu = jnp.mean(xf, axis=-1, keepdims=True)
    var = jnp.mean(jnp.square(xf - mu), axis=-1, keepdims=True)
    return ((xf - mu) * lax.rsqrt(var + LN_EPS) * g.astype(jnp.float32) + b.astype(jnp.float32)).astype(x.dtype)

def rms_norm(x, g):
    xf = x.astype(jnp.float32)
    y = xf * lax.rsqrt(jnp.mean(jnp.square(xf), axis=-1, keepdims=True) + RMS_EPS)
    return (y * g.astype(jnp.float32)).astype(x.dtype)

def split_cols(z, sizes):
    offs = np.cumsum(sizes)[:-1].tolist()
    return jnp.split(z, offs, axis=-1)

def apply_rope(t, positions):
    r = t.shape[-1]
    inv_freq = ROPE_THETA ** (-jnp.arange(0, r, 2, dtype=jnp.float32) / r)
    ang = positions.astype(jnp.float32)[..., None] * inv_freq
    cos = jnp.cos(ang)[:, :, None, :]
    sin = jnp.sin(ang)[:, :, None, :]
    tf = t.astype(jnp.float32)
    t1, t2 = tf[..., : r // 2], tf[..., r // 2:]
    return jnp.concatenate([t1 * cos - t2 * sin, t1 * sin + t2 * cos], axis=-1).astype(t.dtype)

def block_swept_attention(q, k, v, scale, causal_unit, decay_cum=None):
    b, s_len, h, dk = q.shape
    nb = s_len // Q_BLOCK
    k_unit = jnp.arange(s_len) // causal_unit
    q_blocks = jnp.moveaxis(q.reshape(b, nb, Q_BLOCK, h, dk), 1, 0)
    xs = (jnp.arange(nb), q_blocks)
    if decay_cum is not None:
        d_keys = jnp.swapaxes(decay_cum, 1, 2)
        xs = xs + (jnp.moveaxis(decay_cum.reshape(b, nb, Q_BLOCK, h), 1, 0),)

    def one_block(args):
        blk, q_blk = args[0], args[1]
        s = jnp.einsum('bqhd,bkhd->bhqk', q_blk, k, preferred_element_type=jnp.float32) * scale
        if decay_cum is not None:
            d_q = jnp.swapaxes(args[2], 1, 2)
            s = s + (d_q[..., :, None] - d_keys[..., None, :])
        q_unit = (blk * Q_BLOCK + jnp.arange(Q_BLOCK)) // causal_unit
        s = jnp.where(k_unit[None, :] <= q_unit[:, None], s, -jnp.inf)
        p = jax.nn.softmax(s, axis=-1).astype(v.dtype)
        return jnp.einsum('bhqk,bkhd->bqhd', p, v)

    out = lax.map(one_block, xs)
    return jnp.moveaxis(out, 0, 1).reshape(b, s_len, h, v.shape[-1])

def sliding_window_sink_attention(q, k, v, sinks):
    b, s_len, hq, dh = q.shape
    hkv = k.shape[2]
    g = hq // hkv
    n = s_len // CHUNK
    wc = SWA_WINDOW // CHUNK
    qc = q.reshape(b, n, CHUNK, hkv, g, dh)

    def band(t):
        t = t.reshape(b, n, CHUNK, hkv, t.shape[-1])
        parts = []
        for j in range(wc - 1, -1, -1):
            pw = [(0, 0)] * t.ndim
            pw[1] = (j, 0)
            parts.append(jnp.pad(t, pw)[:, :n])
        return jnp.concatenate(parts, axis=2)

    kb, vb = band(k), band(v)
    s = jnp.einsum('bnqhgd,bnkhd->bnhgqk', qc, kb, preferred_element_type=jnp.float32) * (dh ** -0.5)
    key_chunk = jnp.arange(n)[:, None] + (jnp.arange(wc * CHUNK) // CHUNK - (wc - 1))[None, :]
    s = jnp.where((key_chunk >= 0)[None, :, None, None, None, :], s, -jnp.inf)
    sink = jnp.broadcast_to(sinks.astype(jnp.float32).reshape(1, 1, hkv, g, 1, 1), s.shape[:-1] + (1,))
    p = jax.nn.softmax(jnp.concatenate([s, sink], axis=-1), axis=-1)[..., :-1]
    out = jnp.einsum('bnhgqk,bnkhd->bnqhgd', p.astype(v.dtype), vb)
    return out.reshape(b, s_len, hq * dh)

def causal_depthwise_conv(u, w, bias):
    kw, c = w.shape
    y = lax.conv_general_dilated(u, w[:, None, :].astype(u.dtype), window_strides=(1,),
                                 padding=[(kw - 1, 0)], dimension_numbers=('NWC', 'WIO', 'NWC'),
                                 feature_group_count=c)
    return y + bias.astype(u.dtype)

def rg_lru(u, rgate_w, rgate_b, igate_w, igate_b, lam):
    b, s_len, c = u.shape
    uf = u.astype(jnp.float32)
    ub = uf.reshape(b, s_len, LRU_BLOCKS, c // LRU_BLOCKS)
    r = jax.nn.sigmoid(jnp.einsum('bsnc,ncd->bsnd', ub, rgate_w.astype(jnp.float32)).reshape(b, s_len, c) + rgate_b)
    i = jax.nn.sigmoid(jnp.einsum('bsnc,ncd->bsnd', ub, igate_w.astype(jnp.float32)).reshape(b, s_len, c) + igate_b)
    log_a = -LRU_C * r * jax.nn.softplus(-lam.astype(jnp.float32))
    a = jnp.exp(log_a)
    bt = jnp.sqrt(-jnp.expm1(2.0 * log_a)) * (i * uf)

    def combine(left, right):
        a1, b1 = left
        a2, b2 = right
        return a2 * a1, a2 * b1 + b2

    _, h = lax.associative_scan(combine, (a, bt), axis=1)
    return h.astype(u.dtype)

def even_mixer(x, w_in, forget_bias, conv_w, conv_b, rgate_w, rgate_b, igate_w, igate_b, lru_lambda, w_out):
    b, s_len, _ = x.shape
    q, k, v, f_logit, u, g = split_cols(x @ w_in, [FOX_WIDTH, FOX_WIDTH, FOX_WIDTH, FOX_HEADS, LRU_WIDTH, LRU_WIDTH])
    shp = (b, s_len, FOX_HEADS, FOX_HEAD_DIM)
    log_f = jax.nn.log_sigmoid(f_logit.astype(jnp.float32) + forget_bias.astype(jnp.float32))
    a_out = block_swept_attention(q.reshape(shp), k.reshape(shp), v.reshape(shp), FOX_HEAD_DIM ** -0.5, 1,
                                  jnp.cumsum(log_f, axis=1))
    h = rg_lru(causal_depthwise_conv(u, conv_w, conv_b), rgate_w, rgate_b, igate_w, igate_b, lru_lambda)
    b_out = h * jax.nn.gelu(g)
    return jnp.concatenate([a_out.reshape(b, s_len, FOX_WIDTH), b_out], axis=-1) @ w_out

def odd_mixer(x, positions, w_in, sinks, q_norm, w_qb, kv_norm, w_kvb, w_out):
    b, s_len, _ = x.shape
    qs, ks, vs, cq, ckv, kr = split_cols(x @ w_in, [SWA_Q_HEADS * SWA_HEAD_DIM, SWA_KV_HEADS * SWA_HEAD_DIM,
                                                    SWA_KV_HEADS * SWA_HEAD_DIM, MLA_Q_RANK, MLA_KV_RANK, MLA_ROPE])
    c_out = sliding_window_sink_attention(qs.reshape(b, s_len, SWA_Q_HEADS, SWA_HEAD_DIM),
                                          ks.reshape(b, s_len, SWA_KV_HEADS, SWA_HEAD_DIM),
                                          vs.reshape(b, s_len, SWA_KV_HEADS, SWA_HEAD_DIM), sinks)
    qd = (rms_norm(cq, q_norm) @ w_qb).reshape(b, s_len, MLA_HEADS, MLA_NOPE + MLA_ROPE)
    kv = (rms_norm(ckv, kv_norm) @ w_kvb).reshape(b, s_len, MLA_HEADS, MLA_NOPE + MLA_V)
    k_rope = apply_rope(kr[:, :, None, :], positions)
    qd = jnp.concatenate([qd[..., :MLA_NOPE], apply_rope(qd[..., MLA_NOPE:], positions)], axis=-1)
    kd = jnp.concatenate([kv[..., :MLA_NOPE], jnp.broadcast_to(k_rope, (b, s_len, MLA_HEADS, MLA_ROPE))], axis=-1)
    d_out = block_swept_attention(qd, kd, kv[..., MLA_NOPE:], (MLA_NOPE + MLA_ROPE) ** -0.5, CHUNK)
    return jnp.concatenate([c_out, d_out.reshape(b, s_len, MLA_HEADS * MLA_V)], axis=-1) @ w_out

def swiglu(x, w_gate, w_up, w_down):
    return (jax.nn.silu(x @ w_gate) * (x @ w_up)) @ w_down

def setup_inputs(seed: int = 0) -> dict:
    key = jax.random.key(seed)
    ks = iter(jax.random.split(key, 40))
    f32 = jnp.float32

    def nrm(shape, scale):
        return jax.random.normal(next(ks), shape, f32) * scale

    bw = LRU_WIDTH // LRU_BLOCKS
    lam_a = jax.random.uniform(next(ks), (N_EVEN, LRU_WIDTH), f32, 0.9, 0.999)
    return {
        'x': nrm((BATCH, SEQ, D_MODEL), 1.0),
        'positions': jnp.broadcast_to(jnp.arange(SEQ, dtype=jnp.int32), (BATCH, SEQ)),
        'ev_w_in': nrm((N_EVEN, D_MODEL, EVEN_IN), D_MODEL ** -0.5),
        'ev_forget_bias': jax.random.uniform(next(ks), (N_EVEN, FOX_HEADS), f32, 1.0, 6.0),
        'ev_conv_w': nrm((N_EVEN, LRU_CONV, LRU_WIDTH), LRU_CONV ** -0.5),
        'ev_conv_b': nrm((N_EVEN, LRU_WIDTH), 0.02),
        'ev_rgate_w': nrm((N_EVEN, LRU_BLOCKS, bw, bw), bw ** -0.5),
        'ev_rgate_b': nrm((N_EVEN, LRU_WIDTH), 0.02),
        'ev_igate_w': nrm((N_EVEN, LRU_BLOCKS, bw, bw), bw ** -0.5),
        'ev_igate_b': nrm((N_EVEN, LRU_WIDTH), 0.02),
        'ev_lru_lambda': jnp.log(lam_a) - jnp.log1p(-lam_a),
        'ev_w_out': nrm((N_EVEN, EVEN_MIX, D_MODEL), DEEPNORM_BETA * EVEN_MIX ** -0.5),
        'od_w_in': nrm((N_ODD, D_MODEL, ODD_IN), D_MODEL ** -0.5),
        'od_sinks': nrm((N_ODD, SWA_Q_HEADS), 0.5),
        'od_q_norm': 1.0 + nrm((N_ODD, MLA_Q_RANK), 0.02),
        'od_w_qb': nrm((N_ODD, MLA_Q_RANK, MLA_HEADS * (MLA_NOPE + MLA_ROPE)), MLA_Q_RANK ** -0.5),
        'od_kv_norm': 1.0 + nrm((N_ODD, MLA_KV_RANK), 0.02),
        'od_w_kvb': nrm((N_ODD, MLA_KV_RANK, MLA_HEADS * (MLA_NOPE + MLA_V)), MLA_KV_RANK ** -0.5),
        'od_w_out': nrm((N_ODD, ODD_MIX, D_MODEL), DEEPNORM_BETA * ODD_MIX ** -0.5),
        'ln_mix_g': 1.0 + nrm((DEPTH, D_MODEL), 0.02),
        'ln_mix_b': nrm((DEPTH, D_MODEL), 0.02),
        'ffn_w_gate': nrm((DEPTH, D_MODEL, FFN_HIDDEN), D_MODEL ** -0.5),
        'ffn_w_up': nrm((DEPTH, D_MODEL, FFN_HIDDEN), D_MODEL ** -0.5),
        'ffn_w_down': nrm((DEPTH, FFN_HIDDEN, D_MODEL), DEEPNORM_BETA * FFN_HIDDEN ** -0.5),
        'ln_ffn_g': 1.0 + nrm((DEPTH, D_MODEL), 0.02),
        'ln_ffn_b': nrm((DEPTH, D_MODEL), 0.02),
    }

def reference(x, positions, ev_w_in, ev_forget_bias, ev_conv_w, ev_conv_b, ev_rgate_w, ev_rgate_b,
              ev_igate_w, ev_igate_b, ev_lru_lambda, ev_w_out, od_w_in, od_sinks, od_q_norm, od_w_qb,
              od_kv_norm, od_w_kvb, od_w_out, ln_mix_g, ln_mix_b, ffn_w_gate, ffn_w_up, ffn_w_down,
              ln_ffn_g, ln_ffn_b):
    for layer in range(DEPTH):
        i = layer // 2
        if layer % 2 == 0:
            mix = even_mixer(x, ev_w_in[i], ev_forget_bias[i], ev_conv_w[i], ev_conv_b[i], ev_rgate_w[i],
                             ev_rgate_b[i], ev_igate_w[i], ev_igate_b[i], ev_lru_lambda[i], ev_w_out[i])
        else:
            mix = odd_mixer(x, positions, od_w_in[i], od_sinks[i], od_q_norm[i], od_w_qb[i],
                            od_kv_norm[i], od_w_kvb[i], od_w_out[i])
        x = layer_norm(DEEPNORM_ALPHA * x + mix, ln_mix_g[layer], ln_mix_b[layer])
        ffn = swiglu(x, ffn_w_gate[layer], ffn_w_up[layer], ffn_w_down[layer])
        x = layer_norm(DEEPNORM_ALPHA * x + ffn, ln_ffn_g[layer], ln_ffn_b[layer])
    return x


_drawn_inputs = setup_inputs


def setup_inputs(seed=0):
    import zlib

    import numpy as np

    out = dict(_drawn_inputs(seed))
    spreads = {}
    factors = {'ev_conv_b': 7.738,
     'ev_rgate_b': 8.0,
     'ev_igate_b': 8.0,
     'od_sinks': 8.0,
     'od_q_norm': 8.0,
     'od_kv_norm': 8.0}
    for name, (base, spread) in spreads.items():
        noise = np.random.default_rng([zlib.crc32(name.encode()), seed]).standard_normal(out[name].shape)
        drawn = base * np.exp(spread * noise) if base else spread * noise
        out[name] = __import__('jax').numpy.asarray(drawn.astype(out[name].dtype))
    for name, factor in factors.items():
        out[name] = (out[name] * factor).astype(out[name].dtype)
    return out
```

```python
from contextlib import ExitStack
import math

import concourse.bass as bass
from concourse import mybir

ALU = mybir.AluOpType
ACT = mybir.ActivationFunctionType
AX = mybir.AxisListType
F32 = mybir.dt.float32
F32R = mybir.dt.float32r
I32 = mybir.dt.int32

P = 128
T = 256
TT = T // P
D = 2048
KD = D // P
COLS = 512
UK = 2
SLOTS = 4
UNIT = UK * COLS
UPB = KD // UK

FOX_HEADS, FOX_W = 8, 1024
LRU_W, LRU_B, CONV = 1024, 8, 4
LRU_C = 8.0
SWA_Q, SWA_KV, SWA_DH = 16, 2, 64
MLA_H, QR_RANK, KV_RANK, NOPE, ROPE, MLA_V = 8, 512, 256, 128, 64, 128
THETA = 10000.0
FFN = 5632
KF = FFN // P
ALPHA = 4.0 ** 0.25
LN_EPS, RMS_EPS = 1e-5, 1e-6
NEG = -1.0e30

FFN_BLOCKS = FFN // COLS
DOWN_UNITS = KF // UK
STREAM = [
    ("e_u", 2 * UPB, 2), ("e_g", 2 * UPB, 2), ("e_q", 2 * UPB, 2), ("e_k", 2 * UPB, 2), ("e_v", 2 * UPB, 2),
    ("e_out", 4 * UPB, 4), ("gu0", 2 * UPB * FFN_BLOCKS, 2 * FFN_BLOCKS), ("down0", 4 * DOWN_UNITS, 4),
    ("o_q", 2 * UPB, 2), ("o_kv", UPB, 1), ("o_cq", UPB, 1), ("o_ckv", UPB, 1),
    ("qb_nope", 4, 2), ("qb_rope", 4, 1), ("kvb", 4, 4),
    ("o_out", 4 * UPB, 4), ("gu1", 2 * UPB * FFN_BLOCKS, 2 * FFN_BLOCKS), ("down1", 4 * DOWN_UNITS, 4),
]
UNIT0, BLOCK0, BLOCK_END = {}, {}, []
_u = _b = 0
for _name, _nu, _nb in STREAM:
    UNIT0[_name], BLOCK0[_name] = _u, _b
    BLOCK_END += [_u + (_nu if _name == "qb_nope" else (_k + 1) * _nu // _nb) for _k in range(_nb)]
    _u, _b = _u + _nu, _b + _nb
UNITS = _u

TR_STEPS = [("x", 8), ("ln0", 8), ("gu0", 2 * FFN_BLOCKS), ("ln1", 8), ("kswa", 1), ("rms", 3), ("rope", 3),
            ("ln2", 8), ("gu1", 2 * FFN_BLOCKS)]
TR0, HI0 = {}, {}
_n = _h = 0
for _name, _c in TR_STEPS:
    TR0[_name], HI0[_name] = _n, _h
    _n += _c
    _h += 0 if _name in ("kswa", "rope") else _c

LOG1P_TERMS = 9


def hybrid_trunk_kernel(
    nc: bass.Bass, x, positions, ev_w_in, ev_forget_bias, ev_conv_w, ev_conv_b, ev_rgate_w, ev_rgate_b,
    ev_igate_w, ev_igate_b, ev_lru_lambda, ev_w_out, od_w_in, od_sinks, od_q_norm, od_w_qb, od_kv_norm,
    od_w_kvb, od_w_out, ln_mix_g, ln_mix_b, ffn_w_gate, ffn_w_up, ffn_w_down, ln_ffn_g, ln_ffn_b, out,
):
    ctx = ExitStack()
    with ctx:
        base = (nc.sbuf_base + 63) // 64 * 64
        top = [base]

        def place(name, shape, dt, at=None):
            size = 4
            for s in shape[1:]:
                size *= s
            off = top[0] if at is None else at
            if at is None:
                top[0] = off + (size + 31) // 32 * 32
            return nc.alloc_sbuf_tensor_at(name, shape, dt, offset=off)

        xTh = place("xTh", [P, KD, T], F32R)
        xTl = place("xTl", [P, KD, T], F32R)
        xres = place("xres", [P, TT, D], F32)
        raw = place("raw", [P, SLOTS, UNIT], F32)
        whi = place("whi", [P, SLOTS, UNIT], F32R)
        wlo = place("wlo", [P, SLOTS, UNIT], F32R)
        ident = place("ident", [P, P], F32)
        stats = place("stats", [P, TT, 4, 6], F32)
        mv = place("mv", [P, TT, 2], F32)
        lnv = place("lnv", [P, 4, TT], F32)
        g0 = top[0]
        gb = place("gb", [P, 2, D], F32)
        sg = place("sg", [P, TT, COLS], F32, g0)
        hbuf = place("hbuf", [P, TT, COLS], F32, g0 + 4 * TT * COLS)
        nlf = place("nlf", [P, TT, FOX_HEADS, P], F32, g0)
        rgd = place("rgd", [P, LRU_B, T], F32, g0 + 4 * TT * FOX_HEADS * P)
        m0 = top[0]
        hTh = place("hTh", [P, KF, T], F32R)
        hTl = place("hTl", [P, KF, T], F32R)
        end = top[0]
        assert end <= nc.sbuf_usable_end, (end, nc.sbuf_usable_end)

        top[0] = m0
        s_sb = place("s_sb", [P, 2, 2, T], F32)
        p_sb = place("p_sb", [P, 2, 2, T], F32)
        pT = place("pT", [P, 2, 4, P], F32)
        nm = place("nm", [P, 2, 2], F32)
        mx = place("mx", [P, 2, 2], F32)
        lsum = place("lsum", [P, 2, 2], F32)
        rl = place("rl", [P, 2, 2], F32)
        es = place("es", [P, 2, 2], F32)
        mix0 = top[0]
        qT = place("qT", [P, 8, T], F32)
        kT = place("kT", [P, 8, T], F32)
        vt = place("vt", [P, TT, FOX_W], F32)
        uT = place("uT", [P, LRU_B, T + CONV - 1], F32)
        gT = place("gT", [P, LRU_B, T], F32)
        uc = place("uc", [P, LRU_B, T], F32)
        rt = place("rt", [P, LRU_B, T], F32)
        it = place("it", [P, LRU_B, T], F32)
        rw = place("rw", [P, LRU_B, P], F32)
        iw = place("iw", [P, LRU_B, P], F32)
        cmask = place("cmask", [P, T], F32)
        tri = place("tri", [P, T], F32)
        wf = place("wf", [P, KD, FOX_HEADS], F32)
        wfh = place("wfh", [P, KD, FOX_HEADS], F32R)
        wfl = place("wfl", [P, KD, FOX_HEADS], F32R)
        fb = place("fb", [P, FOX_HEADS], F32)
        cw = place("cw", [P, CONV, LRU_B], F32)
        cols = place("cols", [P, 4, LRU_B], F32)
        clam = place("clam", [P, 2, LRU_B], F32)
        lz = place("lz", [P, 6, LRU_B], F32)
        fz = place("fz", [P, 7, TT * FOX_HEADS], F32)
        cq = place("cq", [P, TT, FOX_HEADS], F32)
        assert top[0] <= nc.sbuf_usable_end, (top[0], end)
        top[0] = mix0 + 4 * 8 * T
        qnT = place("qnT", [P, 8, T], F32)
        knT = place("knT", [P, 8, T], F32)
        qr = place("qr", [P, TT, 10, ROPE], F32)
        qro = place("qro", [P, TT, 10, ROPE], F32)
        rtmp = place("rtmp", [P, 10, ROPE // 2], F32)
        qrT = place("qrT", [P, 4, T], F32)
        krz = place("krz", [P, 2, T], F32)
        kvs = place("kvs", [P, TT, 2 * P], F32)
        kz = place("kz", [P, SWA_KV, 2, T], F32)
        vd = place("vd", [P, TT, SWA_KV, P], F32)
        cqs = place("cqs", [P, TT, QR_RANK], F32)
        ckvs = place("ckvs", [P, TT, KV_RANK], F32)
        cTh = place("cTh", [P, 6, T], F32R)
        cTl = place("cTl", [P, 6, T], F32R)
        vm = place("vm", [P, TT, MLA_H, MLA_V], F32)
        bmask = place("bmask", [P, T], F32)
        wmask = place("wmask", [P, T], F32)
        pos_i = place("pos_i", [P, TT], I32)
        pos = place("pos", [P, TT], F32)
        invf = place("invf", [P, ROPE // 2], F32)
        trig = place("trig", [P, 6, TT, ROPE // 2], F32)
        sinks = place("sinks", [P, SWA_Q], F32)
        qkg = place("qkg", [P, 6], F32)
        rms = place("rms", [P, 4, 2 * TT], F32)
        assert top[0] <= nc.sbuf_usable_end, (top[0], end)

        def bank(name):
            return ctx.enter_context(nc.psum_tensor(name, [P, COLS], F32))

        acc = [[bank(f"acc{p}{t}") for t in range(2)] for p in range(2)]
        misc = [bank(f"misc{n}") for n in range(4)]
        scb, trb = misc[0:2], misc[2:4]

        def sem(name):
            return ctx.enter_context(nc.semaphore(name))

        w_in = [sem(f"w_in{s}") for s in range(SLOTS)]
        w_hi = sem("w_hi")
        w_lo = sem("w_lo")
        w_used = sem("w_used")
        acc_free = [sem(f"acc_free{p}") for p in range(2)]
        tr_ready = sem("tr_ready")
        tr_hi = sem("tr_hi")
        tr_free = sem("tr_free")
        x_in = sem("x_in")
        y_ready = sem("y_ready")
        stats_done = sem("stats_done")
        ln_var = sem("ln_var")
        ln_sd = sem("ln_sd")
        gb_in = sem("gb_in")
        out_done = sem("out_done")
        dv = sem("dv")
        av = sem("av")
        pv = sem("pv")
        consts = sem("consts")
        ev_in = sem("ev_in")
        od_in = sem("od_in")
        conv_done = sem("conv_done")
        gates_ready = sem("gates_ready")
        gates_free = sem("gates_free")
        lam_e = sem("lam_e")
        lam_x = sem("lam_x")
        lam_done = sem("lam_done")
        rg_at = sem("rg_at")
        rg_var = sem("rg_var")
        rg_sq = sem("rg_sq")
        rg_out = sem("rg_out")
        rg_hi = sem("rg_hi")
        mix_tail = sem("mix_tail")
        wf_hi = sem("wf_hi")
        wf_split = sem("wf_split")
        f_ready = sem("f_ready")
        f_neg = sem("f_neg")
        f_exp = sem("f_exp")
        f_log = sem("f_log")
        f_rep = sem("f_rep")
        c_ready = sem("c_ready")
        c_done = sem("c_done")
        sc_ready = sem("sc_ready")
        nm_ready = sem("nm_ready")
        ex_ready = sem("ex_ready")
        pr_ready = sem("pr_ready")
        pt_ready = sem("pt_ready")
        pt_copied = sem("pt_copied")
        o_ready = sem("o_ready")
        o_hi = sem("o_hi")
        o_lo = sem("o_lo")
        od_prep = sem("od_prep")
        kv_copied = sem("kv_copied")
        sq_done = sem("sq_done")
        rms_var = sem("rms_var")
        rms_sd = sem("rms_sd")
        c_norm = sem("c_norm")
        ct_hi = sem("ct_hi")
        rope_in = sem("rope_in")
        rope_out = sem("rope_out")
        rope_T = sem("rope_T")
        trig_arg = sem("trig_arg")
        trig_done = sem("trig_done")

        block = ctx.enter_context(nc.Block())

        def at(unit, i=0, per=0):
            return unit % SLOTS, i * (per // SLOTS) + unit // SLOTS

        def number(u):
            return u[1] * SLOTS + u[0]

        def uses(b):
            return b // 2

        def fox_dst(unit):
            j, t = unit
            return [(slice(0, P), (2 * j, 2 * j + 2, t * P), slice(0, 2 * P))]

        def odd_dst(unit):
            kind, j, t = unit
            if kind == "mla":
                return [(slice(0, P), (8 + 2 * j, 8 + 2 * j + 2, t * P), slice(0, 2 * P))]
            return [(slice(g * 64, g * 64 + 64), (j, j + 1, t * P), slice(g * P, (g + 1) * P)) for g in range(2)]

        def wmat(w, l):
            return w[l].rearrange("(k p) n -> p k n", p=P)

        @block.sync
        def _(sp):
            def load(u, src, width=COLS, kts=UK):
                slot, rounds = u
                if not (isinstance(rounds, int) and rounds == 0):
                    sp.wait_ge(w_lo, number(u) - SLOTS + 1)
                dst = raw[:, slot, 0:kts * width].rearrange("p (k n) -> p k n", k=kts)
                sp.dma_start(dst, src).then_inc(w_in[slot], 16)

            for t in range(TT):
                sp.dma_start(xres[:, t, :], x[0, t * P:(t + 1) * P, :]).then_inc(x_in, 16)

            ev_in_w = wmat(ev_w_in, 0)
            f0 = 3 * FOX_W
            for name, c0 in (("e_u", f0 + FOX_HEADS), ("e_g", f0 + FOX_HEADS + LRU_W),
                             ("e_q", 0), ("e_k", FOX_W), ("e_v", 2 * FOX_W)):
                for b in range(2):
                    for j in range(UPB):
                        load(at(UNIT0[name] + b * UPB + j),
                             ev_in_w[:, j * UK:(j + 1) * UK, c0 + b * COLS:c0 + (b + 1) * COLS])

            def square(name, w):
                with sp.Fori(0, 2) as i:
                    for b in range(2):
                        for j in range(UPB):
                            load(at(UNIT0[name] + b * UPB + j, i, 2 * UPB),
                                 w[:, j * UK:(j + 1) * UK, bass.ds(i * (2 * COLS) + b * COLS, COLS)])

            def ffn(l):
                gate, up, down = wmat(ffn_w_gate, l), wmat(ffn_w_up, l), wmat(ffn_w_down, l)
                with sp.Fori(0, FFN_BLOCKS) as i:
                    for b, w in enumerate((gate, up)):
                        for j in range(UPB):
                            load(at(UNIT0[f"gu{l}"] + b * UPB + j, i, 2 * UPB),
                                 w[:, j * UK:(j + 1) * UK, bass.ds(i * COLS, COLS)])
                with sp.Fori(0, 2) as i:
                    for b in range(2):
                        for j in range(DOWN_UNITS):
                            load(at(UNIT0[f"down{l}"] + b * DOWN_UNITS + j, i, 2 * DOWN_UNITS),
                                 down[:, j * UK:(j + 1) * UK, bass.ds(i * (2 * COLS) + b * COLS, COLS)])

            square("e_out", wmat(ev_w_out, 0))
            ffn(0)
            w = wmat(od_w_in, 0)
            for b in range(2):
                for j in range(UPB):
                    load(at(UNIT0["o_q"] + b * UPB + j), w[:, j * UK:(j + 1) * UK, b * COLS:(b + 1) * COLS])
            c0 = SWA_Q * SWA_DH
            for name, width in (("o_kv", 2 * SWA_KV * SWA_DH), ("o_cq", QR_RANK), ("o_ckv", KV_RANK + ROPE)):
                for j in range(UPB):
                    load(at(UNIT0[name] + j), w[:, j * UK:(j + 1) * UK, c0:c0 + width], width)
                c0 += width
            qb = wmat(od_w_qb, 0)
            hw = NOPE + ROPE

            def load_heads(u, k, off, width):
                slot = u[0]
                sp.wait_ge(w_lo, number(u) - SLOTS + 1)
                src = qb[:, k, :].rearrange("p (h n) -> p h n", n=hw)[:, :, off:off + width]
                sp.dma_start(raw[:, slot, 0:MLA_H * width].rearrange("p (h n) -> p h n", n=width),
                             src).then_inc(w_in[slot], 16)

            for k in range(QR_RANK // P):
                load_heads(at(UNIT0["qb_nope"] + k), k, 0, NOPE)
            for k in range(QR_RANK // P):
                load_heads(at(UNIT0["qb_rope"] + k), k, NOPE, ROPE)
            kvb = wmat(od_w_kvb, 0)
            for b in range(4):
                load(at(UNIT0["kvb"] + b), kvb[:, :, b * COLS:(b + 1) * COLS])
            square("o_out", wmat(od_w_out, 0))
            ffn(1)
            for n in range(8):
                t, c = n // 4, n % 4
                sp.wait_ge(y_ready, 3 * 8 + n + 1)
                sp.dma_start(out[0, t * P:(t + 1) * P, c * COLS:(c + 1) * COLS],
                             xres[:, t, c * COLS:(c + 1) * COLS]).then_inc(out_done, 16)
            sp.wait_ge(out_done, 8 * 16)

        @block.gpsimd
        def _(pool):
            chain = [0]

            def link(ins):
                chain[0] += 1
                ins.then_inc(pv, 1)
                pool.wait_ge(pv, chain[0])

            link(pool.memset(ident[:], 0.0))
            link(pool.affine_select(out=ident[:], in_=ident[:], compare_op=ALU.not_equal, fill=1.0, base=0,
                                    pattern=[[-1, P]], channel_multiplier=1))
            link(pool.memset(uT[:, :, 0:CONV - 1], 0.0))
            link(pool.memset(cmask[:], 0.0))
            link(pool.memset(tri[:], 1.0))
            link(pool.affine_select(out=cmask[:, P:T], in_=cmask[:, P:T], compare_op=ALU.is_ge, fill=NEG, base=0,
                                    pattern=[[-1, P]], channel_multiplier=1))
            link(pool.affine_select(out=tri[:, 0:P], in_=tri[:, 0:P], compare_op=ALU.is_ge, fill=0.0, base=0,
                                    pattern=[[1, P]], channel_multiplier=-1))
            pool.sem_inc(consts, 1)
            f0 = 3 * FOX_W
            vec = lambda w: w[0].rearrange("(n p) -> p n", p=P)
            for dst, src in (
                (wf[:], ev_w_in[0].rearrange("(k p) n -> p k n", p=P)[:, :, f0:f0 + FOX_HEADS]),
                (fb[:], ev_forget_bias[0:1, :].broadcast_to([P, FOX_HEADS])),
                (cols[:, 3, :], vec(ev_lru_lambda)),
                (cols[:, 0, :], vec(ev_conv_b)),
                (cols[:, 1, :], vec(ev_rgate_b)),
                (cols[:, 2, :], vec(ev_igate_b)),
                (cw[:, 0, :], ev_conv_w[0, 0].rearrange("(n p) -> p n", p=P)),
                (cw[:, 1, :], ev_conv_w[0, 1].rearrange("(n p) -> p n", p=P)),
                (cw[:, 2, :], ev_conv_w[0, 2].rearrange("(n p) -> p n", p=P)),
                (cw[:, 3, :], ev_conv_w[0, 3].rearrange("(n p) -> p n", p=P)),
                (rw[:], ev_rgate_w[0].rearrange("n c d -> c n d")),
                (iw[:], ev_igate_w[0].rearrange("n c d -> c n d")),
            ):
                pool.dma_start(dst, src, allow_slow_non_contiguous=True).then_inc(ev_in, 16)

            def gains(g, b, l):
                pool.dma_start(gb[:, 0, :], g[l:l + 1, :].broadcast_to([P, D])).then_inc(gb_in, 16)
                pool.dma_start(gb[:, 1, :], b[l:l + 1, :].broadcast_to([P, D])).then_inc(gb_in, 16)

            pool.wait_ge(o_ready, 8)
            pool.wait_ge(mix_tail, 1)
            gains(ln_mix_g, ln_mix_b, 0)
            pool.wait_ge(tr_ready, TR0["gu0"] + 2 * FFN_BLOCKS)
            gains(ln_ffn_g, ln_ffn_b, 0)
            pool.wait_ge(w_used, BLOCK_END[BLOCK0["down0"] + 3])
            link(pool.memset(bmask[:], 0.0))
            link(pool.memset(bmask[0:64, P + 64:T], NEG))
            link(pool.memset(wmask[:], 0.0))
            link(pool.memset(wmask[0:64, 0:64], NEG))
            link(pool.memset(wmask[0:64, P + 64:T], NEG))
            link(pool.memset(wmask[64:P, 0:P], NEG))
            link(pool.memset(kz[:], 0.0))
            link(pool.memset(krz[:], 0.0))
            for n in range(ROPE // 2):
                link(pool.memset(invf[:, n:n + 1], float(THETA ** (-2.0 * n / ROPE))))
            pool.sem_inc(consts, 1)
            for dst, src in (
                (pos_i[:], positions.rearrange("b (t p) -> p (b t)", p=P)),
                (sinks[:], od_sinks[0:1, :].broadcast_to([P, SWA_Q])),
                (qkg[:, 0:4], vec(od_q_norm)),
                (qkg[:, 4:6], vec(od_kv_norm)),
            ):
                pool.dma_start(dst, src, allow_slow_non_contiguous=True).then_inc(od_in, 16)
            pool.wait_ge(y_ready, 16)
            gains(ln_mix_g, ln_mix_b, 1)
            pool.wait_ge(tr_ready, TR0["gu1"] + 2 * FFN_BLOCKS)
            gains(ln_ffn_g, ln_ffn_b, 1)

        @block.tensor
        def _(pe):
            mm = nc.tensor.matmul

            def unit_ready(u):
                pe.wait_ge(w_lo, number(u) + 1)

            def rows_unit(u, pair, k0, first, last, src=(xTh, xTl), width=COLS, kts=UK):
                unit_ready(u)
                s = u[0]
                for kk in range(kts):
                    wh, wl = (w[:, s, kk * width:(kk + 1) * width] for w in (whi, wlo))
                    for t in range(TT):
                        xh, xl = (a[:, k0 + kk, t * P:(t + 1) * P] for a in src)
                        o = acc[pair][t][:, 0:width]
                        mm(o, xh, wh, start=first and kk == 0, stop=False)
                        mm(o, xh, wl, start=False, stop=False)
                        ins = mm(o, xl, wh, start=False, stop=last and kk == kts - 1)
                ins.then_inc(w_used, 1)

            def cols_unit(u, pair, k0, first, last, src=(xTh, xTl)):
                unit_ready(u)
                s = u[0]
                for kk in range(UK):
                    for c in range(4):
                        wh, wl = (w[:, s, kk * COLS + c * P:kk * COLS + (c + 1) * P] for w in (whi, wlo))
                        xh, xl = (a[:, k0 + kk, :] for a in src)
                        o = acc[pair][c // 2][:, (c % 2) * T:(c % 2 + 1) * T]
                        mm(o, wh, xh, start=first and kk == 0 and c % 2 == 0, stop=False, skip_group_check=True)
                        mm(o, wl, xh, start=False, stop=False, skip_group_check=True)
                        ins = mm(o, wh, xl, start=False, stop=last and kk == UK - 1, skip_group_check=True)
                ins.then_inc(w_used, 1)

            def open_block(b, i=0, per=0):
                before = uses(b) + i * (per // 2)
                if not (isinstance(before, int) and before == 0):
                    pe.wait_ge(acc_free[b % 2], before)

            def block_of(unit_fn, u0, b, n_units=UPB, i=0, per_u=0, per_b=0, after=None, **kw):
                open_block(b, i, per_b)
                for j in range(n_units):
                    unit_fn(at(u0 + j, i, per_u), b % 2, j * UK, j == 0, j == n_units - 1, **kw)
                    if after:
                        after(j)

            def transposes(n, parts, parity=None):
                if not (isinstance(n, int) and n < 2):
                    pe.wait_ge(tr_free, n - 1)
                dst = trb[n % 2 if parity is None else parity]
                for q, src in enumerate(parts):
                    ins = nc.tensor.transpose(dst[:, q * P:(q + 1) * P], src, ident[:])
                ins.then_inc(tr_ready, 1)

            def stream_transposes(n0, y0):
                for n in range(8):
                    t, c = n % 2, n // 2
                    if y0 is not None:
                        pe.wait_ge(y_ready, y0 + n + 1)
                    transposes(n0 + n, [xres[:, t, (4 * c + q) * P:(4 * c + q + 1) * P] for q in range(4)])
                pe.wait_ge(tr_free, n0 + 8)

            pe.wait_ge(x_in, 32)
            pe.wait_ge(consts, 1)
            stream_transposes(TR0["x"], None)

            pe.wait_ge(wf_split, 1)
            for t in range(TT):
                o = scb[0][:, t * FOX_HEADS:(t + 1) * FOX_HEADS]
                for k in range(KD):
                    xh, xl = (a[:, k, t * P:(t + 1) * P] for a in (xTh, xTl))
                    mm(o, xh, wfh[:, k, :], start=k == 0, stop=False)
                    mm(o, xh, wfl[:, k, :], start=False, stop=False)
                    ins = mm(o, xl, wfh[:, k, :], start=False, stop=k == KD - 1)
            ins.then_inc(f_ready, 1)

            for name in ("e_u", "e_g"):
                for b in range(2):
                    block_of(cols_unit, UNIT0[name] + b * UPB, BLOCK0[name] + b)
            pe.wait_ge(f_log, 1)
            lf = fz[:, 6, :].rearrange("p (t h) -> p t h", t=TT)
            mm(scb[1][:, 0:8], tri[:, 0:P], lf[:, 0, :], start=True, stop=True)
            mm(scb[1][:, 8:16], tri[:, P:T], lf[:, 0, :], start=True, stop=False)
            mm(scb[1][:, 8:16], tri[:, 0:P], lf[:, 1, :], start=False, stop=True).then_inc(c_ready, 1)
            for b in range(2):
                block_of(cols_unit, UNIT0["e_q"] + b * UPB, BLOCK0["e_q"] + b)

            def gates(n):
                pe.wait_ge(conv_done, n + 1)
                if n == 0:
                    pe.wait_ge(c_done, 1)
                    pe.wait_ge(ev_in, 12 * 16)
                if n >= 2:
                    pe.wait_ge(gates_free, n - 1)
                mm(scb[n % 2][:, 0:T], rw[:, n, :], uc[:, n, :], start=True, stop=True)
                mm(scb[n % 2][:, T:2 * T], iw[:, n, :], uc[:, n, :], start=True, stop=True).then_inc(gates_ready, 1)

            block_of(cols_unit, UNIT0["e_k"], BLOCK0["e_k"], after=gates)
            block_of(cols_unit, UNIT0["e_k"] + UPB, BLOCK0["e_k"] + 1)
            for b in range(2):
                block_of(rows_unit, UNIT0["e_v"] + b * UPB, BLOCK0["e_v"] + b)

            def attention(n0, units, scores, values):
                N = len(units)
                for s in range(N + 3):
                    if s < N:
                        n = n0 + s
                        j, t = units[s][-2:]
                        if s >= 2:
                            pe.wait_ge(nm_ready, n - 1)
                        scores(units[s], scb[n % 2], (t + 1) * P)
                    if 2 <= s < N + 2:
                        n = n0 + s - 2
                        j, t = units[s - 2][-2:]
                        pe.wait_ge(pr_ready, n + 1)
                        if s >= 4:
                            pe.wait_ge(pt_copied, n - 1)
                        for g in range(2):
                            for k in range(t + 1):
                                q = g * (t + 1) + k
                                ins = nc.tensor.transpose(acc[1][n % 2][:, q * P:(q + 1) * P],
                                                          p_sb[:, n % 2, g, k * P:(k + 1) * P], ident[:])
                        ins.then_inc(pt_ready, 1)
                    if s >= 3:
                        n = n0 + s - 3
                        j, t = units[s - 3][-2:]
                        pe.wait_ge(pt_copied, n + 1)
                        if s >= 5:
                            pe.wait_ge(o_lo, n - 1)
                        for g in range(2):
                            for k in range(t + 1):
                                ins = mm(acc[0][n % 2][:, g * P:(g + 1) * P], values(units[s - 3], g, k),
                                         pT[:, n % 2, g * (t + 1) + k, :], start=k == 0, stop=k == t)
                        ins.then_inc(o_ready, 1)

            pe.wait_ge(f_rep, 1)
            pe.wait_ge(gates_free, 8)
            pe.wait_ge(acc_free[0], uses(BLOCK0["e_out"]))
            pe.wait_ge(acc_free[1], uses(BLOCK0["e_out"]))
            FOX = [(j, t) for j in range(4) for t in range(2)]

            def fox(unit, bank_, W):
                j, t = unit
                for g in range(2):
                    h = 2 * j + g
                    o = bank_[:, g * T:g * T + W]
                    mm(o, qT[:, h, t * P:(t + 1) * P], kT[:, h, 0:W], start=True, stop=False)
                    if t == 1:
                        mm(bank_[:, g * T + P:g * T + T], nlf[:, 1, h, :], tri[:, 0:P], start=False, stop=False,
                           skip_group_check=True)
                    ins = mm(o, nlf[:, 0, h, :], tri[:, 0:W], start=False, stop=True)
                ins.then_inc(sc_ready, 1)

            attention(0, FOX, fox, lambda unit, g, k: vt[:, k, (2 * unit[0] + g) * P:(2 * unit[0] + g + 1) * P])

            def square(name):
                with pe.Fori(0, 2) as i:
                    for b in range(2):
                        block_of(rows_unit, UNIT0[name] + b * UPB, BLOCK0[name] + b, i=i, per_u=2 * UPB, per_b=2)

            pe.wait_ge(o_lo, 8)
            pe.wait_ge(mix_tail, 1)
            square("e_out")
            stream_transposes(TR0["ln0"], 0)

            def ffn(l):
                u0, b0, t0 = UNIT0[f"gu{l}"], BLOCK0[f"gu{l}"], TR0[f"gu{l}"]

                def hidden(i):
                    pe.wait_ge(acc_free[1], i + uses(b0 + 1) + 1)
                    for t in range(TT):
                        transposes(i * 2 + (t0 + t), [hbuf[:, t, q * P:(q + 1) * P] for q in range(4)],
                                   (t0 + t) % 2)

                def body(i, first):
                    open_block(b0, i, 2)
                    for j in range(UPB):
                        rows_unit(at(u0 + j, i, 2 * UPB), 0, j * UK, j == 0, j == UPB - 1)
                        if j == 1 and not first:
                            hidden(i - 1)
                    block_of(rows_unit, u0 + UPB, b0 + 1, i=i, per_u=2 * UPB, per_b=2)

                body(0, True)
                with pe.Fori(1, FFN_BLOCKS) as i:
                    body(i, False)
                hidden(FFN_BLOCKS - 1)
                pe.wait_ge(tr_free, t0 + 2 * FFN_BLOCKS)
                with pe.Fori(0, 2) as i:
                    for b in range(2):
                        block_of(rows_unit, UNIT0[f"down{l}"] + b * DOWN_UNITS, BLOCK0[f"down{l}"] + b,
                                 n_units=DOWN_UNITS, i=i, per_u=2 * DOWN_UNITS, per_b=2, src=(hTh, hTl))

            ffn(0)
            stream_transposes(TR0["ln1"], 8)

            for b in range(2):
                block_of(cols_unit, UNIT0["o_q"] + b * UPB, BLOCK0["o_q"] + b)
            for name, width in (("o_kv", 2 * SWA_KV * SWA_DH), ("o_cq", QR_RANK), ("o_ckv", KV_RANK + ROPE)):
                block_of(rows_unit, UNIT0[name], BLOCK0[name], width=width)
            pe.wait_ge(acc_free[0], uses(BLOCK0["o_kv"]) + 1)
            transposes(TR0["kswa"], [kvs[:, t, v * P:(v + 1) * P] for v in range(2) for t in range(TT)])
            pe.wait_ge(c_norm, 1)
            for m in range(3):
                transposes(TR0["rms"] + m, [
                    cqs[:, t, k * P:(k + 1) * P] if k < 4 else ckvs[:, t, (k - 4) * P:(k - 3) * P]
                    for k in (2 * m, 2 * m + 1) for t in range(TT)])
            pe.wait_ge(tr_free, TR0["rms"] + 3)
            b = BLOCK0["qb_nope"]
            open_block(b)
            open_block(b + 1)
            for k in range(QR_RANK // P):
                u = at(UNIT0["qb_nope"] + k)
                unit_ready(u)
                for h in range(MLA_H):
                    wh, wl = (w[:, u[0], h * P:(h + 1) * P] for w in (whi, wlo))
                    o = acc[(b + h // 4) % 2][h % 4 // 2][:, (h % 2) * T:(h % 2 + 1) * T]
                    mm(o, wh, cTh[:, k, :], start=k == 0 and h % 2 == 0, stop=False, skip_group_check=True)
                    mm(o, wl, cTh[:, k, :], start=False, stop=False, skip_group_check=True)
                    ins = mm(o, wh, cTl[:, k, :], start=False, stop=k == QR_RANK // P - 1, skip_group_check=True)
                ins.then_inc(w_used, 1)
            b = BLOCK0["qb_rope"]
            open_block(b)
            for k in range(QR_RANK // P):
                rows_unit(at(UNIT0["qb_rope"] + k), b % 2, k, k == 0, k == QR_RANK // P - 1,
                                src=(cTh, cTl), kts=1)
            for b in range(4):
                u, blk = at(UNIT0["kvb"] + b), BLOCK0["kvb"] + b
                open_block(blk)
                unit_ready(u)
                s = u[0]
                for g in range(2):
                    for k in range(UK):
                        wh, wl = (w[:, s, k * COLS + g * T:k * COLS + g * T + P] for w in (whi, wlo))
                        xh, xl = cTh[:, 4 + k, :], cTl[:, 4 + k, :]
                        o = acc[blk % 2][0][:, g * T:(g + 1) * T]
                        mm(o, wh, xh, start=k == 0, stop=False)
                        mm(o, wl, xh, start=False, stop=False)
                        mm(o, wh, xl, start=False, stop=k == UK - 1)
                for t in range(TT):
                    for g in range(2):
                        for k in range(UK):
                            wh, wl = (w[:, s, k * COLS + g * T + P:k * COLS + (g + 1) * T] for w in (whi, wlo))
                            xh, xl = (a[:, 4 + k, t * P:(t + 1) * P] for a in (cTh, cTl))
                            o = acc[blk % 2][1][:, t * T + g * P:t * T + (g + 1) * P]
                            mm(o, xh, wh, start=k == 0, stop=False)
                            mm(o, xh, wl, start=False, stop=False)
                            ins = mm(o, xl, wh, start=False, stop=k == UK - 1)
                ins.then_inc(w_used, 1)
                pe.wait_ge(rope_out, 1)
            for m in range(3):
                transposes(TR0["rope"] + m, [qro[:, t, 2 * c:2 * c + 2, :].rearrange("p a b -> p (a b)")
                                             for c in range(2 * m, min(2 * m + 2, 5)) for t in range(TT)])
            pe.wait_ge(tr_free, TR0["rope"] + 3)
            for p in range(2):
                pe.wait_ge(acc_free[p], uses(BLOCK0["o_out"]))

            ODD = [("swa", j, t) for j in range(8) for t in range(2)] + [("mla", j, t) for j in range(4) for t in range(2)]

            def odd_scores(unit, bank_, W):
                kind, j, t = unit
                for g in range(2):
                    o = bank_[:, g * T:g * T + W]
                    if kind == "swa":
                        kv = 2 * j // (SWA_Q // SWA_KV)
                        ins = mm(o, qT[:, j, t * P:(t + 1) * P], kz[:, kv, g, 0:W], start=True, stop=True)
                    else:
                        h = 2 * j + g
                        mm(o, qnT[:, h, t * P:(t + 1) * P], knT[:, h, 0:W], start=True, stop=False)
                        ins = mm(o, qrT[:, j, t * P:(t + 1) * P], krz[:, g, 0:W], start=False, stop=True)
                ins.then_inc(sc_ready, 1)

            def odd_values(unit, g, k):
                kind, j, t = unit
                if kind == "swa":
                    return vd[:, k, 2 * j // (SWA_Q // SWA_KV), :]
                return vm[:, k, 2 * j + g, :]

            attention(8, ODD, odd_scores, odd_values)
            pe.wait_ge(o_lo, 8 + len(ODD))
            square("o_out")
            stream_transposes(TR0["ln2"], 16)
            ffn(1)

        @block.scalar
        def _(act):
            chain = [0]
            activate = nc.scalar.activation

            def link(ins):
                chain[0] += 1
                ins.then_inc(av, 1)
                act.wait_ge(av, chain[0])

            def high(u):
                slot, rounds = u
                act.wait_ge(w_in[slot], rounds * 16 + 16)
                if not (isinstance(rounds, int) and rounds == 0):
                    act.wait_ge(w_used, number(u) - (SLOTS - 1))
                activate(whi[:, slot, :], raw[:, slot, :], ACT.Copy).then_inc(w_hi, 1)

            def ahead(u0, j, i=0, per=0):
                if not (isinstance(i, int) and i * per + u0 + j + SLOTS >= UNITS):
                    high(at(u0 + j + SLOTS, i, per))

            def split_out(n, h, dst, parity=None):
                act.wait_ge(tr_ready, n + 1)
                activate(dst, trb[n % 2 if parity is None else parity][:].rearrange("p (k t) -> p k t", k=4),
                         ACT.Copy).then_inc(tr_hi, 1)

            def stream_high(n0, h0):
                for n in range(8):
                    t, c = n % 2, n // 2
                    split_out(n0 + n, h0 + n, xTh[:, 4 * c:4 * c + 4, t * P:(t + 1) * P])

            for u in range(SLOTS):
                high(at(u))
            stream_high(TR0["x"], HI0["x"])
            act.wait_ge(ev_in, 12 * 16)
            activate(wfh[:], wf[:], ACT.Copy).then_inc(wf_hi, 1)

            def read_cols(b, dst, func=ACT.Copy, scale=1.0):
                act.wait_ge(w_used, BLOCK_END[b])
                for k in range(2):
                    ins = activate(dst(k), acc[b % 2][k][:].rearrange("p (c t) -> p c t", c=2), func, scale=scale)
                ins.then_inc(acc_free[b % 2], 1)

            FOX_SCALE = P ** -0.5
            for b in range(2):
                for j in range(UPB):
                    ahead(UNIT0["e_u"] + b * UPB, j)
                    if b == 0 and j == 2:
                        act.wait_ge(f_neg, 1)
                        activate(fz[:, 2, :], fz[:, 1, :], ACT.Exp).then_inc(f_exp, 1)
                    if b == 0 and j == 3:
                        act.wait_ge(lam_x, 1)
                        activate(lz[:, 2, :], lz[:, 1, :], ACT.Exp).then_inc(lam_e, 1)
                read_cols(BLOCK0["e_u"] + b, lambda k: uT[:, 4 * b + 2 * k:4 * b + 2 * k + 2, CONV - 1:])
            for b in range(2):
                for j in range(UPB):
                    ahead(UNIT0["e_g"] + b * UPB, j)
                    if b == 0 and j == 4:
                        act.wait_ge(f_log, 1)
                        activate(nlf[:].rearrange("p t h q -> p (t h) q"),
                                 fz[:, 6, :].unsqueeze(2).broadcast_to([P, TT * FOX_HEADS, P]),
                                 ACT.Copy, scale=-1.0).then_inc(f_rep, 1)
                read_cols(BLOCK0["e_g"] + b, lambda k: gT[:, 4 * b + 2 * k:4 * b + 2 * k + 2, :],
                          ACT.Gelu_apprx_tanh)
            for b in range(2):
                for j in range(UPB):
                    ahead(UNIT0["e_q"] + b * UPB, j)
                read_cols(BLOCK0["e_q"] + b, lambda k: qT[:, 4 * b + 2 * k:4 * b + 2 * k + 2, :], scale=FOX_SCALE)
            for b in range(2):
                for j in range(UPB):
                    ahead(UNIT0["e_k"] + b * UPB, j)
                    if b == 0:
                        act.wait_ge(gates_ready, j + 1)
                        activate(rt[:, j, :], scb[j % 2][:, 0:T], ACT.Sigmoid, bias=cols[:, 1, j:j + 1])
                        activate(it[:, j, :], scb[j % 2][:, T:2 * T], ACT.Sigmoid,
                                 bias=cols[:, 2, j:j + 1]).then_inc(gates_free, 1)
                read_cols(BLOCK0["e_k"] + b, lambda k: kT[:, 4 * b + 2 * k:4 * b + 2 * k + 2, :])
            for b in range(2):
                for j in range(UPB):
                    ahead(UNIT0["e_v"] + b * UPB, j)
                    if b == 0 and j < 4:
                        if j == 0:
                            act.wait_ge(lam_done, 1)
                            act.wait_ge(gates_free, 8)
                            act.wait_ge(conv_done, 8)
                        for n in (2 * j, 2 * j + 1):
                            ins = activate(uT[:, n, 0:T], rt[:, n, :], ACT.Exp, scale=clam[:, 1, n:n + 1])
                        if j == 3:
                            link(ins)
                    if b == 0 and j >= 4:
                        for n in (2 * j - 8, 2 * j - 7):
                            ins = activate(rt[:, n, :], rt[:, n, :], ACT.Tanh, scale=clam[:, 0, n:n + 1])
                        if j == 7:
                            ins.then_inc(rg_at, 1)
                    if b == 1 and j == 5:
                        act.wait_ge(rg_var, 1)
                        activate(rt[:], rt[:], ACT.Sqrt).then_inc(rg_sq, 1)
                blk = BLOCK0["e_v"] + b
                act.wait_ge(w_used, BLOCK_END[blk])
                for t in range(TT):
                    ins = activate(vt[:, t, b * COLS:(b + 1) * COLS], acc[blk % 2][t][:], ACT.Copy)
                ins.then_inc(acc_free[blk % 2], 1)

            def attention(n0, units, dst_of):
                N = len(units)
                for s in range(N + 3):
                    if s < N:
                        n = n0 + s
                        j, t = units[s][-2:]
                        swa = units[s][0] == "swa"
                        act.wait_ge(nm_ready, n + 1)
                        if s >= 2:
                            act.wait_ge(pt_ready, n - 1)
                        W = (t + 1) * P
                        for g in range(2):
                            if swa:
                                h = 2 * j + g
                                activate(es[:, n % 2, g:g + 1], sinks[:, h:h + 1], ACT.Exp,
                                         bias=nm[:, n % 2, g:g + 1])
                            ins = activate(p_sb[:, n % 2, g, 0:W], s_sb[:, n % 2, g, 0:W], ACT.Exp,
                                           bias=nm[:, n % 2, g:g + 1], accum_out=lsum[:, n % 2, g:g + 1])
                        ins.then_inc(ex_ready, 1)
                    if 2 <= s < N + 2:
                        n = n0 + s - 2
                        j, t = units[s - 2][-2:]
                        act.wait_ge(pt_ready, n + 1)
                        if s >= 4:
                            act.wait_ge(o_ready, n - 1)
                        W = 2 * (t + 1) * P
                        activate(pT[:, n % 2, 0:2 * (t + 1), :].rearrange("p a b -> p (a b)"),
                                 acc[1][n % 2][:, 0:W], ACT.Copy).then_inc(pt_copied, 1)
                    if s >= 3:
                        n = n0 + s - 3
                        act.wait_ge(o_ready, n + 1)
                        for ps, dst, cols_ in dst_of(units[s - 3]):
                            ins = activate(xTh[ps, dst[0]:dst[1], dst[2]:dst[2] + P],
                                           acc[0][n % 2][ps, cols_].rearrange("p (a b) -> p a b", b=P), ACT.Copy)
                        ins.then_inc(o_hi, 1)

            attention(0, [(j, t) for j in range(4) for t in range(2)], fox_dst)
            act.wait_ge(rg_out, 1)
            activate(xTh[:, 8:16, :], gT[:], ACT.Copy).then_inc(rg_hi, 1)

            def square(name):
                with act.Fori(0, 2) as i:
                    for b in range(2):
                        for j in range(UPB):
                            ahead(UNIT0[name] + b * UPB, j, i, 2 * UPB)

            def ln_root(l):
                act.wait_ge(ln_var, l + 1)
                activate(lnv[:, 1, :], lnv[:, 0, :], ACT.Sqrt).then_inc(ln_sd, 1)

            square("e_out")
            ln_root(0)
            stream_high(TR0["ln0"], HI0["ln0"])

            def ffn(l):
                u0, b0, t0 = UNIT0[f"gu{l}"], BLOCK0[f"gu{l}"], TR0[f"gu{l}"]

                def hidden(i):
                    for t in range(TT):
                        split_out(i * 2 + (t0 + t), None, hTh[:, bass.ds(i * 4, 4), t * P:(t + 1) * P],
                                  (t0 + t) % 2)

                def body(i, first):
                    for j in range(UPB):
                        ahead(u0, j, i, 2 * UPB)
                        if j == 2 and not first:
                            hidden(i - 1)
                    act.wait_ge(w_used, i * (2 * UPB) + BLOCK_END[b0])
                    act.wait_ge(acc_free[1], i + uses(b0 + 1))
                    for t in range(TT):
                        ins = activate(sg[:, t, :], acc[0][t][:], ACT.Silu)
                    ins.then_inc(acc_free[0], 1)
                    for j in range(UPB, 2 * UPB):
                        ahead(u0, j, i, 2 * UPB)

                body(0, True)
                with act.Fori(1, FFN_BLOCKS) as i:
                    body(i, False)
                hidden(FFN_BLOCKS - 1)
                d0 = UNIT0[f"down{l}"]
                if l == 0:
                    with act.Fori(0, 2) as i:
                        for j in range(2 * DOWN_UNITS):
                            ahead(d0, j, i, 2 * DOWN_UNITS)
                else:
                    for j in range(4 * DOWN_UNITS):
                        ahead(d0, j)

            ffn(0)
            ln_root(1)
            stream_high(TR0["ln1"], HI0["ln1"])

            for b in range(2):
                for j in range(UPB):
                    ahead(UNIT0["o_q"] + b * UPB, j)
                read_cols(BLOCK0["o_q"] + b, lambda k: qT[:, 4 * b + 2 * k:4 * b + 2 * k + 2, :],
                          scale=SWA_DH ** -0.5)
            for j in range(UPB):
                ahead(UNIT0["o_kv"], j)
            b = BLOCK0["o_kv"]
            act.wait_ge(w_used, BLOCK_END[b])
            for t in range(TT):
                src = acc[b % 2][t]
                activate(kvs[:, t, 0:P], src[:, 0:P], ACT.Copy)
                activate(kvs[:, t, P:P + 64], src[:, 64:P], ACT.Copy)
                activate(kvs[:, t, P + 64:2 * P], src[:, 0:64], ACT.Copy)
                for half in range(2):
                    ins = activate(vd[:, t, :, half * 64:(half + 1) * 64],
                                   src[:, P:2 * P].rearrange("p (v d) -> p v d", v=2), ACT.Copy)
            ins.then_inc(acc_free[b % 2], 1)
            for j in range(UPB):
                ahead(UNIT0["o_cq"], j)
            b = BLOCK0["o_cq"]
            act.wait_ge(w_used, BLOCK_END[b])
            for t in range(TT):
                ins = activate(cqs[:, t, :], acc[b % 2][t][:], ACT.Copy)
            ins.then_inc(acc_free[b % 2], 1)
            for j in range(UPB):
                ahead(UNIT0["o_ckv"], j)
                if j == 3:
                    act.wait_ge(trig_arg, 1)
                    activate(trig[:, 4:6, :, :], trig[:, 2:4, :, :], ACT.Sin).then_inc(trig_done, 1)
            b = BLOCK0["o_ckv"]
            act.wait_ge(w_used, BLOCK_END[b])
            for t in range(TT):
                activate(ckvs[:, t, :], acc[b % 2][t][:, 0:KV_RANK], ACT.Copy)
                for c in range(2):
                    ins = activate(qr[:, t, 8 + c, :], acc[b % 2][t][:, KV_RANK:KV_RANK + ROPE], ACT.Copy)
            link(ins)
            act.sem_inc(acc_free[b % 2], 1)
            for t in range(TT):
                activate(p_sb[:, 0, :, :].rearrange("p a b -> p (a b)"), cqs[:, t, :], ACT.Square,
                         accum_out=rms[:, 0, t:t + 1])
                ins = activate(p_sb[:, 1, 0, :], ckvs[:, t, :], ACT.Square, accum_out=rms[:, 0, 2 + t:3 + t])
                if t == 0:
                    link(ins)
            ins.then_inc(sq_done, 1)
            act.wait_ge(rms_var, 1)
            activate(rms[:, 2, :], rms[:, 1, :], ACT.Sqrt).then_inc(rms_sd, 1)
            for m in range(3):
                n = TR0["rms"] + m
                act.wait_ge(tr_ready, n + 1)
                for k in range(2):
                    ins = activate(cTh[:, 2 * m + k, :], trb[n % 2][:, k * T:(k + 1) * T], ACT.Copy,
                                   scale=qkg[:, 2 * m + k:2 * m + k + 1])
                ins.then_inc(tr_hi, 1)
            MLA_SCALE = (NOPE + ROPE) ** -0.5
            for j in range(4):
                ahead(UNIT0["qb_nope"], j)
            for b in range(2):
                read_cols(BLOCK0["qb_nope"] + b, lambda k: qnT[:, 4 * b + 2 * k:4 * b + 2 * k + 2, :], scale=MLA_SCALE)
            for j in range(4):
                ahead(UNIT0["qb_rope"], j)
            b = BLOCK0["qb_rope"]
            act.wait_ge(w_used, BLOCK_END[b])
            for t in range(TT):
                ins = activate(qr[:, t, 0:8, :], acc[b % 2][t][:].rearrange("p (h d) -> p h d", d=ROPE), ACT.Copy,
                               scale=MLA_SCALE)
            ins.then_inc(acc_free[b % 2], 1)
            for b in range(4):
                ahead(UNIT0["kvb"] + b, 0)
                blk = BLOCK0["kvb"] + b
                act.wait_ge(w_used, BLOCK_END[blk])
                activate(knT[:, 2 * b:2 * b + 2, :], acc[blk % 2][0][:].rearrange("p (g t) -> p g t", g=2), ACT.Copy)
                activate(vm[:, :, 2 * b:2 * b + 2, :].rearrange("p t g d -> p t (g d)"),
                         acc[blk % 2][1][:].rearrange("p (t d) -> p t d", t=2), ACT.Copy).then_inc(acc_free[blk % 2], 1)
            attention(8, [("swa", j, t) for j in range(8) for t in range(2)]
                      + [("mla", j, t) for j in range(4) for t in range(2)], odd_dst)
            square("o_out")
            ln_root(2)
            stream_high(TR0["ln2"], HI0["ln2"])
            ffn(1)
            ln_root(3)

        @block.vector
        def _(dve):
            chain = [0]
            v = nc.vector

            def link(ins):
                chain[0] += 1
                ins.then_inc(dv, 1)
                dve.wait_ge(dv, chain[0])

            def low(u):
                slot = u[0]
                dve.wait_ge(w_hi, number(u) + 1)
                v.tensor_tensor(wlo[:, slot, :], raw[:, slot, :], whi[:, slot, :].bitcast(F32),
                                ALU.subtract).then_inc(w_lo, 1)

            def ahead(u0, j, i=0, per=0):
                if not (isinstance(i, int) and i * per + u0 + j + SLOTS >= UNITS):
                    low(at(u0 + j + SLOTS, i, per))

            def rest_out(n, h, hi, dst, parity=None):
                dve.wait_ge(tr_hi, h + 1)
                v.tensor_tensor(dst, trb[n % 2 if parity is None else parity][:].rearrange("p (k t) -> p k t", k=4),
                                hi.bitcast(F32), ALU.subtract).then_inc(tr_free, 1)

            def stream_low(n0, h0, n):
                t, c = n % 2, n // 2
                at_ = (slice(None), slice(4 * c, 4 * c + 4), slice(t * P, (t + 1) * P))
                rest_out(n0 + n, h0 + n, xTh[at_], xTl[at_])

            def log1p_of(e, y, q, s, out_):
                link(v.tensor_scalar(y, e, 2.0, None, ALU.add))
                link(v.reciprocal(y, y))
                link(v.tensor_tensor(s, e, y, ALU.mult))
                link(v.tensor_tensor(q, s, s, ALU.mult))
                link(v.tensor_scalar(y, q, 1.0 / (2 * LOG1P_TERMS + 1), None, ALU.mult))
                for k in range(LOG1P_TERMS - 1, 0, -1):
                    link(v.scalar_tensor_tensor(out=y, in0=y, scalar=1.0 / (2 * k + 1), in1=q, op0=ALU.add, op1=ALU.mult))
                link(v.scalar_tensor_tensor(out=y, in0=y, scalar=1.0, in1=s, op0=ALU.add, op1=ALU.mult))
                link(v.tensor_scalar(out_, y, 2.0, None, ALU.mult))

            for u in range(SLOTS):
                low(at(u))
            for n in range(8):
                stream_low(TR0["x"], HI0["x"], n)
            dve.wait_ge(wf_hi, 1)
            v.tensor_tensor(wfl[:], wf[:], wfh[:].bitcast(F32), ALU.subtract).then_inc(wf_split, 1)

            def conv(n):
                link(v.tensor_scalar(uc[:, n, :], uT[:, n, 0:T], cw[:, 0, n:n + 1], cols[:, 0, n:n + 1],
                                     ALU.mult, ALU.add))
                for k in range(1, CONV):
                    ins = v.scalar_tensor_tensor(out=uc[:, n, :], in0=uT[:, n, k:k + T], scalar=cw[:, k, n:n + 1],
                                                 in1=uc[:, n, :], op0=ALU.mult, op1=ALU.add)
                    if k < CONV - 1:
                        link(ins)
                ins.then_inc(conv_done, 1)

            for b in range(2):
                for j in range(UPB):
                    ahead(UNIT0["e_u"] + b * UPB, j)
                    if b == 0 and j == 0:
                        dve.wait_ge(f_ready, 1)
                        for t in range(TT):
                            ins = v.tensor_tensor(fz[:, 0, t * 8:t * 8 + 8], scb[0][:, t * 8:t * 8 + 8], fb[:], ALU.add)
                        link(ins)
                        link(v.tensor_scalar(fz[:, 1, :], fz[:, 0, :], -1.0, None, ALU.mult))
                        v.tensor_tensor(fz[:, 1, :], fz[:, 1, :], fz[:, 0, :], ALU.min).then_inc(f_neg, 1)
                    if b == 0 and j == 1:
                        link(v.tensor_scalar(lz[:, 0, :], cols[:, 3, :], -1.0, None, ALU.mult))
                        v.tensor_tensor(lz[:, 1, :], lz[:, 0, :], cols[:, 3, :], ALU.min).then_inc(lam_x, 1)
                    if b == 1 and j == 0:
                        dve.wait_ge(f_exp, 1)
                        log1p_of(fz[:, 2, :], fz[:, 3, :], fz[:, 4, :], fz[:, 5, :], fz[:, 1, :])
                        v.scalar_tensor_tensor(out=fz[:, 6, :], in0=fz[:, 0, :], scalar=0.0, in1=fz[:, 1, :],
                                               op0=ALU.min, op1=ALU.subtract).then_inc(f_log, 1)
                    if b == 1 and j == 3:
                        dve.wait_ge(lam_e, 1)
                        log1p_of(lz[:, 2, :], lz[:, 3, :], lz[:, 4, :], lz[:, 5, :], lz[:, 1, :])
                        link(v.scalar_tensor_tensor(out=lz[:, 3, :], in0=lz[:, 0, :], scalar=0.0, in1=lz[:, 1, :],
                                                    op0=ALU.max, op1=ALU.add))
                        v.tensor_scalar(clam[:, 0, :], lz[:, 3, :], LRU_C, None, ALU.mult)
                        v.tensor_scalar(clam[:, 1, :], lz[:, 3, :], -LRU_C, None, ALU.mult).then_inc(lam_done, 1)
            for b in range(2):
                for j in range(UPB):
                    ahead(UNIT0["e_g"] + b * UPB, j)
            for b in range(2):
                for j in range(UPB):
                    ahead(UNIT0["e_q"] + b * UPB, j)
                    if b == 0 and j == 0:
                        dve.wait_ge(c_ready, 1)
                        v.tensor_copy(cq[:].rearrange("p t h -> p (t h)"), scb[1][:, 0:16]).then_inc(c_done, 1)
                        dve.wait_ge(acc_free[0], uses(BLOCK0["e_g"]))
                        dve.wait_ge(acc_free[1], uses(BLOCK0["e_g"]))
                        dve.wait_ge(consts, 1)
                    if b == 0:
                        conv(j)
            for b in range(2):
                for j in range(UPB):
                    ahead(UNIT0["e_k"] + b * UPB, j)
            for b in range(2):
                for j in range(UPB):
                    ahead(UNIT0["e_v"] + b * UPB, j)
                    if b == 1 and j == 0:
                        dve.wait_ge(rg_at, 1)
                        link(v.tensor_scalar(rgd[:], rt[:], 1.0, None, ALU.add))
                    if b == 1 and j == 1:
                        link(v.reciprocal(rgd[:], rgd[:]))
                    if b == 1 and j == 2:
                        link(v.scalar_tensor_tensor(out=rt[:], in0=rt[:], scalar=2.0, in1=rgd[:], op0=ALU.mult, op1=ALU.mult))
                    if b == 1 and j == 3:
                        v.tensor_scalar(rt[:], rt[:], 1e-34, None, ALU.max).then_inc(rg_var, 1)
                    if b == 1 and j == 4:
                        link(v.tensor_tensor(it[:], it[:], uc[:], ALU.mult))

            def attention(n0, units, dst_of, score_parts):
                N = len(units)
                for s in range(N + 4):
                    if s < N:
                        n = n0 + s
                        j, t = units[s][-2:]
                        W = (t + 1) * P
                        dve.wait_ge(sc_ready, n + 1)
                        if s >= 2:
                            dve.wait_ge(ex_ready, n - 1)
                        for g in range(2):
                            add, mask = score_parts(units[s], g)
                            ins = v.scalar_tensor_tensor(out=s_sb[:, n % 2, g, 0:W], in0=scb[n % 2][:, g * T:g * T + W],
                                                         scalar=add, in1=mask, op0=ALU.add, op1=ALU.add)
                        link(ins)
                        link(v.tensor_reduce(mx[:, n % 2, :], s_sb[:, n % 2, :, 0:W], AX.X, ALU.max))
                        if units[s][0] == "swa":
                            link(v.tensor_tensor(mx[:, n % 2, :], mx[:, n % 2, :], sinks[:, 2 * j:2 * j + 2], ALU.max))
                        v.tensor_scalar(nm[:, n % 2, :], mx[:, n % 2, :], -1.0, None, ALU.mult).then_inc(nm_ready, 1)
                    if 1 <= s < N + 1:
                        n = n0 + s - 1
                        j, t = units[s - 1][-2:]
                        W = (t + 1) * P
                        dve.wait_ge(ex_ready, n + 1)
                        if units[s - 1][0] == "swa":
                            link(v.tensor_tensor(lsum[:, n % 2, :], lsum[:, n % 2, :], es[:, n % 2, :], ALU.add))
                        link(v.reciprocal(rl[:, n % 2, :], lsum[:, n % 2, :]))
                        v.tensor_tensor(p_sb[:, n % 2, :, 0:W], p_sb[:, n % 2, :, 0:W],
                                        rl[:, n % 2, :].unsqueeze(2).broadcast_to([P, 2, W]), ALU.mult).then_inc(pr_ready, 1)
                    if s >= 4:
                        n = n0 + s - 4
                        dve.wait_ge(o_hi, n + 1)
                        for ps, dst, cols_ in dst_of(units[s - 4]):
                            ins = v.tensor_tensor(xTl[ps, dst[0]:dst[1], dst[2]:dst[2] + P],
                                                  acc[0][n % 2][ps, cols_].rearrange("p (a b) -> p a b", b=P),
                                                  xTh[ps, dst[0]:dst[1], dst[2]:dst[2] + P].bitcast(F32), ALU.subtract)
                        ins.then_inc(o_lo, 1)

            def fox_parts(unit, g):
                j, t = unit
                return cq[:, t, 2 * j + g:2 * j + g + 1], (cmask[:, P:T] if t == 0 else cmask[:])

            def odd_parts(unit, g):
                kind, j, t = unit
                if t == 0:
                    return 0.0, bmask[:, P:T]
                return 0.0, (wmask[:] if kind == "swa" else bmask[:])

            attention(0, [(j, t) for j in range(4) for t in range(2)], fox_dst, fox_parts)
            dve.wait_ge(rg_sq, 1)
            link(v.tensor_tensor(it[:], it[:], rt[:], ALU.mult))
            for n in range(LRU_B):
                ins = v.tensor_tensor_scan(rt[:, n, :], uT[:, n, 0:T], it[:, n, :], 0.0, ALU.mult, ALU.add)
            link(ins)
            v.tensor_tensor(gT[:], rt[:], gT[:], ALU.mult).then_inc(rg_out, 1)
            dve.wait_ge(rg_hi, 1)
            v.tensor_tensor(xTl[:, 8:16, :], gT[:], xTh[:, 8:16, :].bitcast(F32), ALU.subtract).then_inc(mix_tail, 1)

            def residual(b, i, c):
                pair = b % 2
                dve.wait_ge(w_used, i * (BLOCK_END[b + 2 - c] - BLOCK_END[b - c]) + BLOCK_END[b])
                for t in range(TT):
                    at_ = xres[:, t, bass.ds(i * (2 * COLS) + c * COLS, COLS)]
                    ins = v.scalar_tensor_tensor(out=at_, in0=at_, scalar=ALPHA, in1=acc[pair][t][:],
                                                 op0=ALU.mult, op1=ALU.add)
                ins.then_inc(acc_free[pair], 1)
                dve.wait_ge(acc_free[pair], i + uses(b) + 1)
                for t in range(TT):
                    ins = v.bn_stats(stats[:, t, bass.ds(i * 2 + c, 1), :].rearrange("p a b -> p (a b)"),
                                     xres[:, t, bass.ds(i * (2 * COLS) + c * COLS, COLS)])
                ins.then_inc(stats_done, 1)

            def square(name):
                with dve.Fori(0, 2) as i:
                    for b in range(2):
                        for j in range(UPB):
                            ahead(UNIT0[name] + b * UPB, j, i, 2 * UPB)
                        residual(BLOCK0[name] + b, i, b)

            def layer_norm(l, n0=None, h0=None):
                dve.wait_ge(stats_done, 4 * (l + 1))
                for t in range(TT):
                    ins = v.bn_aggr(mv[:, t, :], stats[:, t, :, :].rearrange("p a b -> p (a b)"))
                link(ins)
                v.tensor_scalar(lnv[:, 0, :], mv[:, :, 1:2].rearrange("p t a -> p (t a)"), LN_EPS, None,
                                ALU.add).then_inc(ln_var, 1)
                dve.wait_ge(ln_sd, l + 1)
                link(v.reciprocal(lnv[:, 2, :], lnv[:, 1, :]))
                dve.wait_ge(gb_in, 32 * (l + 1))
                for n in range(8):
                    t, c = (n % 2, n // 2) if n0 is not None else (n // 4, n % 4)
                    xc = xres[:, t, c * COLS:(c + 1) * COLS]
                    link(v.tensor_scalar(xc, xc, mv[:, t, 0:1], lnv[:, 2, t:t + 1], ALU.subtract, ALU.mult))
                    link(v.tensor_tensor(xc, xc, gb[:, 0, c * COLS:(c + 1) * COLS], ALU.mult))
                    v.tensor_tensor(xc, xc, gb[:, 1, c * COLS:(c + 1) * COLS], ALU.add).then_inc(y_ready, 1)
                    if n0 is not None and n >= 2:
                        stream_low(n0, h0, n - 2)
                if n0 is not None:
                    stream_low(n0, h0, 6)
                    stream_low(n0, h0, 7)

            square("e_out")
            layer_norm(0, TR0["ln0"], HI0["ln0"])

            def ffn(l):
                u0, b0, t0, h0 = UNIT0[f"gu{l}"], BLOCK0[f"gu{l}"], TR0[f"gu{l}"], HI0[f"gu{l}"]

                def hidden(i):
                    for t in range(TT):
                        at_ = (slice(None), bass.ds(i * 4, 4), slice(t * P, (t + 1) * P))
                        rest_out(None, i * 2 + (h0 + t), hTh[at_], hTl[at_], (t0 + t) % 2)

                def body(i, first):
                    for j in range(2 * UPB):
                        ahead(u0, j, i, 2 * UPB)
                        if j == 2 and not first:
                            hidden(i - 1)
                    dve.wait_ge(w_used, i * (2 * UPB) + BLOCK_END[b0 + 1])
                    dve.wait_ge(acc_free[0], i + uses(b0) + 1)
                    if not first:
                        dve.wait_ge(tr_ready, i * 2 + t0)
                    for t in range(TT):
                        ins = v.tensor_tensor(hbuf[:, t, :], sg[:, t, :], acc[1][t][:], ALU.mult)
                    ins.then_inc(acc_free[1], 1)

                body(0, True)
                with dve.Fori(1, FFN_BLOCKS) as i:
                    body(i, False)
                hidden(FFN_BLOCKS - 1)
                d0, b0 = UNIT0[f"down{l}"], BLOCK0[f"down{l}"]

                def down(i):
                    for b in range(2):
                        for j in range(DOWN_UNITS):
                            ahead(d0 + b * DOWN_UNITS, j, i, 2 * DOWN_UNITS)
                        residual(b0 + b, i, b)

                if l == 0:
                    with dve.Fori(0, 2) as i:
                        down(i)
                else:
                    down(0)
                    down(1)

            ffn(0)
            layer_norm(1, TR0["ln1"], HI0["ln1"])

            for b in range(2):
                for j in range(UPB):
                    ahead(UNIT0["o_q"] + b * UPB, j)
            for j in range(UPB):
                ahead(UNIT0["o_kv"], j)
                if j == 0:
                    dve.wait_ge(od_in, 4 * 16)
                    dve.wait_ge(consts, 2)
                    link(v.tensor_copy(pos[:], pos_i[:]))
                    for t in range(TT):
                        ins = v.tensor_scalar(trig[:, 0, t, :], invf[:], pos[:, t:t + 1], None, ALU.mult)
                    link(ins)
                    rnd = 1.5 * 2.0 ** 23
                    c1 = 6.28125
                    c2 = 2 * math.pi - c1
                    link(v.tensor_scalar(trig[:, 1], trig[:, 0], 1.0 / (2 * math.pi), rnd, ALU.mult, ALU.add))
                    link(v.tensor_scalar(trig[:, 1], trig[:, 1], -rnd, None, ALU.add))
                    link(v.scalar_tensor_tensor(out=trig[:, 2], in0=trig[:, 1], scalar=-c1, in1=trig[:, 0],
                                                op0=ALU.mult, op1=ALU.add))
                    link(v.scalar_tensor_tensor(out=trig[:, 2], in0=trig[:, 1], scalar=-c2, in1=trig[:, 2],
                                                op0=ALU.mult, op1=ALU.add))
                    link(v.tensor_scalar(trig[:, 3], trig[:, 2], math.pi / 2, None, ALU.add))
                    link(v.tensor_scalar(trig[:, 1], trig[:, 3], math.pi, -2 * math.pi, ALU.is_gt, ALU.mult))
                    link(v.tensor_tensor(trig[:, 3], trig[:, 3], trig[:, 1], ALU.add))
                    pi = 3.1415925
                    v.tensor_scalar(trig[:, 2:4], trig[:, 2:4], pi, -pi, ALU.min, ALU.max).then_inc(trig_arg, 1)
            for j in range(UPB):
                ahead(UNIT0["o_cq"], j)
            for j in range(UPB):
                ahead(UNIT0["o_ckv"], j)
            dve.wait_ge(tr_ready, TR0["kswa"] + 1)
            for h in range(SWA_KV):
                bank_ = trb[TR0["kswa"] % 2]
                v.tensor_copy(kz[0:64, h, 0, :], bank_[0:64, h * T:(h + 1) * T])
                ins = v.tensor_copy(kz[64:P, 1 - h, 1, :], bank_[64:P, h * T:(h + 1) * T])
            ins.then_inc(tr_free, 1)
            dve.wait_ge(sq_done, 1)
            link(v.tensor_scalar(rms[:, 1, 0:2], rms[:, 0, 0:2], 1.0 / QR_RANK, RMS_EPS, ALU.mult, ALU.add))
            v.tensor_scalar(rms[:, 1, 2:4], rms[:, 0, 2:4], 1.0 / KV_RANK, RMS_EPS, ALU.mult, ALU.add).then_inc(rms_var, 1)
            dve.wait_ge(rms_sd, 1)
            link(v.reciprocal(rms[:, 3, :], rms[:, 2, :]))
            for t in range(TT):
                v.tensor_scalar(cqs[:, t, :], cqs[:, t, :], rms[:, 3, t:t + 1], None, ALU.mult)
                ins = v.tensor_scalar(ckvs[:, t, :], ckvs[:, t, :], rms[:, 3, 2 + t:3 + t], None, ALU.mult)
            ins.then_inc(c_norm, 1)
            for m in range(3):
                n = TR0["rms"] + m
                dve.wait_ge(tr_hi, HI0["rms"] + m + 1)
                for k in range(2):
                    ins = v.scalar_tensor_tensor(out=cTl[:, 2 * m + k, :], in0=trb[n % 2][:, k * T:(k + 1) * T],
                                                 scalar=qkg[:, 2 * m + k:2 * m + k + 1],
                                                 in1=cTh[:, 2 * m + k, :].bitcast(F32), op0=ALU.mult, op1=ALU.subtract)
                ins.then_inc(tr_free, 1)
            for j in range(4):
                ahead(UNIT0["qb_nope"], j)
            for j in range(4):
                ahead(UNIT0["qb_rope"], j)
            b = BLOCK0["qb_rope"]
            dve.wait_ge(acc_free[b % 2], uses(b) + 1)
            dve.wait_ge(trig_done, 1)
            H = ROPE // 2
            for t in range(TT):
                sin, cos = (trig[:, f, t, :].unsqueeze(1).broadcast_to([P, 10, H]) for f in (4, 5))
                x1, x2, y1, y2 = (a[:, t, :, c * H:(c + 1) * H] for a in (qr, qro) for c in range(2))
                v.tensor_tensor(y1, x1, cos, ALU.mult)
                link(v.tensor_tensor(rtmp[:], x2, sin, ALU.mult))
                link(v.tensor_tensor(y1, y1, rtmp[:], ALU.subtract))
                v.tensor_tensor(y2, x2, cos, ALU.mult)
                link(v.tensor_tensor(rtmp[:], x1, sin, ALU.mult))
                ins = v.tensor_tensor(y2, y2, rtmp[:], ALU.add)
                if t == 0:
                    link(ins)
            ins.then_inc(rope_out, 1)
            for j in range(4):
                ahead(UNIT0["kvb"], j)
            for m in range(3):
                n = TR0["rope"] + m
                dve.wait_ge(tr_ready, n + 1)
                if m < 2:
                    ins = v.tensor_copy(qrT[:, 2 * m:2 * m + 2, :].rearrange("p a b -> p (a b)"), trb[n % 2][:])
                else:
                    for g in range(2):
                        rows = slice(g * 64, (g + 1) * 64)
                        ins = v.tensor_copy(krz[rows, g, :], trb[n % 2][rows, 0:T])
                ins.then_inc(tr_free, 1)
            attention(8, [("swa", j, t) for j in range(8) for t in range(2)]
                      + [("mla", j, t) for j in range(4) for t in range(2)], odd_dst, odd_parts)
            square("o_out")
            layer_norm(2, TR0["ln2"], HI0["ln2"])
            ffn(1)
            layer_norm(3)


_INS = ['x', 'positions', 'ev_w_in', 'ev_forget_bias', 'ev_conv_w', 'ev_conv_b', 'ev_rgate_w', 'ev_rgate_b',
        'ev_igate_w', 'ev_igate_b', 'ev_lru_lambda', 'ev_w_out', 'od_w_in', 'od_sinks', 'od_q_norm', 'od_w_qb',
        'od_kv_norm', 'od_w_kvb', 'od_w_out', 'ln_mix_g', 'ln_mix_b', 'ffn_w_gate', 'ffn_w_up', 'ffn_w_down',
        'ln_ffn_g', 'ln_ffn_b']
_OUTS = [((1, 256, 2048), 'float32')]


def kernel(**inputs):
    import numpy as _np
    import concourse.bacc as _bacc
    from concourse import mybir as _mybir
    from concourse.bass_utils import run_bass_kernel_spmd as _run

    nc = _bacc.Bacc("TRN2", target_bir_lowering=False, num_devices=1)
    arrays, args = {}, []
    for name in _INS:
        a = _np.ascontiguousarray(inputs[name])
        arrays[f"in_{name}_dram"] = a
        args.append(nc.dram_tensor(f"in_{name}_dram", a.shape, _mybir.dt.from_np(a.dtype), kind="ExternalInput").ap())
    for i, (shape, dtype) in enumerate(_OUTS):
        dt = _mybir.dt.from_np(_np.dtype(dtype))
        args.append(nc.dram_tensor(f"out_{i}_dram", shape, dt, kind="ExternalOutput").ap())
    hybrid_trunk_kernel(nc, *args)
    r = _run(nc, [arrays], core_ids=[0])
    got = tuple(r.results[0][f"out_{i}_dram"] for i in range(len(_OUTS)))
    return got[0]
```

```python
from contextlib import ExitStack
import math

import concourse.bass as bass
from concourse import mybir

ALU = mybir.AluOpType
ACT = mybir.ActivationFunctionType
AX = mybir.AxisListType
F32 = mybir.dt.float32
F32R = mybir.dt.float32r
I32 = mybir.dt.int32

P = 128
T = 256
TT = T // P
D = 2048
KD = D // P
COLS = 512
UK = 2
SLOTS = 4
UNIT = UK * COLS
UPB = KD // UK

FOX_HEADS, FOX_W = 8, 1024
LRU_W, LRU_B, CONV = 1024, 8, 4
LRU_C = 8.0
SWA_Q, SWA_KV, SWA_DH = 16, 2, 64
MLA_H, QR_RANK, KV_RANK, NOPE, ROPE, MLA_V = 8, 512, 256, 128, 64, 128
THETA = 10000.0
FFN = 5632
KF = FFN // P
ALPHA = 4.0 ** 0.25
LN_EPS, RMS_EPS = 1e-5, 1e-6
NEG = -1.0e30

FFN_BLOCKS = FFN // COLS
DOWN_UNITS = KF // UK
STREAM = [
    ("e_u", 2 * UPB, 2), ("e_q", 2 * UPB, 2), ("e_k", 2 * UPB, 2), ("e_v", 2 * UPB, 2), ("e_g", 2 * UPB, 2),
    ("e_out", 4 * UPB, 4), ("gu0", 2 * UPB * FFN_BLOCKS, 2 * FFN_BLOCKS), ("down0", 4 * DOWN_UNITS, 4),
    ("o_ckv", UPB, 1), ("o_cq", UPB, 1), ("o_kv", UPB, 1), ("qb_nope", 4, 2), ("qb_rope", 4, 1), ("kvb", 4, 4),
    ("o_q", 2 * UPB, 2),
    ("o_out", 4 * UPB, 4), ("gu1", 2 * UPB * FFN_BLOCKS, 2 * FFN_BLOCKS), ("down1", 4 * DOWN_UNITS, 4),
]
SPAN = []
UNIT0, BLOCK0, BLOCK_END = {}, {}, []
_u = _b = 0
for _name, _nu, _nb in STREAM:
    UNIT0[_name], BLOCK0[_name] = _u, _b
    _ends = {"qb_nope": [4, 4], "o_out": [14, 16, 24, 32]}.get(_name, [(_k + 1) * _nu // _nb for _k in range(_nb)])
    BLOCK_END += [_u + _e for _e in _ends]
    SPAN += [{"o_ckv": UK * (KV_RANK + ROPE), "o_kv": UK * 2 * SWA_KV * SWA_DH, "qb_rope": MLA_H * ROPE}.get(
        _name, UK * COLS)] * _nu
    _u, _b = _u + _nu, _b + _nb
UNITS = _u

TR_STEPS = [("x", 8), ("ln0", 8), ("gu0", 2 * FFN_BLOCKS), ("ln1", 8), ("rms", 3), ("kswa", 1), ("rope", 3),
            ("ln2", 8), ("gu1", 2 * FFN_BLOCKS)]
TR0, HI0 = {}, {}
_n = _h = 0
for _name, _c in TR_STEPS:
    TR0[_name], HI0[_name] = _n, _h
    _n += _c
    _h += 0 if _name in ("kswa", "rope") else _c

E_OUT_K = [8, 10, 0, 2, 4, 6, 12, 14]
O_OUT_HEAD = [(b, k) for ks in ((8, 10, 12, 14), (0, 2), (4, 6)) for b in range(2) for k in ks]

FOX = [("fox", j, t) for j in range(4) for t in range(2)]
ODD = [("mla", j, t) for j in range(4) for t in range(2)] + [("swa", j, t) for j in range(8) for t in range(2)]
FOX_STEPS, ODD_STEPS = len(FOX) + 3, len(ODD) + 3
FOX_AFTER = [j for j in range(16) if j % 4][:FOX_STEPS]

LOG1P_TERMS = 9


def hybrid_trunk_kernel(
    nc: bass.Bass, x, positions, ev_w_in, ev_forget_bias, ev_conv_w, ev_conv_b, ev_rgate_w, ev_rgate_b,
    ev_igate_w, ev_igate_b, ev_lru_lambda, ev_w_out, od_w_in, od_sinks, od_q_norm, od_w_qb, od_kv_norm,
    od_w_kvb, od_w_out, ln_mix_g, ln_mix_b, ffn_w_gate, ffn_w_up, ffn_w_down, ln_ffn_g, ln_ffn_b, out,
):
    ctx = ExitStack()
    with ctx:
        base = (nc.sbuf_base + 63) // 64 * 64
        top = [base]

        def place(name, shape, dt, at=None):
            size = 4
            for s in shape[1:]:
                size *= s
            off = top[0] if at is None else at
            if at is None:
                top[0] = off + (size + 31) // 32 * 32
            return nc.alloc_sbuf_tensor_at(name, shape, dt, offset=off)

        xTh = place("xTh", [P, KD, T], F32R)
        xTl = place("xTl", [P, KD, T], F32R)
        xres = place("xres", [P, TT, D], F32)
        raw = place("raw", [P, SLOTS, UNIT], F32)
        whi = place("whi", [P, SLOTS, UNIT], F32R)
        wlo = place("wlo", [P, SLOTS, UNIT], F32R)
        ident = place("ident", [P, P], F32)
        identr = place("identr", [P, P], F32R)
        stats = place("stats", [P, TT, 4, 6], F32)
        mv = place("mv", [P, TT, 2], F32)
        lnv = place("lnv", [P, 4, TT], F32)
        g0 = top[0]
        gb = place("gb", [P, 2, D], F32)
        sg = place("sg", [P, TT, COLS], F32, g0)
        hbuf = place("hbuf", [P, TT, COLS], F32, g0 + 4 * TT * COLS)
        nlf = place("nlf", [P, TT, FOX_HEADS, P], F32, g0)
        rgd = place("rgd", [P, LRU_B, T], F32, g0 + 4 * TT * FOX_HEADS * P)
        m0 = top[0]
        hTh = place("hTh", [P, KF, T], F32R)
        hTl = place("hTl", [P, KF, T], F32R)
        end = top[0]
        assert end <= nc.sbuf_usable_end, (end, nc.sbuf_usable_end)

        top[0] = m0
        s_sb = place("s_sb", [P, 2, 2, T], F32)
        p_sb = place("p_sb", [P, 2, 2, T], F32)
        pT = place("pT", [P, 2, 4, P], F32)
        nm = place("nm", [P, 2, 2], F32)
        mx = place("mx", [P, 2, 2], F32)
        lsum = place("lsum", [P, 2, 2], F32)
        rl = place("rl", [P, 2, 2], F32)
        es = place("es", [P, 2, 2], F32)
        mix0 = top[0]
        qT = place("qT", [P, 8, T], F32)
        kT = place("kT", [P, 8, T], F32)
        vt = place("vt", [P, TT, FOX_W], F32)
        u0_ = top[0]
        uT = place("uT", [P, LRU_B, T + CONV - 1], F32)
        gT = place("gT", [P, LRU_B, T], F32)
        uc0 = top[0]
        uc = place("uc", [P, LRU_B, T], F32)
        rt = place("rt", [P, LRU_B, T], F32)
        it0 = top[0]
        it = place("it", [P, LRU_B, T], F32)
        rw0 = top[0]
        rw = place("rw", [P, LRU_B, P], F32)
        iw = place("iw", [P, LRU_B, P], F32)
        eTh = [place("eTh0", [P, 8, T], F32R, uc0), place("eTh1", [P, 8, T], F32R, u0_)]
        eTl = [place("eTl0", [P, 8, T], F32R, it0), place("eTl1", [P, 8, T], F32R, rw0)]
        cmask = place("cmask", [P, T], F32)
        tri = place("tri", [P, T], F32)
        wf = place("wf", [P, KD, FOX_HEADS], F32)
        wfh = place("wfh", [P, KD, P], F32R, g0)
        wfl = place("wfl", [P, KD, P], F32R, g0 + 4 * KD * P)
        fT = place("fT", [P, T], F32, u0_ + 4 * LRU_B * (T + CONV - 1))
        fb = place("fb", [P, FOX_HEADS], F32)
        cw = place("cw", [P, CONV, LRU_B], F32)
        cols = place("cols", [P, 4, LRU_B], F32)
        clam = place("clam", [P, 2, LRU_B], F32)
        lz = place("lz", [P, 6, LRU_B], F32)
        fz = place("fz", [P, 7, TT * FOX_HEADS], F32)
        cq = place("cq", [P, TT, FOX_HEADS], F32)
        assert top[0] <= nc.sbuf_usable_end, (top[0], nc.sbuf_usable_end)
        top[0] = mix0 + 4 * 8 * T
        qnT = place("qnT", [P, 8, T], F32)
        knT = place("knT", [P, 8, T], F32)
        qr0 = top[0]
        qr = place("qr", [P, TT, 10, ROPE], F32)
        qro = place("qro", [P, TT, 10, ROPE], F32)
        rtmp = place("rtmp", [P, 10, ROPE // 2], F32)
        c0_ = top[0]
        cTh = place("cTh", [P, 6, T], F32R)
        cTl = place("cTl", [P, 6, T], F32R)
        cqs = place("cqs", [P, TT, QR_RANK], F32)
        ckvs = place("ckvs", [P, TT, KV_RANK], F32)
        mTh = place("mTh", [P, 8, T], F32R, c0_)
        mTl = place("mTl", [P, 8, T], F32R, c0_ + 4 * 8 * T)
        sTh = place("sTh", [P, 4, T], F32R, qr0)
        sTl = place("sTl", [P, 4, T], F32R, qr0 + 4 * 4 * T)
        assert 2 * 4 * 4 * T <= c0_ - qr0 and 2 * 4 * 8 * T <= top[0] - c0_
        qrT = place("qrT", [P, 4, T], F32)
        krz = place("krz", [P, 2, T], F32)
        kvs = place("kvs", [P, TT, 2 * P], F32)
        kz = place("kz", [P, SWA_KV, 2, T], F32)
        vd = place("vd", [P, TT, SWA_KV, P], F32)
        vm = place("vm", [P, TT, MLA_H, MLA_V], F32)
        bmask = place("bmask", [P, 2, T], F32, m0)
        wmask = place("wmask", [P, 2, T], F32, m0 + 4 * 2 * T)
        bmr = place("bmr", [P, 2, T], F32R)
        wmr = place("wmr", [P, 2, T], F32R)
        pos_i = place("pos_i", [P, TT], I32)
        pos = place("pos", [P, TT], F32)
        invf = place("invf", [P, ROPE // 2], F32)
        trig = place("trig", [P, 6, TT, ROPE // 2], F32)
        sinks = place("sinks", [P, SWA_Q], F32)
        qkg = place("qkg", [P, 6], F32)
        rms = place("rms", [P, 4, 2 * TT], F32)
        assert top[0] <= nc.sbuf_usable_end, (top[0], nc.sbuf_usable_end)

        def bank(name):
            return ctx.enter_context(nc.psum_tensor(name, [P, COLS], F32))

        acc = [[bank(f"acc{p}{t}") for t in range(2)] for p in range(2)]
        misc = [bank(f"misc{n}") for n in range(4)]
        scb, trb = misc[0:2], misc[2:4]

        def sem(name):
            return ctx.enter_context(nc.semaphore(name))

        w_in = [sem(f"w_in{s}") for s in range(SLOTS)]
        w_hi = sem("w_hi")
        w_lo = sem("w_lo")
        w_used = sem("w_used")
        acc_free = [sem(f"acc_free{p}") for p in range(2)]
        tr_ready = sem("tr_ready")
        tr_hi = sem("tr_hi")
        tr_free = sem("tr_free")
        x_in = [sem(f"x_in{c}") for c in range(4)]
        y_ready = sem("y_ready")
        tile0_done = sem("tile0_done")
        res0_done = sem("res0_done")
        up0_done = sem("up0_done")
        h0_ready = sem("h0_ready")
        stats_done = sem("stats_done")
        ln_var = sem("ln_var")
        ln_sd = sem("ln_sd")
        gb_in = sem("gb_in")
        out_done = sem("out_done")
        dv = sem("dv")
        av = sem("av")
        pv = sem("pv")
        consts = sem("consts")
        ev_in = sem("ev_in")
        od_in = sem("od_in")
        conv_done = sem("conv_done")
        gates_ready = sem("gates_ready")
        gates_free = sem("gates_free")
        lam_e = sem("lam_e")
        lam_x = sem("lam_x")
        lam_done = sem("lam_done")
        rg_t = sem("rg_t")
        rg_at = sem("rg_at")
        rg_var = sem("rg_var")
        rg_sq = sem("rg_sq")
        rg_h = sem("rg_h")
        rg_out = sem("rg_out")
        rg_hi = sem("rg_hi")
        rg_lo = sem("rg_lo")
        masks_r = sem("masks_r")
        wf_hi = sem("wf_hi")
        wf_split = sem("wf_split")
        wf_in = sem("wf_in")
        f_copied = sem("f_copied")
        f_ready = sem("f_ready")
        f_neg = sem("f_neg")
        f_exp = sem("f_exp")
        f_log = sem("f_log")
        f_rep = sem("f_rep")
        c_ready = sem("c_ready")
        c_done = sem("c_done")
        sc_ready = sem("sc_ready")
        nm_ready = sem("nm_ready")
        ex_ready = sem("ex_ready")
        pr_ready = sem("pr_ready")
        pt_ready = sem("pt_ready")
        pt_copied = sem("pt_copied")
        o_ready = sem("o_ready")
        o_hi = sem("o_hi")
        o_lo = sem("o_lo")
        od_prep = sem("od_prep")
        kv_copied = sem("kv_copied")
        sq_done = sem("sq_done")
        rms_var = sem("rms_var")
        rms_sd = sem("rms_sd")
        c_norm = sem("c_norm")
        ct_hi = sem("ct_hi")
        rope_in = sem("rope_in")
        rope_out = sem("rope_out")
        rope_T = sem("rope_T")
        trig_arg = sem("trig_arg")
        trig_done = sem("trig_done")

        block = ctx.enter_context(nc.Block())

        def at(unit, i=0, per=0):
            return unit % SLOTS, i * (per // SLOTS) + unit // SLOTS

        def number(u):
            return u[1] * SLOTS + u[0]

        def uses(b):
            return b // 2

        SCALES = {"fox": P ** -0.5, "swa": SWA_DH ** -0.5, "mla": (NOPE + ROPE) ** -0.5}

        def out_parts(unit):
            kind, j, t = unit
            if kind == "fox":
                return [(slice(0, P), eTh[0], eTl[0], 2 * j, 2 * j + 2, slice(0, 2 * P))]
            if kind == "mla":
                return [(slice(0, P), mTh, mTl, 2 * j, 2 * j + 2, slice(0, 2 * P))]
            hi, lo, k = (sTh, sTl, j) if j < 4 else (xTh, xTl, j)
            return [(slice(g * 64, g * 64 + 64), hi, lo, k, k + 1, slice(g * P, (g + 1) * P)) for g in range(2)]

        def wmat(w, l):
            return w[l].rearrange("(k p) n -> p k n", p=P)

        @block.sync
        def _(sp):
            def load(u, src, width=COLS, kts=UK):
                slot, rounds = u
                if not (isinstance(rounds, int) and rounds == 0):
                    sp.wait_ge(w_lo, number(u) - SLOTS + 1)
                dst = raw[:, slot, 0:kts * width].rearrange("p (k n) -> p k n", k=kts)
                sp.dma_start(dst, src).then_inc(w_in[slot], 16)

            def load_x(c):
                sp.dma_start(xres[:, :, c * COLS:(c + 1) * COLS],
                             x[0].rearrange("(t p) n -> p t n", p=P)[:, :, c * COLS:(c + 1) * COLS]).then_inc(x_in[c], 16)

            load_x(0)

            ev_in_w = wmat(ev_w_in, 0)
            f0 = 3 * FOX_W
            for name, c0 in (("e_u", f0 + FOX_HEADS), ("e_q", 0), ("e_k", FOX_W), ("e_v", 2 * FOX_W),
                             ("e_g", f0 + FOX_HEADS + LRU_W)):
                for b in range(2):
                    for j in range(UPB):
                        load(at(UNIT0[name] + b * UPB + j),
                             ev_in_w[:, j * UK:(j + 1) * UK, c0 + b * COLS:c0 + (b + 1) * COLS])
                        if name == "e_u" and b == 0 and j < 3:
                            load_x(j + 1)

            def ffn(l):
                gate, up, down = wmat(ffn_w_gate, l), wmat(ffn_w_up, l), wmat(ffn_w_down, l)
                with sp.Fori(0, FFN_BLOCKS) as i:
                    for b, w in enumerate((gate, up)):
                        for j in range(UPB):
                            load(at(UNIT0[f"gu{l}"] + b * UPB + j, i, 2 * UPB),
                                 w[:, j * UK:(j + 1) * UK, bass.ds(i * COLS, COLS)])
                with sp.Fori(0, 2) as i:
                    for b in range(2):
                        for j in range(DOWN_UNITS):
                            load(at(UNIT0[f"down{l}"] + b * DOWN_UNITS + j, i, 2 * DOWN_UNITS),
                                 down[:, j * UK:(j + 1) * UK, bass.ds(i * (2 * COLS) + b * COLS, COLS)])

            w = wmat(ev_w_out, 0)
            for b in range(4):
                for j, k in enumerate(E_OUT_K):
                    load(at(UNIT0["e_out"] + b * UPB + j), w[:, k:k + UK, b * COLS:(b + 1) * COLS])
            ffn(0)
            w = wmat(od_w_in, 0)
            kv0 = SWA_Q * SWA_DH
            cq0 = kv0 + 2 * SWA_KV * SWA_DH
            for name, c0, width in (("o_ckv", cq0 + QR_RANK, KV_RANK + ROPE), ("o_cq", cq0, QR_RANK),
                                    ("o_kv", kv0, cq0 - kv0)):
                for j in range(UPB):
                    load(at(UNIT0[name] + j), w[:, j * UK:(j + 1) * UK, c0:c0 + width], width)
            qb = wmat(od_w_qb, 0)
            hw = NOPE + ROPE

            def load_heads(u, k, off, width):
                slot = u[0]
                sp.wait_ge(w_lo, number(u) - SLOTS + 1)
                src = qb[:, k, :].rearrange("p (h n) -> p h n", n=hw)[:, :, off:off + width]
                sp.dma_start(raw[:, slot, 0:MLA_H * width].rearrange("p (h n) -> p h n", n=width),
                             src).then_inc(w_in[slot], 16)

            for k in range(QR_RANK // P):
                load_heads(at(UNIT0["qb_nope"] + k), k, 0, NOPE)
            for k in range(QR_RANK // P):
                load_heads(at(UNIT0["qb_rope"] + k), k, NOPE, ROPE)
            kvb = wmat(od_w_kvb, 0)
            for b in range(4):
                load(at(UNIT0["kvb"] + b), kvb[:, :, b * COLS:(b + 1) * COLS])
            for b in range(2):
                for j in range(UPB):
                    load(at(UNIT0["o_q"] + b * UPB + j), w[:, j * UK:(j + 1) * UK, b * COLS:(b + 1) * COLS])
            w = wmat(od_w_out, 0)
            for j, (b, k) in enumerate(O_OUT_HEAD + [(b, j * UK) for b in range(2, 4) for j in range(UPB)]):
                load(at(UNIT0["o_out"] + j), w[:, k:k + UK, b * COLS:(b + 1) * COLS])
            ffn(1)
            for n in range(8):
                t, c = n // 4, n % 4
                sp.wait_ge(y_ready, 3 * 8 + n + 1)
                sp.dma_start(out[0, t * P:(t + 1) * P, c * COLS:(c + 1) * COLS],
                             xres[:, t, c * COLS:(c + 1) * COLS]).then_inc(out_done, 16)
            sp.wait_ge(out_done, 8 * 16)

        @block.gpsimd
        def _(pool):
            chain = [0]

            def link(ins):
                chain[0] += 1
                ins.then_inc(pv, 1)
                pool.wait_ge(pv, chain[0])

            link(pool.memset(ident[:], 0.0))
            link(pool.affine_select(out=ident[:], in_=ident[:], compare_op=ALU.not_equal, fill=1.0, base=0,
                                    pattern=[[-1, P]], channel_multiplier=1))
            pool.sem_inc(consts, 1)
            vec = lambda w: w[0].rearrange("(n p) -> p n", p=P)
            f0 = 3 * FOX_W
            pool.dma_start(wf[:], wmat(ev_w_in, 0)[:, :, f0:f0 + FOX_HEADS]).then_inc(wf_in, 16)
            for dst, src in (
                (fb[:], ev_forget_bias[0:1, :].broadcast_to([P, FOX_HEADS])),
                (cols[:, 3, :], vec(ev_lru_lambda)),
                (cols[:, 0, :], vec(ev_conv_b)),
                (cols[:, 1, :], vec(ev_rgate_b)),
                (cols[:, 2, :], vec(ev_igate_b)),
                (cw[:, 0, :], ev_conv_w[0, 0].rearrange("(n p) -> p n", p=P)),
                (cw[:, 1, :], ev_conv_w[0, 1].rearrange("(n p) -> p n", p=P)),
                (cw[:, 2, :], ev_conv_w[0, 2].rearrange("(n p) -> p n", p=P)),
                (cw[:, 3, :], ev_conv_w[0, 3].rearrange("(n p) -> p n", p=P)),
                (rw[:], ev_rgate_w[0].rearrange("n c d -> c n d")),
                (iw[:], ev_igate_w[0].rearrange("n c d -> c n d")),
            ):
                pool.dma_start(dst, src, allow_slow_non_contiguous=True).then_inc(ev_in, 16)
            link(pool.memset(wfh[:].bitcast(F32), 0.0))
            link(pool.memset(wfl[:].bitcast(F32), 0.0))
            link(pool.memset(uT[:, :, 0:CONV - 1], 0.0))
            link(pool.memset(cmask[:], 0.0))
            link(pool.memset(tri[:], 1.0))
            link(pool.affine_select(out=cmask[:, P:T], in_=cmask[:, P:T], compare_op=ALU.is_ge, fill=NEG, base=0,
                                    pattern=[[-1, P]], channel_multiplier=1))
            link(pool.affine_select(out=tri[:, 0:P], in_=tri[:, 0:P], compare_op=ALU.is_ge, fill=0.0, base=0,
                                    pattern=[[1, P]], channel_multiplier=-1))
            pool.sem_inc(consts, 1)
            vec = lambda w: w[0].rearrange("(n p) -> p n", p=P)

            def gains(g, b, l):
                pool.dma_start(gb[:, 0, :], g[l:l + 1, :].broadcast_to([P, D])).then_inc(gb_in, 16)
                pool.dma_start(gb[:, 1, :], b[l:l + 1, :].broadcast_to([P, D])).then_inc(gb_in, 16)

            pool.wait_ge(sc_ready, len(FOX))
            pool.wait_ge(rg_h, 1)
            gains(ln_mix_g, ln_mix_b, 0)
            pool.wait_ge(tr_ready, TR0["gu0"] + 2 * FFN_BLOCKS)
            gains(ln_ffn_g, ln_ffn_b, 0)
            pool.wait_ge(w_used, BLOCK_END[BLOCK0["down0"] + 3])
            link(pool.memset(bmask[:], 0.0))
            link(pool.memset(wmask[:], 0.0))
            for g in range(2):
                link(pool.memset(bmask[0:64, g, P + 64:T], NEG))
                link(pool.memset(wmask[0:64, g, 0:64], NEG))
                link(pool.memset(wmask[0:64, g, P + 64:T], NEG))
                link(pool.memset(wmask[64:P, g, 0:P], NEG))
            link(pool.memset(kz[:], 0.0))
            link(pool.memset(krz[:], 0.0))
            for n in range(ROPE // 2):
                link(pool.memset(invf[:, n:n + 1], float(THETA ** (-2.0 * n / ROPE))))
            pool.sem_inc(consts, 1)
            for dst, src in (
                (pos_i[:], positions.rearrange("b (t p) -> p (b t)", p=P)),
                (sinks[:], od_sinks[0:1, :].broadcast_to([P, SWA_Q])),
                (qkg[:, 0:4], vec(od_q_norm)),
                (qkg[:, 4:6], vec(od_kv_norm)),
            ):
                pool.dma_start(dst, src, allow_slow_non_contiguous=True).then_inc(od_in, 16)
            pool.wait_ge(y_ready, 16)
            gains(ln_mix_g, ln_mix_b, 1)
            pool.wait_ge(tr_ready, TR0["gu1"] + 2 * FFN_BLOCKS)
            gains(ln_ffn_g, ln_ffn_b, 1)

        @block.tensor
        def _(pe):
            mm = nc.tensor.matmul

            def unit_ready(u):
                pe.wait_ge(w_lo, number(u) + 1)

            def rows_unit(u, pair, k0, first, last, src=(xTh, xTl), width=COLS, kts=UK, first_tile=None, between=None):
                unit_ready(u)
                s = u[0]
                for t in range(TT):
                    if t == 1 and between:
                        between()
                    for kk in range(kts):
                        wh, wl = (w[:, s, kk * width:(kk + 1) * width] for w in (whi, wlo))
                        xh, xl = (a[:, k0 + kk, t * P:(t + 1) * P] for a in src)
                        o = acc[pair][t][:, 0:width]
                        mm(o, xh, wh, start=first and kk == 0, stop=False)
                        mm(o, xh, wl, start=False, stop=False)
                        ins = mm(o, xl, wh, start=False, stop=last and kk == kts - 1)
                    if t == 0 and last and first_tile:
                        ins.then_inc(first_tile, 1)
                ins.then_inc(w_used, 1)

            def cols_unit(u, pair, k0, first, last, src=(xTh, xTl), between=None):
                if between:
                    between()
                unit_ready(u)
                s = u[0]
                for kk in range(UK):
                    for c in range(4):
                        wh, wl = (w[:, s, kk * COLS + c * P:kk * COLS + (c + 1) * P] for w in (whi, wlo))
                        xh, xl = (a[:, k0 + kk, :] for a in src)
                        o = acc[pair][c // 2][:, (c % 2) * T:(c % 2 + 1) * T]
                        mm(o, wh, xh, start=first and kk == 0 and c % 2 == 0, stop=False, skip_group_check=True)
                        mm(o, wl, xh, start=False, stop=False, skip_group_check=True)
                        ins = mm(o, wh, xl, start=False, stop=last and kk == UK - 1, skip_group_check=True)
                ins.then_inc(w_used, 1)

            def open_block(b, i=0, per=0):
                before = uses(b) + i * (per // 2)
                if not (isinstance(before, int) and before == 0):
                    pe.wait_ge(acc_free[b % 2], before)

            def block_of(unit_fn, u0, b, i=0, per_u=0, per_b=0, n_units=UPB, after=None, before=None,
                         between=None, src=None, **kw):
                open_block(b, i, per_b)
                for j in range(n_units):
                    if before:
                        before(j)
                    s_, k0 = src(j) if src else ((xTh, xTl), j * UK)
                    if j == 0 and between:
                        kw["between"] = between
                    unit_fn(at(u0 + j, i, per_u), b % 2, k0, j == 0, j == n_units - 1, src=s_, **kw)
                    kw.pop("between", None)
                    if after:
                        after(j)

            def transposes(n, parts, parity=None):
                if not (isinstance(n, int) and n < 2):
                    pe.wait_ge(tr_free, n - 1)
                dst = trb[n % 2 if parity is None else parity]
                for q, src in enumerate(parts):
                    ins = nc.tensor.transpose(dst[:, q * P:(q + 1) * P], src, ident[:])
                ins.then_inc(tr_ready, 1)

            def turned(n0, arrived):
                def turn(c):
                    for t in range(TT):
                        arrived(2 * c + t)
                        transposes(n0 + 2 * c + t,
                                   [xres[:, t, (4 * c + q) * P:(4 * c + q + 1) * P] for q in range(4)])

                def before(j):
                    if j == 0:
                        turn(0)
                        pe.wait_ge(tr_free, n0 + 1)
                    elif j % 2 == 0:
                        pe.wait_ge(tr_free, n0 + j + 2)
                    elif j < 6:
                        turn((j + 1) // 2)
                return dict(before=before, between=lambda: pe.wait_ge(tr_free, n0 + 2))

            def normalised(y0):
                return lambda n: pe.wait_ge(y_ready, y0 + n + 1)

            def attention_step(n0, units, s, scores, values):
                N = len(units)
                if s < N:
                    n = n0 + s
                    if s >= 2:
                        pe.wait_ge(ex_ready, n - 1)
                    scores(units[s], scb[n % 2], (units[s][2] + 1) * P)
                if 2 <= s < N + 2:
                    n = n0 + s - 2
                    kind, j, t = units[s - 2]
                    pe.wait_ge(pr_ready, n + 1)
                    if s >= 3:
                        pe.wait_ge(pt_copied, n)
                    for g in range(2):
                        for k in range(t + 1):
                            q = g * (t + 1) + k
                            ins = nc.tensor.transpose(trb[0][:, q * P:(q + 1) * P],
                                                      p_sb[:, n % 2, g, k * P:(k + 1) * P], ident[:])
                    ins.then_inc(pt_ready, 1)
                if 3 <= s < N + 3:
                    n = n0 + s - 3
                    kind, j, t = units[s - 3]
                    pe.wait_ge(pt_copied, n + 1)
                    if s >= 4:
                        pe.wait_ge(o_lo, n)
                    for g in range(2):
                        for k in range(t + 1):
                            ins = mm(trb[1][:, g * P:(g + 1) * P], values(units[s - 3], g, k),
                                     pT[:, n % 2, g * (t + 1) + k, :], start=k == 0, stop=k == t)
                    ins.then_inc(o_ready, 1)

            pe.wait_ge(consts, 1)
            for b in range(2):
                block_of(cols_unit, UNIT0["e_u"] + b * UPB, BLOCK0["e_u"] + b,
                         **(turned(TR0["x"], lambda n: pe.wait_ge(x_in[n // 2], 16)) if b == 0 else {}))
            pe.wait_ge(wf_split, 1)
            for k in range(KD):
                mm(scb[0][:, 0:T], wfh[:, k, :], xTh[:, k, :], start=k == 0, stop=False)
                mm(scb[0][:, 0:T], wfl[:, k, :], xTh[:, k, :], start=False, stop=False)
                ins = mm(scb[0][:, 0:T], wfh[:, k, :], xTl[:, k, :], start=False, stop=k == KD - 1)
            ins.then_inc(f_ready, 1)

            def f_turned(j):
                if j == 0:
                    pe.wait_ge(f_copied, 1)
                    for t in range(TT):
                        ins = nc.tensor.transpose(scb[1][:, t * P:(t + 1) * P], fT[:, t * P:(t + 1) * P], ident[:])
                    ins.then_inc(f_ready, 1)

            def cumulative(j):
                if j == 2:
                    pe.wait_ge(consts, 2)
                    pe.wait_ge(f_log, 1)
                    lf = fz[:, 6, :].rearrange("p (t h) -> p t h", t=TT)
                    mm(scb[1][:, 0:8], tri[:, 0:P], lf[:, 0, :], start=True, stop=True)
                    mm(scb[1][:, 8:16], tri[:, P:T], lf[:, 0, :], start=True, stop=False)
                    mm(scb[1][:, 8:16], tri[:, 0:P], lf[:, 1, :], start=False, stop=True).then_inc(c_ready, 1)

            for b, after in enumerate((f_turned, cumulative)):
                block_of(cols_unit, UNIT0["e_q"] + b * UPB, BLOCK0["e_q"] + b, after=after)

            def gates(n):
                pe.wait_ge(conv_done, n + 1)
                if n == 0:
                    pe.wait_ge(c_done, 1)
                if n >= 2:
                    pe.wait_ge(gates_free, n - 1)
                mm(scb[n % 2][:, 0:T], rw[:, n, :], uc[:, n, :], start=True, stop=True)
                mm(scb[n % 2][:, T:2 * T], iw[:, n, :], uc[:, n, :], start=True, stop=True).then_inc(gates_ready, 1)

            block_of(cols_unit, UNIT0["e_k"], BLOCK0["e_k"], after=gates)
            block_of(cols_unit, UNIT0["e_k"] + UPB, BLOCK0["e_k"] + 1)
            for b in range(2):
                block_of(rows_unit, UNIT0["e_v"] + b * UPB, BLOCK0["e_v"] + b)

            def fox_scores(unit, bank_, W):
                kind, j, t = unit
                for g in range(2):
                    h = 2 * j + g
                    o = bank_[:, g * T:g * T + W]
                    mm(o, qT[:, h, t * P:(t + 1) * P], kT[:, h, 0:W], start=True, stop=False)
                    if t == 1:
                        mm(bank_[:, g * T + P:g * T + T], nlf[:, 1, h, :], tri[:, 0:P], start=False, stop=False,
                           skip_group_check=True)
                    ins = mm(o, nlf[:, 0, h, :], tri[:, 0:W], start=False, stop=True)
                ins.then_inc(sc_ready, 1)

            def fox_values(unit, g, k):
                h = 2 * unit[1] + g
                return vt[:, k, h * P:(h + 1) * P]

            def fox_after(b):
                def after(j):
                    if b * UPB + j in FOX_AFTER:
                        s = FOX_AFTER.index(b * UPB + j)
                        if s == 0:
                            pe.wait_ge(f_rep, 1)
                            pe.wait_ge(gates_free, 8)
                            pe.wait_ge(acc_free[BLOCK0["e_v"] % 2], uses(BLOCK0["e_v"]) + 1)
                            pe.wait_ge(acc_free[1 - BLOCK0["e_v"] % 2], uses(BLOCK0["e_v"]) + 1)
                        attention_step(0, FOX, s, fox_scores, fox_values)
                return after

            for b in range(2):
                block_of(cols_unit, UNIT0["e_g"] + b * UPB, BLOCK0["e_g"] + b, after=fox_after(b))

            def e_out_ready(j):
                if j == 0:
                    pe.wait_ge(rg_lo, 1)
                if j == 2:
                    pe.wait_ge(o_lo, len(FOX))
                if j == 6:
                    pe.wait_ge(rg_lo, 2)

            with pe.Fori(0, 2) as i:
                for b in range(2):
                    block_of(rows_unit, UNIT0["e_out"] + b * UPB, BLOCK0["e_out"] + b, i=i, per_u=2 * UPB, per_b=2,
                             before=e_out_ready if b == 0 else None, first_tile=tile0_done,
                             src=lambda j: ((eTh[E_OUT_K[j] // 8], eTl[E_OUT_K[j] // 8]), E_OUT_K[j] % 8))

            def ffn(l, y0):
                u0, b0, t0 = UNIT0[f"gu{l}"], BLOCK0[f"gu{l}"], TR0[f"gu{l}"]

                def hidden(i):
                    for t in range(TT):
                        if t == 0:
                            pe.wait_ge(h0_ready, i + (l * FFN_BLOCKS + 1))
                        else:
                            pe.wait_ge(acc_free[1], i + uses(b0 + 1) + 1)
                        transposes(i * 2 + (t0 + t), [hbuf[:, t, q * P:(q + 1) * P] for q in range(4)],
                                   (t0 + t) % 2)

                def body(i, first):
                    block_of(rows_unit, u0, b0, i=i, per_u=2 * UPB, per_b=2,
                             **(turned(TR0[f"ln{2 * l}"], normalised(y0)) if first else
                                dict(after=lambda j: hidden(i - 1) if j == 1 else None)))
                    block_of(rows_unit, u0 + UPB, b0 + 1, i=i, per_u=2 * UPB, per_b=2, first_tile=up0_done)

                body(0, True)
                with pe.Fori(1, FFN_BLOCKS) as i:
                    body(i, False)
                hidden(FFN_BLOCKS - 1)
                pe.wait_ge(tr_free, t0 + 2 * FFN_BLOCKS - 2)

                def last_hidden(j):
                    if j == DOWN_UNITS - 2:
                        pe.wait_ge(tr_free, t0 + 2 * FFN_BLOCKS)

                with pe.Fori(0, 2) as i:
                    for b in range(2):
                        block_of(rows_unit, UNIT0[f"down{l}"] + b * DOWN_UNITS, BLOCK0[f"down{l}"] + b,
                                 n_units=DOWN_UNITS, i=i, per_u=2 * DOWN_UNITS, per_b=2,
                                 before=last_hidden, src=lambda j: ((hTh, hTl), j * UK), first_tile=tile0_done)

            ffn(0, 0)

            def compressed(j):
                m = j - 4
                if 0 <= m < 3:
                    b = BLOCK0["o_cq"]
                    pe.wait_ge(acc_free[b % 2], uses(b) + 1)
                    if m == 2:
                        pe.wait_ge(c_norm, 1)
                    transposes(TR0["rms"] + m, [
                        cqs[:, t, k * P:(k + 1) * P] if k < 4 else ckvs[:, t, (k - 4) * P:(k - 3) * P]
                        for k in (2 * m, 2 * m + 1) for t in range(TT)])

            for name, width in (("o_ckv", KV_RANK + ROPE), ("o_cq", QR_RANK), ("o_kv", 2 * SWA_KV * SWA_DH)):
                block_of(rows_unit, UNIT0[name], BLOCK0[name], width=width,
                         **(turned(TR0["ln1"], normalised(8)) if name == "o_ckv" else {}),
                         after=compressed if name == "o_kv" else None)
            pe.wait_ge(tr_free, TR0["rms"] + 2)
            b = BLOCK0["qb_nope"]
            open_block(b)
            for k in range(QR_RANK // P):
                u = at(UNIT0["qb_nope"] + k)
                unit_ready(u)
                for h in range(MLA_H):
                    if (k, h) == (0, 4):
                        open_block(b + 1)
                    wh, wl = (w[:, u[0], h * P:(h + 1) * P] for w in (whi, wlo))
                    o = acc[(b + h // 4) % 2][h % 4 // 2][:, (h % 2) * T:(h % 2 + 1) * T]
                    mm(o, wh, cTh[:, k, :], start=k == 0 and h % 2 == 0, stop=False, skip_group_check=True)
                    mm(o, wl, cTh[:, k, :], start=False, stop=False, skip_group_check=True)
                    ins = mm(o, wh, cTl[:, k, :], start=False, stop=k == QR_RANK // P - 1, skip_group_check=True)
                ins.then_inc(w_used, 1)
            b = BLOCK0["o_kv"]
            pe.wait_ge(acc_free[b % 2], uses(b) + 1)
            transposes(TR0["kswa"], [kvs[:, t, v * P:(v + 1) * P] for v in range(2) for t in range(TT)])
            b = BLOCK0["qb_rope"]
            open_block(b)
            for k in range(QR_RANK // P):
                rows_unit(at(UNIT0["qb_rope"] + k), b % 2, k, k == 0, k == QR_RANK // P - 1, src=(cTh, cTl), kts=1)
            pe.wait_ge(tr_free, TR0["rms"] + 3)
            for b in range(4):
                u, blk = at(UNIT0["kvb"] + b), BLOCK0["kvb"] + b
                open_block(blk)
                unit_ready(u)
                s = u[0]
                for g in range(2):
                    for k in range(UK):
                        wh, wl = (w[:, s, k * COLS + g * T:k * COLS + g * T + P] for w in (whi, wlo))
                        xh, xl = cTh[:, 4 + k, :], cTl[:, 4 + k, :]
                        o = acc[blk % 2][0][:, g * T:(g + 1) * T]
                        mm(o, wh, xh, start=k == 0, stop=False)
                        mm(o, wl, xh, start=False, stop=False)
                        mm(o, wh, xl, start=False, stop=k == UK - 1)
                for t in range(TT):
                    for k in range(UK):
                        wh, wl = (w[:, s, k * COLS:(k + 1) * COLS].rearrange("p (g n) -> p g n", g=2)[:, :, P:T]
                                  for w in (whi, wlo))
                        xh, xl = (a[:, 4 + k, t * P:(t + 1) * P] for a in (cTh, cTl))
                        o = acc[blk % 2][1][:, t * T:(t + 1) * T].rearrange("p (g n) -> p g n", g=2)
                        mm(o, xh, wh, start=k == 0, stop=False)
                        mm(o, xh, wl, start=False, stop=False)
                        ins = mm(o, xl, wh, start=False, stop=k == UK - 1)
                ins.then_inc(w_used, 1)

            def rope_turned():
                pe.wait_ge(rope_out, 1)
                for m in range(3):
                    transposes(TR0["rope"] + m, [qro[:, t, 2 * c:2 * c + 2, :].rearrange("p a b -> p (a b)")
                                                 for c in range(2 * m, min(2 * m + 2, 5)) for t in range(TT)])

            def odd_scores(unit, bank_, W):
                kind, j, t = unit
                mask = wmr if (kind, t) == ("swa", 1) else bmr
                both = bank_[:].rearrange("p (g k) -> p g k", g=2)[:, :, 0:W]
                mm(both, identr[:], mask[:, :, T - W:T], start=True, stop=False, skip_group_check=True)
                for g in range(2):
                    o = bank_[:, g * T:g * T + W]
                    if kind == "swa":
                        kv = 2 * j // (SWA_Q // SWA_KV)
                        ins = mm(o, qT[:, j, t * P:(t + 1) * P], kz[:, kv, g, 0:W], start=False, stop=True,
                                 skip_group_check=True)
                    else:
                        h = 2 * j + g
                        mm(o, qnT[:, h, t * P:(t + 1) * P], knT[:, h, 0:W], start=False, stop=False,
                           skip_group_check=True)
                        ins = mm(o, qrT[:, j, t * P:(t + 1) * P], krz[:, g, 0:W], start=False, stop=True,
                                 skip_group_check=True)
                ins.then_inc(sc_ready, 1)

            def odd_values(unit, g, k):
                kind, j, t = unit
                if kind == "swa":
                    return vd[:, k, 2 * j // (SWA_Q // SWA_KV), :]
                return vm[:, k, 2 * j + g, :]

            def odd_step(s):
                if s == 0:
                    pe.wait_ge(tr_free, TR0["rope"] + 3)
                    pe.wait_ge(masks_r, 1)
                    for p in range(2):
                        pe.wait_ge(acc_free[p], uses(BLOCK0["o_q"] + p))
                if s == 8:
                    b = BLOCK0["o_q"]
                    pe.wait_ge(acc_free[b % 2], uses(b) + 1)
                if s == 16:
                    b = BLOCK0["o_q"] + 1
                    pe.wait_ge(acc_free[b % 2], uses(b) + 1)
                attention_step(len(FOX), ODD, s, odd_scores, odd_values)

            for b in range(2):
                block_of(cols_unit, UNIT0["o_q"] + b * UPB, BLOCK0["o_q"] + b,
                         after=lambda j: (rope_turned() if j == 0 else odd_step(j - 1)) if b == 0 else odd_step(UPB - 1 + j))

            b0 = BLOCK0["o_out"]
            steps = 2 * UPB - 1
            for j, (b, k) in enumerate(O_OUT_HEAD):
                if k == 8:
                    open_block(b0 + b)
                if j == 0:
                    pe.wait_ge(o_lo, len(FOX) + 8)
                if j == 8:
                    pe.wait_ge(o_lo, len(FOX) + 16)
                if j == 12:
                    pe.wait_ge(o_lo, len(FOX) + len(ODD))
                src, k0 = ((mTh, mTl), k - 8) if k >= 8 else ((sTh, sTl), k) if k < 4 else ((xTh, xTl), k)
                rows_unit(at(UNIT0["o_out"] + j), (b0 + b) % 2, k0, k == 8, k == 6, src=src, first_tile=tile0_done)
                if steps < ODD_STEPS:
                    odd_step(steps)
                    steps += 1
            for b in range(2, 4):
                block_of(rows_unit, UNIT0["o_out"] + b * UPB, b0 + b, first_tile=tile0_done,
                         src=lambda j: ((mTh, mTl), j * UK - 8) if j >= 4 else ((sTh, sTl), j * UK) if j < 2
                         else ((xTh, xTl), j * UK))
            assert steps == ODD_STEPS, steps
            ffn(1, 16)

        @block.scalar
        def _(act):
            chain = [0]
            activate = nc.scalar.activation

            def link(ins):
                chain[0] += 1
                ins.then_inc(av, 1)
                act.wait_ge(av, chain[0])

            def high(u, span=UK * COLS):
                slot, rounds = u
                act.wait_ge(w_in[slot], rounds * 16 + 16)
                if not (isinstance(rounds, int) and rounds == 0):
                    act.wait_ge(w_used, number(u) - (SLOTS - 1))
                activate(whi[:, slot, 0:span], raw[:, slot, 0:span], ACT.Copy).then_inc(w_hi, 1)

            def ahead(u0, j, i=0, per=0):
                if not (isinstance(i, int) and i * per + u0 + j + SLOTS >= UNITS):
                    high(at(u0 + j + SLOTS, i, per), SPAN[i * per + u0 + j + SLOTS] if isinstance(i, int) else UK * COLS)

            def split_out(n, h, dst, parity=None):
                act.wait_ge(tr_ready, n + 1)
                activate(dst, trb[n % 2 if parity is None else parity][:].rearrange("p (k t) -> p k t", k=4),
                         ACT.Copy).then_inc(tr_hi, 1)

            def stream_high(n0, h0, c):
                for t in range(TT):
                    split_out(n0 + 2 * c + t, h0 + 2 * c + t, xTh[:, 4 * c:4 * c + 4, t * P:(t + 1) * P])

            def first_block(n0, h0, u0, hook=None):
                for c in range(4):
                    stream_high(n0, h0, c)
                    if hook and c < 2:
                        high(at(2 * c))
                        high(at(2 * c + 1))
                    for j in {1: (0,), 2: (1, 2), 3: (3, 4, 5, 6, 7)}.get(c, ()):
                        if hook and j == 6:
                            hook()
                        ahead(u0, j)

            act.wait_ge(consts, 1)
            activate(identr[:], ident[:], ACT.Copy)

            def read_cols(b, dst, func=ACT.Copy, scale=1.0):
                act.wait_ge(w_used, BLOCK_END[b])
                for k in range(2):
                    ins = activate(dst(k), acc[b % 2][k][:].rearrange("p (c t) -> p c t", c=2), func, scale=scale)
                ins.then_inc(acc_free[b % 2], 1)

            def forget_high():
                act.wait_ge(wf_in, 16)
                act.wait_ge(consts, 2)
                activate(wfh[:, :, 0:FOX_HEADS], wf[:], ACT.Copy).then_inc(wf_hi, 1)

            for b in range(2):
                if b == 0:
                    first_block(TR0["x"], HI0["x"], UNIT0["e_u"], forget_high)
                else:
                    for j in range(UPB):
                        ahead(UNIT0["e_u"] + b * UPB, j)
                read_cols(BLOCK0["e_u"] + b, lambda k: uT[:, 4 * b + 2 * k:4 * b + 2 * k + 2, CONV - 1:])
            for b in range(2):
                for j in range(UPB):
                    ahead(UNIT0["e_q"] + b * UPB, j)
                    if b == 0 and j == 1:
                        act.wait_ge(f_neg, 1)
                        activate(fz[:, 2, :], fz[:, 1, :], ACT.Exp).then_inc(f_exp, 1)
                    if b == 0 and j == 3:
                        act.wait_ge(lam_x, 1)
                        activate(lz[:, 2, :], lz[:, 1, :], ACT.Exp).then_inc(lam_e, 1)
                    if b == 1 and j == 2:
                        act.wait_ge(f_log, 1)
                        activate(nlf[:].rearrange("p t h q -> p (t h) q"),
                                 fz[:, 6, :].unsqueeze(2).broadcast_to([P, TT * FOX_HEADS, P]),
                                 ACT.Copy, scale=-1.0).then_inc(f_rep, 1)
                read_cols(BLOCK0["e_q"] + b, lambda k: qT[:, 4 * b + 2 * k:4 * b + 2 * k + 2, :], scale=SCALES["fox"])
            for b in range(2):
                for j in range(UPB):
                    ahead(UNIT0["e_k"] + b * UPB, j)
                    if b == 0:
                        act.wait_ge(gates_ready, j + 1)
                        activate(rt[:, j, :], scb[j % 2][:, 0:T], ACT.Sigmoid, bias=cols[:, 1, j:j + 1])
                        activate(it[:, j, :], scb[j % 2][:, T:2 * T], ACT.Sigmoid,
                                 bias=cols[:, 2, j:j + 1]).then_inc(gates_free, 1)
                    if b == 1 and j < 4:
                        if j == 0:
                            act.wait_ge(lam_done, 1)
                            act.wait_ge(gates_free, 8)
                            act.wait_ge(conv_done, 8)
                            act.wait_ge(c_done, 1)
                        for n in (2 * j, 2 * j + 1):
                            ins = activate(gT[:, n, :], rt[:, n, :], ACT.Tanh, scale=clam[:, 0, n:n + 1])
                        ins.then_inc(rg_t, 1)
                    if b == 1 and j >= 4:
                        for n in (2 * j - 8, 2 * j - 7):
                            ins = activate(uT[:, n, 0:T], rt[:, n, :], ACT.Exp, scale=clam[:, 1, n:n + 1])
                        if j == 7:
                            ins.then_inc(rg_at, 1)
                read_cols(BLOCK0["e_k"] + b, lambda k: kT[:, 4 * b + 2 * k:4 * b + 2 * k + 2, :])
            for b in range(2):
                for j in range(UPB):
                    ahead(UNIT0["e_v"] + b * UPB, j)
                    if b == 1 and j == 1:
                        act.wait_ge(rg_var, 1)
                        activate(gT[:], gT[:], ACT.Sqrt).then_inc(rg_sq, 1)
                blk = BLOCK0["e_v"] + b
                act.wait_ge(w_used, BLOCK_END[blk])
                for t in range(TT):
                    ins = activate(vt[:, t, b * COLS:(b + 1) * COLS], acc[blk % 2][t][:], ACT.Copy)
                ins.then_inc(acc_free[blk % 2], 1)

            def attention_step(n0, units, s):
                N = len(units)
                if 2 <= s < N + 2:
                    n = n0 + s - 2
                    kind, j, t = units[s - 2]
                    act.wait_ge(pt_ready, n + 1)
                    if s >= 4:
                        act.wait_ge(o_ready, n - 1)
                    W = 2 * (t + 1) * P
                    activate(pT[:, n % 2, 0:2 * (t + 1), :].rearrange("p a b -> p (a b)"),
                             trb[0][:, 0:W], ACT.Copy).then_inc(pt_copied, 1)
                if s < N:
                    n = n0 + s
                    kind, j, t = units[s]
                    act.wait_ge(nm_ready, n + 1)
                    if s >= 2:
                        act.wait_ge(pt_ready, n - 1)
                    W = (t + 1) * P
                    for g in range(2):
                        if kind == "swa":
                            h = 2 * j + g
                            activate(es[:, n % 2, g:g + 1], sinks[:, h:h + 1], ACT.Exp, bias=nm[:, n % 2, g:g + 1])
                        src = s_sb[:, n % 2, g, 0:W] if kind == "fox" else scb[n % 2][:, g * T:g * T + W]
                        ins = activate(p_sb[:, n % 2, g, 0:W], src, ACT.Exp,
                                       bias=nm[:, n % 2, g:g + 1], accum_out=lsum[:, n % 2, g:g + 1])
                    ins.then_inc(ex_ready, 1)
                if 3 <= s < N + 3:
                    n = n0 + s - 3
                    act.wait_ge(o_ready, n + 1)
                    t = units[s - 3][2]
                    for rows, hi, lo, k0, k1, cols_ in out_parts(units[s - 3]):
                        ins = activate(hi[rows, k0:k1, t * P:(t + 1) * P],
                                       trb[1][rows, cols_].rearrange("p (a b) -> p a b", b=P), ACT.Copy)
                    ins.then_inc(o_hi, 1)

            for b in range(2):
                for j in range(UPB):
                    if b * UPB + j in FOX_AFTER:
                        attention_step(0, FOX, FOX_AFTER.index(b * UPB + j))
                    ahead(UNIT0["e_g"] + b * UPB, j)
                read_cols(BLOCK0["e_g"] + b, lambda k: gT[:, 4 * b + 2 * k:4 * b + 2 * k + 2, :],
                          ACT.Gelu_apprx_tanh)
                act.wait_ge(rg_out, b + 1)
                activate(eTh[1][:, 4 * b:4 * b + 4, :], gT[:, 4 * b:4 * b + 4, :], ACT.Copy).then_inc(rg_hi, 1)

            with act.Fori(0, 2) as i:
                for j in range(2 * UPB):
                    ahead(UNIT0["e_out"], j, i, 2 * UPB)

            def ln_root(l):
                activate(lnv[:, 3, 0:1], ident[:, 0:1], ACT.Sqrt)
                act.wait_ge(ln_var, l + 1)
                activate(lnv[:, 1, :], lnv[:, 0, :], ACT.Sqrt).then_inc(ln_sd, 1)

            def ffn(l):
                u0, b0, t0 = UNIT0[f"gu{l}"], BLOCK0[f"gu{l}"], TR0[f"gu{l}"]

                def hidden(i):
                    for t in range(TT):
                        split_out(i * 2 + (t0 + t), None, hTh[:, bass.ds(i * 4, 4), t * P:(t + 1) * P],
                                  (t0 + t) % 2)

                def body(i, first):
                    if first:
                        ln_root(2 * l)
                        first_block(TR0[f"ln{2 * l}"], HI0[f"ln{2 * l}"], u0)
                    else:
                        for j in range(UPB):
                            ahead(u0, j, i, 2 * UPB)
                            if j == 2:
                                hidden(i - 1)
                    act.wait_ge(w_used, i * (2 * UPB) + BLOCK_END[b0])
                    act.wait_ge(acc_free[1], i + uses(b0 + 1))
                    for t in range(TT):
                        ins = activate(sg[:, t, :], acc[0][t][:], ACT.Silu)
                    ins.then_inc(acc_free[0], 1)
                    for j in range(UPB, 2 * UPB):
                        ahead(u0, j, i, 2 * UPB)

                body(0, True)
                with act.Fori(1, FFN_BLOCKS) as i:
                    body(i, False)
                hidden(FFN_BLOCKS - 1)
                d0 = UNIT0[f"down{l}"]
                if l == 0:
                    with act.Fori(0, 2) as i:
                        for j in range(2 * DOWN_UNITS):
                            ahead(d0, j, i, 2 * DOWN_UNITS)
                else:
                    for j in range(4 * DOWN_UNITS):
                        ahead(d0, j)

            ffn(0)

            ln_root(1)
            first_block(TR0["ln1"], HI0["ln1"], UNIT0["o_ckv"])
            b = BLOCK0["o_ckv"]
            act.wait_ge(w_used, BLOCK_END[b])
            for t in range(TT):
                src = acc[b % 2][t]
                activate(ckvs[:, t, :], src[:, 0:KV_RANK], ACT.Copy)
                activate(p_sb[:, 1, t, :], src[:, 0:KV_RANK], ACT.Square, accum_out=rms[:, 0, 2 + t:3 + t])
                for c in range(2):
                    ins = activate(qr[:, t, 8 + c, :], src[:, KV_RANK:KV_RANK + ROPE], ACT.Copy)
            ins.then_inc(acc_free[b % 2], 1)
            for j in range(UPB - 1):
                ahead(UNIT0["o_cq"], j)
                if j == 3:
                    act.wait_ge(trig_arg, 1)
                    activate(trig[:, 4:6, :, :], trig[:, 2:4, :, :], ACT.Sin).then_inc(trig_done, 1)
                if j == 4:
                    act.wait_ge(consts, 3)
                    activate(bmr[:], bmask[:], ACT.Copy)
                    activate(wmr[:], wmask[:], ACT.Copy).then_inc(masks_r, 1)
                if j == 5:
                    activate(lnv[:, 3, 0:1], ident[:, 0:1], ACT.Sqrt)
            b = BLOCK0["o_cq"]
            act.wait_ge(w_used, BLOCK_END[b])
            act.wait_ge(masks_r, 1)
            for t, scratch in enumerate((p_sb, s_sb)):
                ins = activate(scratch[:, 0, :, :].rearrange("p a b -> p (a b)"), acc[b % 2][t][:], ACT.Square,
                               accum_out=rms[:, 0, t:t + 1])
            ins.then_inc(sq_done, 1)
            act.wait_ge(rms_var, 1)
            activate(rms[:, 2, :], rms[:, 1, :], ACT.Sqrt).then_inc(rms_sd, 1)
            ahead(UNIT0["o_cq"], UPB - 1)
            for j in range(UPB - 1):
                m = j - 4
                if m >= 0:
                    n = TR0["rms"] + m
                    act.wait_ge(tr_ready, n + 1)
                    for k in range(2):
                        ins = activate(cTh[:, 2 * m + k, :], trb[n % 2][:, k * T:(k + 1) * T], ACT.Copy,
                                       scale=qkg[:, 2 * m + k:2 * m + k + 1])
                    ins.then_inc(tr_hi, 1)
                if j < UPB - 2:
                    ahead(UNIT0["o_kv"], j)
            b = BLOCK0["o_kv"]
            act.wait_ge(w_used, BLOCK_END[b])
            for t in range(TT):
                src = acc[b % 2][t]
                activate(kvs[:, t, 0:P], src[:, 0:P], ACT.Copy)
                activate(kvs[:, t, P:P + 64], src[:, 64:P], ACT.Copy)
                activate(kvs[:, t, P + 64:2 * P], src[:, 0:64], ACT.Copy)
                for half in range(2):
                    ins = activate(vd[:, t, :, half * 64:(half + 1) * 64],
                                   src[:, P:2 * P].rearrange("p (v d) -> p v d", v=2), ACT.Copy)
            ins.then_inc(acc_free[b % 2], 1)
            ahead(UNIT0["o_kv"], UPB - 2)
            ahead(UNIT0["o_kv"], UPB - 1)
            for j in range(3):
                ahead(UNIT0["qb_nope"], j)
            for b in range(2):
                read_cols(BLOCK0["qb_nope"] + b, lambda k: qnT[:, 4 * b + 2 * k:4 * b + 2 * k + 2, :],
                          scale=SCALES["mla"])
            ahead(UNIT0["qb_nope"], 3)
            for j in range(3):
                ahead(UNIT0["qb_rope"], j)
            b = BLOCK0["qb_rope"]
            act.wait_ge(w_used, BLOCK_END[b])
            for t in range(TT):
                ins = activate(qr[:, t, 0:8, :], acc[b % 2][t][:].rearrange("p (h d) -> p h d", d=ROPE), ACT.Copy,
                               scale=SCALES["mla"])
            ins.then_inc(acc_free[b % 2], 1)
            ahead(UNIT0["qb_rope"], 3)
            for b in range(4):
                ahead(UNIT0["kvb"], b)
                blk = BLOCK0["kvb"] + b
                act.wait_ge(w_used, BLOCK_END[blk])
                activate(knT[:, 2 * b:2 * b + 2, :], acc[blk % 2][0][:].rearrange("p (g t) -> p g t", g=2), ACT.Copy)
                activate(vm[:, :, 2 * b:2 * b + 2, :].rearrange("p t g d -> p t (g d)"),
                         acc[blk % 2][1][:].rearrange("p (t d) -> p t d", t=2), ACT.Copy).then_inc(acc_free[blk % 2], 1)
            for b in range(2):
                for j in range(UPB):
                    if b * UPB + j >= 1:
                        attention_step(len(FOX), ODD, b * UPB + j - 1)
                    ahead(UNIT0["o_q"] + b * UPB, j)
                read_cols(BLOCK0["o_q"] + b, lambda k: qT[:, 4 * b + 2 * k:4 * b + 2 * k + 2, :], scale=SCALES["swa"])
            for j in range(4 * UPB):
                if 2 * UPB - 1 + j < ODD_STEPS:
                    attention_step(len(FOX), ODD, 2 * UPB - 1 + j)
                ahead(UNIT0["o_out"], j)
            ffn(1)
            ln_root(3)

        @block.vector
        def _(dve):
            chain = [0]
            v = nc.vector

            def link(ins):
                chain[0] += 1
                ins.then_inc(dv, 1)
                dve.wait_ge(dv, chain[0])

            def low(u, span=UK * COLS):
                slot = u[0]
                dve.wait_ge(w_hi, number(u) + 1)
                v.tensor_tensor(wlo[:, slot, 0:span], raw[:, slot, 0:span], whi[:, slot, 0:span].bitcast(F32),
                                ALU.subtract).then_inc(w_lo, 1)

            def ahead(u0, j, i=0, per=0):
                if not (isinstance(i, int) and i * per + u0 + j + SLOTS >= UNITS):
                    low(at(u0 + j + SLOTS, i, per), SPAN[i * per + u0 + j + SLOTS] if isinstance(i, int) else UK * COLS)

            def rest_out(n, h, hi, dst, parity=None):
                dve.wait_ge(tr_hi, h + 1)
                v.tensor_tensor(dst, trb[n % 2 if parity is None else parity][:].rearrange("p (k t) -> p k t", k=4),
                                hi.bitcast(F32), ALU.subtract).then_inc(tr_free, 1)

            def stream_low(n0, h0, n):
                t, c = n % 2, n // 2
                at_ = (slice(None), slice(4 * c, 4 * c + 4), slice(t * P, (t + 1) * P))
                rest_out(n0 + n, h0 + n, xTh[at_], xTl[at_])

            def log1p_of(e, y, q, s, out_):
                link(v.tensor_scalar(y, e, 2.0, None, ALU.add))
                link(v.reciprocal(y, y))
                link(v.tensor_tensor(s, e, y, ALU.mult))
                link(v.tensor_tensor(q, s, s, ALU.mult))
                link(v.tensor_scalar(y, q, 1.0 / (2 * LOG1P_TERMS + 1), None, ALU.mult))
                for k in range(LOG1P_TERMS - 1, 0, -1):
                    link(v.scalar_tensor_tensor(out=y, in0=y, scalar=1.0 / (2 * k + 1), in1=q, op0=ALU.add, op1=ALU.mult))
                link(v.scalar_tensor_tensor(out=y, in0=y, scalar=1.0, in1=s, op0=ALU.add, op1=ALU.mult))
                link(v.tensor_scalar(out_, y, 2.0, None, ALU.mult))

            def first_block(n0, h0, u0, affine=None, hook=None):
                if affine:
                    affine(0)
                for c in range(4):
                    stream_low(n0, h0, 2 * c)
                    stream_low(n0, h0, 2 * c + 1)
                    if affine and c < 3:
                        affine(c + 1)
                    if hook and c < 2:
                        low(at(2 * c))
                        low(at(2 * c + 1))
                    for j in {1: (0,), 2: (1, 2), 3: (3, 4, 5, 6, 7)}.get(c, ()):
                        if hook and j == 6:
                            hook()
                        ahead(u0, j)

            def conv(n):
                link(v.tensor_scalar(uc[:, n, :], uT[:, n, 0:T], cw[:, 0, n:n + 1], cols[:, 0, n:n + 1],
                                     ALU.mult, ALU.add))
                for k in range(1, CONV):
                    ins = v.scalar_tensor_tensor(out=uc[:, n, :], in0=uT[:, n, k:k + T], scalar=cw[:, k, n:n + 1],
                                                 in1=uc[:, n, :], op0=ALU.mult, op1=ALU.add)
                    if k < CONV - 1:
                        link(ins)
                ins.then_inc(conv_done, 1)

            def forget_low():
                dve.wait_ge(wf_hi, 1)
                v.tensor_tensor(wfl[:, :, 0:FOX_HEADS], wf[:], wfh[:, :, 0:FOX_HEADS].bitcast(F32),
                                ALU.subtract).then_inc(wf_split, 1)

            first_block(TR0["x"], HI0["x"], UNIT0["e_u"], hook=forget_low)
            for j in range(UPB):
                ahead(UNIT0["e_u"] + UPB, j)
                if j == 3:
                    dve.wait_ge(acc_free[0], uses(BLOCK0["e_u"]) + 1)
                    dve.wait_ge(ev_in, 11 * 16)
                    dve.wait_ge(consts, 2)
                if j >= 4:
                    conv(j - 4)
            for b in range(2):
                for j in range(UPB):
                    if b == 0 and j == 0:
                        dve.wait_ge(f_ready, 1)
                        v.tensor_copy(fT[:], scb[0][:, 0:T]).then_inc(f_copied, 1)
                    ahead(UNIT0["e_q"] + b * UPB, j)
                    if b == 0 and j == 1:
                        dve.wait_ge(ev_in, 11 * 16)
                        dve.wait_ge(f_ready, 2)
                        for t in range(TT):
                            ins = v.tensor_tensor(fz[:, 0, t * 8:t * 8 + 8], scb[1][:, t * P:t * P + 8], fb[:], ALU.add)
                        link(ins)
                        link(v.tensor_scalar(fz[:, 1, :], fz[:, 0, :], -1.0, None, ALU.mult))
                        v.tensor_tensor(fz[:, 1, :], fz[:, 1, :], fz[:, 0, :], ALU.min).then_inc(f_neg, 1)
                    if b == 0 and j == 1:
                        link(v.tensor_scalar(lz[:, 0, :], cols[:, 3, :], -1.0, None, ALU.mult))
                        v.tensor_tensor(lz[:, 1, :], lz[:, 0, :], cols[:, 3, :], ALU.min).then_inc(lam_x, 1)
                    if b == 0 and j == 4:
                        dve.wait_ge(f_exp, 1)
                        log1p_of(fz[:, 2, :], fz[:, 3, :], fz[:, 4, :], fz[:, 5, :], fz[:, 1, :])
                        v.scalar_tensor_tensor(out=fz[:, 6, :], in0=fz[:, 0, :], scalar=0.0, in1=fz[:, 1, :],
                                               op0=ALU.min, op1=ALU.subtract).then_inc(f_log, 1)
                    if b == 0 and j == 6:
                        dve.wait_ge(lam_e, 1)
                        log1p_of(lz[:, 2, :], lz[:, 3, :], lz[:, 4, :], lz[:, 5, :], lz[:, 1, :])
                        link(v.scalar_tensor_tensor(out=lz[:, 3, :], in0=lz[:, 0, :], scalar=0.0, in1=lz[:, 1, :],
                                                    op0=ALU.max, op1=ALU.add))
                        v.tensor_scalar(clam[:, 0, :], lz[:, 3, :], LRU_C, None, ALU.mult)
                        v.tensor_scalar(clam[:, 1, :], lz[:, 3, :], -LRU_C, None, ALU.mult).then_inc(lam_done, 1)
                    if b == 1:
                        if j == 0:
                            dve.wait_ge(acc_free[1], uses(BLOCK0["e_u"]) + 1)
                        if j < 4:
                            conv(j + 4)
                        if j == 4:
                            dve.wait_ge(c_ready, 1)
                            v.tensor_copy(cq[:].rearrange("p t h -> p (t h)"), scb[1][:, 0:16]).then_inc(c_done, 1)
            def decayed(m):
                n = m // 2
                if m % 2 == 0:
                    dve.wait_ge(rg_t, n // 2 + 1)
                    link(v.tensor_scalar(rgd[:, n, :], gT[:, n, :], 1.0, None, ALU.add))
                    link(v.reciprocal(rgd[:, n, :], rgd[:, n, :]))
                else:
                    link(v.scalar_tensor_tensor(out=gT[:, n, :], in0=gT[:, n, :], scalar=2.0, in1=rgd[:, n, :],
                                                op0=ALU.mult, op1=ALU.mult))
                    ins = v.tensor_scalar(gT[:, n, :], gT[:, n, :], 1e-34, None, ALU.max)
                    if n == 7:
                        ins.then_inc(rg_var, 1)

            for b in range(2):
                for j in range(UPB):
                    ahead(UNIT0["e_k"] + b * UPB, j)
                    if b == 1 and j >= 1:
                        decayed(j - 1)
            for b in range(2):
                for j in range(UPB):
                    ahead(UNIT0["e_v"] + b * UPB, j)
                    n = b * UPB + j
                    if n < 9:
                        decayed(n + UPB - 1)
                    if n == 8:
                        link(v.tensor_tensor(it[:], it[:], uc[:], ALU.mult))
                    if n == 9:
                        dve.wait_ge(rg_at, 1)
                        dve.wait_ge(rg_sq, 1)
                        link(v.tensor_tensor(it[:], it[:], gT[:], ALU.mult))
                    if 10 <= n < 14:
                        for m in (2 * n - 20, 2 * n - 19):
                            ins = v.tensor_tensor_scan(rt[:, m, :], uT[:, m, 0:T], it[:, m, :], 0.0, ALU.mult, ALU.add)
                        if n == 13:
                            ins.then_inc(rg_h, 1)

            def attention_step(n0, units, s, scores):
                N = len(units)
                if s < N:
                    n = n0 + s
                    kind, j, t = units[s]
                    W = (t + 1) * P
                    dve.wait_ge(sc_ready, n + 1)
                    if s >= 2:
                        dve.wait_ge(ex_ready, n - 1)
                    link(v.tensor_reduce(mx[:, n % 2, :], scores(units[s], n, W), AX.X, ALU.max))
                    if kind == "swa":
                        link(v.tensor_tensor(mx[:, n % 2, :], mx[:, n % 2, :], sinks[:, 2 * j:2 * j + 2], ALU.max))
                    v.tensor_scalar(nm[:, n % 2, :], mx[:, n % 2, :], -1.0, None, ALU.mult).then_inc(nm_ready, 1)
                if 1 <= s < N + 1:
                    n = n0 + s - 1
                    kind, j, t = units[s - 1]
                    W = (t + 1) * P
                    dve.wait_ge(ex_ready, n + 1)
                    if kind == "swa":
                        link(v.tensor_tensor(lsum[:, n % 2, :], lsum[:, n % 2, :], es[:, n % 2, :], ALU.add))
                    link(v.reciprocal(rl[:, n % 2, :], lsum[:, n % 2, :]))
                    v.tensor_tensor(p_sb[:, n % 2, :, 0:W], p_sb[:, n % 2, :, 0:W],
                                    rl[:, n % 2, :].unsqueeze(2).broadcast_to([P, 2, W]), ALU.mult).then_inc(pr_ready, 1)
                if s >= 3:
                    n = n0 + s - 3
                    t = units[s - 3][2]
                    dve.wait_ge(o_hi, n + 1)
                    for rows, hi, lo, k0, k1, cols_ in out_parts(units[s - 3]):
                        ins = v.tensor_tensor(lo[rows, k0:k1, t * P:(t + 1) * P],
                                              trb[1][rows, cols_].rearrange("p (a b) -> p a b", b=P),
                                              hi[rows, k0:k1, t * P:(t + 1) * P].bitcast(F32), ALU.subtract)
                    ins.then_inc(o_lo, 1)

            def fox_masked(unit, n, W):
                kind, j, t = unit
                for g in range(2):
                    h = 2 * j + g
                    ins = v.scalar_tensor_tensor(out=s_sb[:, n % 2, g, 0:W], in0=scb[n % 2][:, g * T:g * T + W],
                                                 scalar=cq[:, t, h:h + 1], in1=cmask[:, T - W:T],
                                                 op0=ALU.add, op1=ALU.add)
                link(ins)
                return s_sb[:, n % 2, :, 0:W]

            def odd_masked(unit, n, W):
                return scb[n % 2][:].rearrange("p (g k) -> p g k", g=2)[:, :, 0:W]

            for b in range(2):
                for j in range(UPB):
                    if b * UPB + j in FOX_AFTER:
                        attention_step(0, FOX, FOX_AFTER.index(b * UPB + j), fox_masked)
                    ahead(UNIT0["e_g"] + b * UPB, j)
                blk = BLOCK0["e_g"] + b
                part = (slice(None), slice(4 * b, 4 * b + 4), slice(None))
                if b == 0:
                    dve.wait_ge(rg_h, 1)
                dve.wait_ge(acc_free[blk % 2], uses(blk) + 1)
                v.tensor_tensor(gT[part], rt[part], gT[part], ALU.mult).then_inc(rg_out, 1)
                dve.wait_ge(rg_hi, b + 1)
                v.tensor_tensor(eTl[1][part], gT[part], eTh[1][part].bitcast(F32), ALU.subtract).then_inc(rg_lo, 1)

            def residual(b, i, c, phase):
                pair = b % 2
                n = i * 2 + (4 * phase + c + 1)
                for t in range(TT):
                    if t == 0:
                        dve.wait_ge(tile0_done, n)
                    elif isinstance(i, int):
                        dve.wait_ge(w_used, BLOCK_END[b + 2 * i])
                    else:
                        dve.wait_ge(w_used, i * (BLOCK_END[b + 2 - c] - BLOCK_END[b - c]) + BLOCK_END[b])
                    at_ = xres[:, t, bass.ds(i * (2 * COLS) + c * COLS, COLS)]
                    v.scalar_tensor_tensor(out=at_, in0=at_, scalar=ALPHA, in1=acc[pair][t][:], op0=ALU.mult,
                                           op1=ALU.add).then_inc(acc_free[pair] if t == 1 else res0_done, 1)
                    if t == 0:
                        dve.wait_ge(res0_done, n)
                    else:
                        dve.wait_ge(acc_free[pair], i + uses(b) + 1)
                    ins = v.bn_stats(stats[:, t, bass.ds(i * 2 + c, 1), :].rearrange("p a b -> p (a b)"),
                                     xres[:, t, bass.ds(i * (2 * COLS) + c * COLS, COLS)])
                ins.then_inc(stats_done, 1)

            with dve.Fori(0, 2) as i:
                for b in range(2):
                    for j in range(UPB - 1):
                        ahead(UNIT0["e_out"] + b * UPB, j, i, 2 * UPB)
                    residual(BLOCK0["e_out"] + b, i, b, 0)
                    ahead(UNIT0["e_out"] + b * UPB, UPB - 1, i, 2 * UPB)

            def layer_norm(l, chunk):
                dve.wait_ge(stats_done, 4 * (l + 1))
                for t in range(TT):
                    ins = v.bn_aggr(mv[:, t, :], stats[:, t, :, :].rearrange("p a b -> p (a b)"))
                link(ins)
                v.tensor_scalar(lnv[:, 0, :], mv[:, :, 1:2].rearrange("p t a -> p (t a)"), LN_EPS, None,
                                ALU.add).then_inc(ln_var, 1)
                dve.wait_ge(gb_in, 32 * (l + 1))

                def affine(c):
                    parts = []
                    for n in (2 * c, 2 * c + 1):
                        t, c_ = chunk(n)
                        cs = slice(c_ * COLS, (c_ + 1) * COLS)
                        parts.append((t, cs))
                        ins = v.scalar_tensor_tensor(out=xres[:, t, cs], in0=xres[:, t, cs], scalar=mv[:, t, 0:1],
                                                     in1=gb[:, 0, cs], op0=ALU.subtract, op1=ALU.mult)
                    link(ins)
                    if c == 0:
                        dve.wait_ge(ln_sd, l + 1)
                        link(v.reciprocal(lnv[:, 2, :], lnv[:, 1, :]))
                    for t, cs in parts:
                        v.scalar_tensor_tensor(out=xres[:, t, cs], in0=xres[:, t, cs], scalar=lnv[:, 2, t:t + 1],
                                               in1=gb[:, 1, cs], op0=ALU.mult, op1=ALU.add).then_inc(y_ready, 1)
                return affine

            def by_columns(n):
                return n % 2, n // 2

            def by_rows(n):
                return n // 4, n % 4

            def ffn(l):
                u0, b0, t0, h0 = UNIT0[f"gu{l}"], BLOCK0[f"gu{l}"], TR0[f"gu{l}"], HI0[f"gu{l}"]

                def hidden(i):
                    for t in range(TT):
                        at_ = (slice(None), bass.ds(i * 4, 4), slice(t * P, (t + 1) * P))
                        rest_out(None, i * 2 + (h0 + t), hTh[at_], hTl[at_], (t0 + t) % 2)

                def body(i, first):
                    if first:
                        first_block(TR0[f"ln{2 * l}"], HI0[f"ln{2 * l}"], u0, layer_norm(2 * l, by_columns))
                    else:
                        for j in range(UPB):
                            ahead(u0, j, i, 2 * UPB)
                            if j == 2:
                                hidden(i - 1)
                    for j in range(UPB, 2 * UPB - 1):
                        ahead(u0, j, i, 2 * UPB)
                    dve.wait_ge(acc_free[0], i + uses(b0) + 1)
                    if not first:
                        dve.wait_ge(tr_ready, i * 2 + t0)
                    for t, done in enumerate((h0_ready, acc_free[1])):
                        if t == 0:
                            dve.wait_ge(up0_done, i + (l * FFN_BLOCKS + 1))
                        else:
                            dve.wait_ge(w_used, i * (2 * UPB) + BLOCK_END[b0 + 1])
                        v.tensor_tensor(hbuf[:, t, :], sg[:, t, :], acc[1][t][:], ALU.mult).then_inc(done, 1)
                    ahead(u0, 2 * UPB - 1, i, 2 * UPB)

                body(0, True)
                with dve.Fori(1, FFN_BLOCKS) as i:
                    body(i, False)
                hidden(FFN_BLOCKS - 1)
                d0, b0 = UNIT0[f"down{l}"], BLOCK0[f"down{l}"]

                def down(i):
                    for b in range(2):
                        for j in range(DOWN_UNITS - 1):
                            ahead(d0 + b * DOWN_UNITS, j, i, 2 * DOWN_UNITS)
                        residual(b0 + b, i, b, 1 + 2 * l)
                        ahead(d0 + b * DOWN_UNITS, DOWN_UNITS - 1, i, 2 * DOWN_UNITS)

                if l == 0:
                    with dve.Fori(0, 2) as i:
                        down(i)
                else:
                    down(0)
                    down(1)

            ffn(0)

            first_block(TR0["ln1"], HI0["ln1"], UNIT0["o_ckv"], layer_norm(1, by_columns))
            for j in range(UPB - 1):
                ahead(UNIT0["o_cq"], j)
                if j == 0:
                    dve.wait_ge(od_in, 4 * 16)
                    dve.wait_ge(consts, 3)
                    link(v.tensor_copy(pos[:], pos_i[:]))
                    for t in range(TT):
                        ins = v.tensor_scalar(trig[:, 0, t, :], invf[:], pos[:, t:t + 1], None, ALU.mult)
                    link(ins)
                    rnd = 1.5 * 2.0 ** 23
                    c1 = 6.28125
                    c2 = 2 * math.pi - c1
                    link(v.tensor_scalar(trig[:, 1], trig[:, 0], 1.0 / (2 * math.pi), rnd, ALU.mult, ALU.add))
                    link(v.tensor_scalar(trig[:, 1], trig[:, 1], -rnd, None, ALU.add))
                    link(v.scalar_tensor_tensor(out=trig[:, 2], in0=trig[:, 1], scalar=-c1, in1=trig[:, 0],
                                                op0=ALU.mult, op1=ALU.add))
                    link(v.scalar_tensor_tensor(out=trig[:, 2], in0=trig[:, 1], scalar=-c2, in1=trig[:, 2],
                                                op0=ALU.mult, op1=ALU.add))
                if j == 1:
                    link(v.tensor_scalar(trig[:, 3], trig[:, 2], math.pi / 2, None, ALU.add))
                    link(v.tensor_scalar(trig[:, 1], trig[:, 3], math.pi, -2 * math.pi, ALU.is_gt, ALU.mult))
                    link(v.tensor_tensor(trig[:, 3], trig[:, 3], trig[:, 1], ALU.add))
                    pi = 3.1415925
                    v.tensor_scalar(trig[:, 2:4], trig[:, 2:4], pi, -pi, ALU.min, ALU.max).then_inc(trig_arg, 1)
            dve.wait_ge(sq_done, 1)
            link(v.tensor_scalar(rms[:, 1, 0:2], rms[:, 0, 0:2], 1.0 / QR_RANK, RMS_EPS, ALU.mult, ALU.add))
            v.tensor_scalar(rms[:, 1, 2:4], rms[:, 0, 2:4], 1.0 / KV_RANK, RMS_EPS, ALU.mult,
                            ALU.add).then_inc(rms_var, 1)
            dve.wait_ge(rms_sd, 1)
            link(v.reciprocal(rms[:, 3, :], rms[:, 2, :]))
            b = BLOCK0["o_cq"]
            for t in range(TT):
                ins = v.tensor_scalar(cqs[:, t, :], acc[b % 2][t][:], rms[:, 3, t:t + 1], None, ALU.mult)
            ins.then_inc(acc_free[b % 2], 1)
            ahead(UNIT0["o_cq"], UPB - 1)
            for t in range(TT):
                ins = v.tensor_scalar(ckvs[:, t, :], ckvs[:, t, :], rms[:, 3, 2 + t:3 + t], None, ALU.mult)
            ins.then_inc(c_norm, 1)
            for j in range(UPB):
                m = j - 4
                if 0 <= m < 3:
                    n = TR0["rms"] + m
                    dve.wait_ge(tr_hi, HI0["rms"] + m + 1)
                    for k in range(2):
                        ins = v.scalar_tensor_tensor(out=cTl[:, 2 * m + k, :], in0=trb[n % 2][:, k * T:(k + 1) * T],
                                                     scalar=qkg[:, 2 * m + k:2 * m + k + 1],
                                                     in1=cTh[:, 2 * m + k, :].bitcast(F32), op0=ALU.mult, op1=ALU.subtract)
                    ins.then_inc(tr_free, 1)
                ahead(UNIT0["o_kv"], j)
            for j in range(4):
                ahead(UNIT0["qb_nope"], j)
            dve.wait_ge(tr_ready, TR0["kswa"] + 1)
            for h in range(SWA_KV):
                bank_ = trb[TR0["kswa"] % 2]
                v.tensor_copy(kz[0:64, h, 0, :], bank_[0:64, h * T:(h + 1) * T])
                ins = v.tensor_copy(kz[64:P, 1 - h, 1, :], bank_[64:P, h * T:(h + 1) * T])
            ins.then_inc(tr_free, 1)
            for j in range(4):
                ahead(UNIT0["qb_rope"], j)
            b = BLOCK0["qb_rope"]
            dve.wait_ge(acc_free[b % 2], uses(b) + 1)
            dve.wait_ge(trig_done, 1)
            H = ROPE // 2
            for t in range(TT):
                sin, cos = (trig[:, f, t, :].unsqueeze(1).broadcast_to([P, 10, H]) for f in (4, 5))
                x1, x2, y1, y2 = (a[:, t, :, c * H:(c + 1) * H] for a in (qr, qro) for c in range(2))
                v.tensor_tensor(y1, x1, cos, ALU.mult)
                link(v.tensor_tensor(rtmp[:], x2, sin, ALU.mult))
                link(v.tensor_tensor(y1, y1, rtmp[:], ALU.subtract))
                v.tensor_tensor(y2, x2, cos, ALU.mult)
                link(v.tensor_tensor(rtmp[:], x1, sin, ALU.mult))
                ins = v.tensor_tensor(y2, y2, rtmp[:], ALU.add)
                if t == 0:
                    link(ins)
                    ahead(UNIT0["kvb"], 0)
            ins.then_inc(rope_out, 1)
            for j in range(1, 4):
                ahead(UNIT0["kvb"], j)
            for b in range(2):
                for j in range(UPB):
                    if (b, j) == (0, 0):
                        for m in range(3):
                            n = TR0["rope"] + m
                            dve.wait_ge(tr_ready, n + 1)
                            if m < 2:
                                ins = v.tensor_copy(qrT[:, 2 * m:2 * m + 2, :].rearrange("p a b -> p (a b)"), trb[n % 2][:])
                            else:
                                for g in range(2):
                                    rows = slice(g * 64, (g + 1) * 64)
                                    ins = v.tensor_copy(krz[rows, g, :], trb[n % 2][rows, 0:T])
                            ins.then_inc(tr_free, 1)
                    else:
                        attention_step(len(FOX), ODD, b * UPB + j - 1, odd_masked)
                    ahead(UNIT0["o_q"] + b * UPB, j)
            b0 = BLOCK0["o_out"]
            for j in range(4 * UPB):
                if 2 * UPB - 1 + j < ODD_STEPS:
                    attention_step(len(FOX), ODD, 2 * UPB - 1 + j, odd_masked)
                if j + 1 in (14, 16, 24, 32):
                    c = (14, 16, 24, 32).index(j + 1)
                    residual(b0 + c % 2, c // 2, c % 2, 2)
                ahead(UNIT0["o_out"], j)
            ffn(1)
            affine = layer_norm(3, by_rows)
            for c in range(4):
                affine(c)


_INS = ['x', 'positions', 'ev_w_in', 'ev_forget_bias', 'ev_conv_w', 'ev_conv_b', 'ev_rgate_w', 'ev_rgate_b',
        'ev_igate_w', 'ev_igate_b', 'ev_lru_lambda', 'ev_w_out', 'od_w_in', 'od_sinks', 'od_q_norm', 'od_w_qb',
        'od_kv_norm', 'od_w_kvb', 'od_w_out', 'ln_mix_g', 'ln_mix_b', 'ffn_w_gate', 'ffn_w_up', 'ffn_w_down',
        'ln_ffn_g', 'ln_ffn_b']
_OUTS = [((1, 256, 2048), 'float32')]


def kernel(**inputs):
    import numpy as _np
    import concourse.bacc as _bacc
    from concourse import mybir as _mybir
    from concourse.bass_utils import run_bass_kernel_spmd as _run

    nc = _bacc.Bacc("TRN2", target_bir_lowering=False, num_devices=1)
    arrays, args = {}, []
    for name in _INS:
        a = _np.ascontiguousarray(inputs[name])
        arrays[f"in_{name}_dram"] = a
        args.append(nc.dram_tensor(f"in_{name}_dram", a.shape, _mybir.dt.from_np(a.dtype), kind="ExternalInput").ap())
    for i, (shape, dtype) in enumerate(_OUTS):
        dt = _mybir.dt.from_np(_np.dtype(dtype))
        args.append(nc.dram_tensor(f"out_{i}_dram", shape, dt, kind="ExternalOutput").ap())
    hybrid_trunk_kernel(nc, *args)
    r = _run(nc, [arrays], core_ids=[0])
    got = tuple(r.results[0][f"out_{i}_dram"] for i in range(len(_OUTS)))
    return got[0]
```

```python
from contextlib import ExitStack
import math

import concourse.bass as bass
from concourse import mybir

ALU = mybir.AluOpType
ACT = mybir.ActivationFunctionType
AX = mybir.AxisListType
F32 = mybir.dt.float32
F32R = mybir.dt.float32r
I32 = mybir.dt.int32

P = 128
T = 256
TT = T // P
D = 2048
KD = D // P
COLS = 512
UK = 2
SLOTS = 4
UNIT = UK * COLS
UPB = KD // UK

FOX_HEADS, FOX_W = 8, 1024
LRU_W, LRU_B, CONV = 1024, 8, 4
LRU_C = 8.0
SWA_Q, SWA_KV, SWA_DH = 16, 2, 64
MLA_H, QR_RANK, KV_RANK, NOPE, ROPE, MLA_V = 8, 512, 256, 128, 64, 128
THETA = 10000.0
FFN = 5632
KF = FFN // P
ALPHA = 4.0 ** 0.25
LN_EPS, RMS_EPS = 1e-5, 1e-6
NEG = -1.0e30

FFN_BLOCKS = FFN // COLS
DOWN_UNITS = KF // UK
STREAM = [
    ("e_u", 2 * UPB, 2), ("e_q", 2 * UPB, 2), ("e_k", 2 * UPB, 2), ("e_v", 2 * UPB, 2), ("e_g", 2 * UPB, 2),
    ("e_out", 4 * UPB, 4), ("gu0", 2 * UPB * FFN_BLOCKS, 2 * FFN_BLOCKS), ("down0", 4 * DOWN_UNITS, 4),
    ("o_ckv", UPB, 1), ("o_cq", UPB, 1), ("o_kv", UPB, 1), ("qb_nope", 4, 2), ("qb_rope", 4, 1), ("kvb", 4, 4),
    ("o_q", 2 * UPB, 2),
    ("o_out", 4 * UPB, 4), ("gu1", 2 * UPB * FFN_BLOCKS, 2 * FFN_BLOCKS), ("down1", 4 * DOWN_UNITS, 4),
]
SPAN = []
UNIT0, BLOCK0, BLOCK_END = {}, {}, []
_u = _b = 0
for _name, _nu, _nb in STREAM:
    UNIT0[_name], BLOCK0[_name] = _u, _b
    _ends = {"qb_nope": [4, 4], "o_out": [14, 16, 24, 32]}.get(_name, [(_k + 1) * _nu // _nb for _k in range(_nb)])
    BLOCK_END += [_u + _e for _e in _ends]
    SPAN += [{"o_ckv": UK * (KV_RANK + ROPE), "o_kv": UK * 2 * SWA_KV * SWA_DH, "qb_rope": MLA_H * ROPE}.get(
        _name, UNIT)] * _nu
    _u, _b = _u + _nu, _b + _nb
UNITS = _u

TR_STEPS = [("x", 8), ("ln0", 8), ("gu0", 2 * FFN_BLOCKS), ("ln1", 8), ("rms", 3), ("kswa", 1), ("rope", 3),
            ("ln2", 8), ("gu1", 2 * FFN_BLOCKS)]
TR0, HI0 = {}, {}
_n = _h = 0
for _name, _c in TR_STEPS:
    TR0[_name], HI0[_name] = _n, _h
    _n += _c
    _h += 0 if _name in ("kswa", "rope") else _c

E_OUT_K = [8, 10, 0, 2, 4, 6, 12, 14]
O_OUT_HEAD = [(b, k) for ks in ((8, 10, 12, 14), (0, 2), (4, 6)) for b in range(2) for k in ks]

FOX = [("fox", j, t) for j in range(4) for t in range(2)]
ODD = [("mla", j, t) for j in range(4) for t in range(2)] + [("swa", j, t) for j in range(8) for t in range(2)]
FOX_STEPS, ODD_STEPS = len(FOX) + 3, len(ODD) + 3
FOX_AFTER = [j for j in range(16) if j % 4][:FOX_STEPS]

AHEAD_OF_CHUNK = [(), (0,), (1, 2), (3, 4, 5, 6, 7)]

LOG1P_TERMS = 9


def hybrid_trunk_kernel(
    nc: bass.Bass, x, positions, ev_w_in, ev_forget_bias, ev_conv_w, ev_conv_b, ev_rgate_w, ev_rgate_b,
    ev_igate_w, ev_igate_b, ev_lru_lambda, ev_w_out, od_w_in, od_sinks, od_q_norm, od_w_qb, od_kv_norm,
    od_w_kvb, od_w_out, ln_mix_g, ln_mix_b, ffn_w_gate, ffn_w_up, ffn_w_down, ln_ffn_g, ln_ffn_b, out,
):
    ctx = ExitStack()
    with ctx:
        base = (nc.sbuf_base + 63) // 64 * 64
        top = [base]

        def place(name, shape, dt, at=None):
            size = 4
            for s in shape[1:]:
                size *= s
            off = top[0] if at is None else at
            if at is None:
                top[0] = off + (size + 31) // 32 * 32
            return nc.alloc_sbuf_tensor_at(name, shape, dt, offset=off)

        xTh = place("xTh", [P, KD, T], F32R)
        xTl = place("xTl", [P, KD, T], F32R)
        xres = place("xres", [P, TT, D], F32)
        raw = place("raw", [P, SLOTS, UNIT], F32)
        whi = place("whi", [P, SLOTS, UNIT], F32R)
        wlo = place("wlo", [P, SLOTS, UNIT], F32R)
        ident = place("ident", [P, P], F32)
        identr = place("identr", [P, P], F32R)
        stats = place("stats", [P, TT, 4, 6], F32)
        mv = place("mv", [P, TT, 2], F32)
        lnv = place("lnv", [P, 4, TT], F32)
        g0 = top[0]
        gb = place("gb", [P, 2, D], F32)
        sg = place("sg", [P, TT, COLS], F32, g0)
        hbuf = place("hbuf", [P, TT, COLS], F32, g0 + 4 * TT * COLS)
        nlf = place("nlf", [P, TT, FOX_HEADS, P], F32, g0)
        rgd = place("rgd", [P, LRU_B, T], F32, g0 + 4 * TT * FOX_HEADS * P)
        m0 = top[0]
        hTh = place("hTh", [P, KF, T], F32R)
        hTl = place("hTl", [P, KF, T], F32R)
        end = top[0]
        assert end <= nc.sbuf_usable_end, (end, nc.sbuf_usable_end)

        top[0] = m0
        s_sb = place("s_sb", [P, 2, 2, T], F32)
        p_sb = place("p_sb", [P, 2, 2, T], F32)
        pT = place("pT", [P, 2, 4, P], F32)
        nm = place("nm", [P, 2, 2], F32)
        mx = place("mx", [P, 2, 2], F32)
        lsum = place("lsum", [P, 2, 2], F32)
        rl = place("rl", [P, 2, 2], F32)
        es = place("es", [P, 2, 2], F32)
        mix0 = top[0]
        qT = place("qT", [P, 8, T], F32)
        kT = place("kT", [P, 8, T], F32)
        vt = place("vt", [P, TT, FOX_W], F32)
        uT0 = top[0]
        uT = place("uT", [P, LRU_B, T + CONV - 1], F32)
        gT = place("gT", [P, LRU_B, T], F32)
        uc0 = top[0]
        uc = place("uc", [P, LRU_B, T], F32)
        rt = place("rt", [P, LRU_B, T], F32)
        it0 = top[0]
        it = place("it", [P, LRU_B, T], F32)
        rw0 = top[0]
        rw = place("rw", [P, LRU_B, P], F32)
        iw = place("iw", [P, LRU_B, P], F32)
        eTh = [place("eTh0", [P, 8, T], F32R, uc0), place("eTh1", [P, 8, T], F32R, uT0)]
        eTl = [place("eTl0", [P, 8, T], F32R, it0), place("eTl1", [P, 8, T], F32R, rw0)]
        cmask = place("cmask", [P, T], F32)
        tri = place("tri", [P, T], F32)
        wf = place("wf", [P, KD, FOX_HEADS], F32)
        wfh = place("wfh", [P, KD, P], F32R, g0)
        wfl = place("wfl", [P, KD, P], F32R, g0 + 4 * KD * P)
        fT = place("fT", [P, T], F32, uT0 + 4 * LRU_B * (T + CONV - 1))
        fb = place("fb", [P, FOX_HEADS], F32)
        cw = place("cw", [P, CONV, LRU_B], F32)
        cols = place("cols", [P, 4, LRU_B], F32)
        clam = place("clam", [P, 2, LRU_B], F32)
        lz = place("lz", [P, 6, LRU_B], F32)
        fz = place("fz", [P, 7, TT * FOX_HEADS], F32)
        cq = place("cq", [P, TT, FOX_HEADS], F32)
        assert top[0] <= nc.sbuf_usable_end, (top[0], nc.sbuf_usable_end)
        top[0] = mix0 + 4 * 8 * T
        qnT = place("qnT", [P, 8, T], F32)
        knT = place("knT", [P, 8, T], F32)
        qr0 = top[0]
        qr = place("qr", [P, TT, 10, ROPE], F32)
        qro = place("qro", [P, TT, 10, ROPE], F32)
        rtmp = place("rtmp", [P, 10, ROPE // 2], F32)
        cT0 = top[0]
        cTh = place("cTh", [P, 6, T], F32R)
        cTl = place("cTl", [P, 6, T], F32R)
        cqs = place("cqs", [P, TT, QR_RANK], F32)
        ckvs = place("ckvs", [P, TT, KV_RANK], F32)
        mTh = place("mTh", [P, 8, T], F32R, cT0)
        mTl = place("mTl", [P, 8, T], F32R, cT0 + 4 * 8 * T)
        sTh = place("sTh", [P, 4, T], F32R, qr0)
        sTl = place("sTl", [P, 4, T], F32R, qr0 + 4 * 4 * T)
        assert 2 * 4 * 4 * T <= cT0 - qr0 and 2 * 4 * 8 * T <= top[0] - cT0
        qrT = place("qrT", [P, 4, T], F32)
        krz = place("krz", [P, 2, T], F32)
        kvs = place("kvs", [P, TT, 2 * P], F32)
        kz = place("kz", [P, SWA_KV, 2, T], F32)
        vd = place("vd", [P, TT, SWA_KV, P], F32)
        vm = place("vm", [P, TT, MLA_H, MLA_V], F32)
        bmask = place("bmask", [P, 2, T], F32, m0)
        wmask = place("wmask", [P, 2, T], F32, m0 + 4 * 2 * T)
        bmr = place("bmr", [P, 2, T], F32R)
        wmr = place("wmr", [P, 2, T], F32R)
        pos_i = place("pos_i", [P, TT], I32)
        pos = place("pos", [P, TT], F32)
        invf = place("invf", [P, ROPE // 2], F32)
        trig = place("trig", [P, 6, TT, ROPE // 2], F32)
        sinks = place("sinks", [P, SWA_Q], F32)
        qkg = place("qkg", [P, 6], F32)
        rms = place("rms", [P, 4, 2 * TT], F32)
        assert top[0] <= nc.sbuf_usable_end, (top[0], nc.sbuf_usable_end)

        def bank(name):
            return ctx.enter_context(nc.psum_tensor(name, [P, COLS], F32))

        acc = [[bank(f"acc{p}{t}") for t in range(2)] for p in range(2)]
        misc = [bank(f"misc{n}") for n in range(4)]
        scb, trb = misc[0:2], misc[2:4]

        def sem(name):
            return ctx.enter_context(nc.semaphore(name))

        w_in = [sem(f"w_in{s}") for s in range(SLOTS)]
        w_hi = sem("w_hi")
        w_lo = sem("w_lo")
        w_used = sem("w_used")
        acc_free = [sem(f"acc_free{p}") for p in range(2)]
        tr_ready = sem("tr_ready")
        tr_hi = sem("tr_hi")
        tr_free = sem("tr_free")
        x0_in = sem("x0_in")
        x_in = [sem(f"x_in{c}") for c in range(4)]
        y_ready = sem("y_ready")
        tile0_done = sem("tile0_done")
        res0_done = sem("res0_done")
        up0_done = sem("up0_done")
        h0_ready = sem("h0_ready")
        stats_done = [sem(f"stats_done{t}") for t in range(TT)]
        ln_var = sem("ln_var")
        ln_sd = sem("ln_sd")
        gb_in = sem("gb_in")
        out_done = sem("out_done")
        dv = sem("dv")
        av = sem("av")
        pv = sem("pv")
        consts = sem("consts")
        ev_in = sem("ev_in")
        od_in = sem("od_in")
        wf_in = sem("wf_in")
        wf_hi = sem("wf_hi")
        wf_split = sem("wf_split")
        f_ready = sem("f_ready")
        f_copied = sem("f_copied")
        f_neg = sem("f_neg")
        f_exp = sem("f_exp")
        f_log = sem("f_log")
        f_rep = sem("f_rep")
        c_ready = sem("c_ready")
        c_done = sem("c_done")
        lam_x = sem("lam_x")
        lam_e = sem("lam_e")
        lam_done = sem("lam_done")
        conv_done = sem("conv_done")
        gates_ready = sem("gates_ready")
        gates_free = sem("gates_free")
        rg_t = sem("rg_t")
        rg_at = sem("rg_at")
        rg_var = sem("rg_var")
        rg_sq = sem("rg_sq")
        rg_h = sem("rg_h")
        rg_out = sem("rg_out")
        rg_hi = sem("rg_hi")
        rg_lo = sem("rg_lo")
        sc_ready = sem("sc_ready")
        nm_ready = sem("nm_ready")
        ex_ready = sem("ex_ready")
        pr_ready = sem("pr_ready")
        pt_ready = sem("pt_ready")
        pt_copied = sem("pt_copied")
        o_ready = sem("o_ready")
        o_hi = sem("o_hi")
        o_lo = sem("o_lo")
        masks_r = sem("masks_r")
        sq_done = sem("sq_done")
        rms_var = sem("rms_var")
        rms_sd = sem("rms_sd")
        c_norm = sem("c_norm")
        rope_out = sem("rope_out")
        trig_arg = sem("trig_arg")
        trig_done = sem("trig_done")

        block = ctx.enter_context(nc.Block())

        def at(unit, i=0, per=0):
            return unit % SLOTS, i * (per // SLOTS) + unit // SLOTS

        def number(u):
            return u[1] * SLOTS + u[0]

        def span_of(unit, i=0, per=0):
            return SPAN[i * per + unit] if isinstance(i, int) else UNIT

        def uses(b):
            return b // 2

        SCALES = {"fox": P ** -0.5, "swa": SWA_DH ** -0.5, "mla": (NOPE + ROPE) ** -0.5}

        def out_parts(unit):
            kind, j, t = unit
            if kind == "fox":
                return [(slice(0, P), eTh[0], eTl[0], 2 * j, 2 * j + 2, slice(0, 2 * P))]
            if kind == "mla":
                return [(slice(0, P), mTh, mTl, 2 * j, 2 * j + 2, slice(0, 2 * P))]
            hi, lo, k = (sTh, sTl, j) if j < 4 else (xTh, xTl, j)
            return [(slice(g * 64, g * 64 + 64), hi, lo, k, k + 1, slice(g * P, (g + 1) * P)) for g in range(2)]

        def wmat(w, l):
            return w[l].rearrange("(k p) n -> p k n", p=P)

        @block.sync
        def _(sp):
            def load(u, src, width=COLS, kts=UK):
                slot, rounds = u
                if not (isinstance(rounds, int) and rounds == 0):
                    sp.wait_ge(w_lo, number(u) - SLOTS + 1)
                dst = raw[:, slot, 0:kts * width].rearrange("p (k n) -> p k n", k=kts)
                sp.dma_start(dst, src).then_inc(w_in[slot], 16)

            def load_x(c):
                cs = slice(c * COLS, (c + 1) * COLS)
                sp.dma_start(xres[:, :, cs], x[0].rearrange("(t p) n -> p t n", p=P)[:, :, cs]).then_inc(x_in[c], 16)

            for t, arrived in enumerate((x0_in, x_in[0])):
                sp.dma_start(xres[:, t, 0:COLS], x[0, t * P:(t + 1) * P, 0:COLS]).then_inc(arrived, 16)

            ev_in_w = wmat(ev_w_in, 0)
            f0 = 3 * FOX_W
            for name, c0 in (("e_u", f0 + FOX_HEADS), ("e_q", 0), ("e_k", FOX_W), ("e_v", 2 * FOX_W),
                             ("e_g", f0 + FOX_HEADS + LRU_W)):
                for b in range(2):
                    for j in range(UPB):
                        load(at(UNIT0[name] + b * UPB + j),
                             ev_in_w[:, j * UK:(j + 1) * UK, c0 + b * COLS:c0 + (b + 1) * COLS])
                        if name == "e_u" and b == 0 and j < 3:
                            load_x(j + 1)

            def ffn(l):
                gate, up, down = wmat(ffn_w_gate, l), wmat(ffn_w_up, l), wmat(ffn_w_down, l)
                with sp.Fori(0, FFN_BLOCKS) as i:
                    for b, w in enumerate((gate, up)):
                        for j in range(UPB):
                            load(at(UNIT0[f"gu{l}"] + b * UPB + j, i, 2 * UPB),
                                 w[:, j * UK:(j + 1) * UK, bass.ds(i * COLS, COLS)])
                with sp.Fori(0, 2) as i:
                    for b in range(2):
                        for j in range(DOWN_UNITS):
                            load(at(UNIT0[f"down{l}"] + b * DOWN_UNITS + j, i, 2 * DOWN_UNITS),
                                 down[:, j * UK:(j + 1) * UK, bass.ds(i * (2 * COLS) + b * COLS, COLS)])

            w = wmat(ev_w_out, 0)
            for b in range(4):
                for j, k in enumerate(E_OUT_K):
                    load(at(UNIT0["e_out"] + b * UPB + j), w[:, k:k + UK, b * COLS:(b + 1) * COLS])
            ffn(0)
            w = wmat(od_w_in, 0)
            kv0 = SWA_Q * SWA_DH
            cq0 = kv0 + 2 * SWA_KV * SWA_DH
            for name, c0, width in (("o_ckv", cq0 + QR_RANK, KV_RANK + ROPE), ("o_cq", cq0, QR_RANK),
                                    ("o_kv", kv0, cq0 - kv0)):
                for j in range(UPB):
                    load(at(UNIT0[name] + j), w[:, j * UK:(j + 1) * UK, c0:c0 + width], width)
            qb = wmat(od_w_qb, 0)
            hw = NOPE + ROPE

            def load_heads(u, k, off, width):
                slot = u[0]
                sp.wait_ge(w_lo, number(u) - SLOTS + 1)
                src = qb[:, k, :].rearrange("p (h n) -> p h n", n=hw)[:, :, off:off + width]
                sp.dma_start(raw[:, slot, 0:MLA_H * width].rearrange("p (h n) -> p h n", n=width),
                             src).then_inc(w_in[slot], 16)

            for k in range(QR_RANK // P):
                load_heads(at(UNIT0["qb_nope"] + k), k, 0, NOPE)
            for k in range(QR_RANK // P):
                load_heads(at(UNIT0["qb_rope"] + k), k, NOPE, ROPE)
            kvb = wmat(od_w_kvb, 0)
            for b in range(4):
                load(at(UNIT0["kvb"] + b), kvb[:, :, b * COLS:(b + 1) * COLS])
            for b in range(2):
                for j in range(UPB):
                    load(at(UNIT0["o_q"] + b * UPB + j), w[:, j * UK:(j + 1) * UK, b * COLS:(b + 1) * COLS])
            w = wmat(od_w_out, 0)
            for j, (b, k) in enumerate(O_OUT_HEAD + [(b, j * UK) for b in range(2, 4) for j in range(UPB)]):
                load(at(UNIT0["o_out"] + j), w[:, k:k + UK, b * COLS:(b + 1) * COLS])
            ffn(1)
            for n in range(8):
                t, c = n // 4, n % 4
                sp.wait_ge(y_ready, 3 * 8 + n + 1)
                sp.dma_start(out[0, t * P:(t + 1) * P, c * COLS:(c + 1) * COLS],
                             xres[:, t, c * COLS:(c + 1) * COLS]).then_inc(out_done, 16)
            sp.wait_ge(out_done, 8 * 16)

        @block.gpsimd
        def _(pool):
            chain = [0]

            def link(ins):
                chain[0] += 1
                ins.then_inc(pv, 1)
                pool.wait_ge(pv, chain[0])

            link(pool.memset(ident[:], 0.0))
            link(pool.affine_select(out=ident[:], in_=ident[:], compare_op=ALU.not_equal, fill=1.0, base=0,
                                    pattern=[[-1, P]], channel_multiplier=1))
            pool.sem_inc(consts, 1)
            vec = lambda w: w[0].rearrange("(n p) -> p n", p=P)
            f0 = 3 * FOX_W
            pool.dma_start(wf[:], wmat(ev_w_in, 0)[:, :, f0:f0 + FOX_HEADS]).then_inc(wf_in, 16)
            for dst, src in (
                (fb[:], ev_forget_bias[0:1, :].broadcast_to([P, FOX_HEADS])),
                (cols[:, 3, :], vec(ev_lru_lambda)),
                (cols[:, 0, :], vec(ev_conv_b)),
                (cols[:, 1, :], vec(ev_rgate_b)),
                (cols[:, 2, :], vec(ev_igate_b)),
                (cw[:, 0, :], ev_conv_w[0, 0].rearrange("(n p) -> p n", p=P)),
                (cw[:, 1, :], ev_conv_w[0, 1].rearrange("(n p) -> p n", p=P)),
                (cw[:, 2, :], ev_conv_w[0, 2].rearrange("(n p) -> p n", p=P)),
                (cw[:, 3, :], ev_conv_w[0, 3].rearrange("(n p) -> p n", p=P)),
                (rw[:], ev_rgate_w[0].rearrange("n c d -> c n d")),
                (iw[:], ev_igate_w[0].rearrange("n c d -> c n d")),
            ):
                pool.dma_start(dst, src, allow_slow_non_contiguous=True).then_inc(ev_in, 16)
            link(pool.memset(wfh[:].bitcast(F32), 0.0))
            link(pool.memset(wfl[:].bitcast(F32), 0.0))
            link(pool.memset(uT[:, :, 0:CONV - 1], 0.0))
            link(pool.memset(cmask[:], 0.0))
            link(pool.memset(tri[:], 1.0))
            link(pool.affine_select(out=cmask[:, P:T], in_=cmask[:, P:T], compare_op=ALU.is_ge, fill=NEG, base=0,
                                    pattern=[[-1, P]], channel_multiplier=1))
            link(pool.affine_select(out=tri[:, 0:P], in_=tri[:, 0:P], compare_op=ALU.is_ge, fill=0.0, base=0,
                                    pattern=[[1, P]], channel_multiplier=-1))
            pool.sem_inc(consts, 1)

            def gains(g, b, l):
                pool.dma_start(gb[:, 0, :], g[l:l + 1, :].broadcast_to([P, D])).then_inc(gb_in, 16)
                pool.dma_start(gb[:, 1, :], b[l:l + 1, :].broadcast_to([P, D])).then_inc(gb_in, 16)

            pool.wait_ge(sc_ready, len(FOX))
            pool.wait_ge(rg_h, 1)
            gains(ln_mix_g, ln_mix_b, 0)
            pool.wait_ge(tr_ready, TR0["gu0"] + 2 * FFN_BLOCKS)
            gains(ln_ffn_g, ln_ffn_b, 0)
            pool.wait_ge(w_used, BLOCK_END[BLOCK0["down0"] + 3])
            link(pool.memset(bmask[:], 0.0))
            link(pool.memset(wmask[:], 0.0))
            for g in range(2):
                link(pool.memset(bmask[0:64, g, P + 64:T], NEG))
                link(pool.memset(wmask[0:64, g, 0:64], NEG))
                link(pool.memset(wmask[0:64, g, P + 64:T], NEG))
                link(pool.memset(wmask[64:P, g, 0:P], NEG))
            link(pool.memset(kz[:], 0.0))
            link(pool.memset(krz[:], 0.0))
            for n in range(ROPE // 2):
                link(pool.memset(invf[:, n:n + 1], float(THETA ** (-2.0 * n / ROPE))))
            pool.sem_inc(consts, 1)
            for dst, src in (
                (pos_i[:], positions.rearrange("b (t p) -> p (b t)", p=P)),
                (sinks[:], od_sinks[0:1, :].broadcast_to([P, SWA_Q])),
                (qkg[:, 0:4], vec(od_q_norm)),
                (qkg[:, 4:6], vec(od_kv_norm)),
            ):
                pool.dma_start(dst, src, allow_slow_non_contiguous=True).then_inc(od_in, 16)
            pool.wait_ge(y_ready, 16)
            gains(ln_mix_g, ln_mix_b, 1)
            pool.wait_ge(tr_ready, TR0["gu1"] + 2 * FFN_BLOCKS)
            gains(ln_ffn_g, ln_ffn_b, 1)

        @block.tensor
        def _(pe):
            mm = nc.tensor.matmul

            def unit_ready(u):
                pe.wait_ge(w_lo, number(u) + 1)

            def rows_unit(u, pair, k0, first, last, src=(xTh, xTl), width=COLS, kts=UK, tiles=(0, 1), first_tile=None):
                unit_ready(u)
                s = u[0]
                for t in tiles:
                    for kk in range(kts):
                        wh, wl = (w[:, s, kk * width:(kk + 1) * width] for w in (whi, wlo))
                        xh, xl = (a[:, k0 + kk, t * P:(t + 1) * P] for a in src)
                        o = acc[pair][t][:, 0:width]
                        mm(o, xh, wh, start=first and kk == 0, stop=False)
                        mm(o, xh, wl, start=False, stop=False)
                        ins = mm(o, xl, wh, start=False, stop=last and kk == kts - 1)
                    if t == 0 and last and first_tile:
                        ins.then_inc(first_tile, 1)
                if tiles[-1] == 1:
                    ins.then_inc(w_used, 1)

            def cols_unit(u, pair, k0, first, last, src=(xTh, xTl)):
                unit_ready(u)
                s = u[0]
                for kk in range(UK):
                    for c in range(4):
                        wh, wl = (w[:, s, kk * COLS + c * P:kk * COLS + (c + 1) * P] for w in (whi, wlo))
                        xh, xl = (a[:, k0 + kk, :] for a in src)
                        o = acc[pair][c // 2][:, (c % 2) * T:(c % 2 + 1) * T]
                        mm(o, wh, xh, start=first and kk == 0 and c % 2 == 0, stop=False, skip_group_check=True)
                        mm(o, wl, xh, start=False, stop=False, skip_group_check=True)
                        ins = mm(o, wh, xl, start=False, stop=last and kk == UK - 1, skip_group_check=True)
                ins.then_inc(w_used, 1)

            def open_block(b, i=0, per=0):
                before = uses(b) + i * (per // 2)
                if not (isinstance(before, int) and before == 0):
                    pe.wait_ge(acc_free[b % 2], before)

            def block_of(unit_fn, u0, b, i=0, per_u=0, per_b=0, n_units=UPB, after=None, before=None, src=None,
                         head=None, tail=0, **kw):
                open_block(b, i, per_b)

                def one(j, **tiles):
                    s_, k0 = src(j) if src else ((xTh, xTl), j * UK)
                    unit_fn(at(u0 + j, i, per_u), b % 2, k0, j == 0, j == n_units - 1, src=s_, **kw, **tiles)

                if head:
                    turn, n0 = head
                    turn(0, 0)
                    pe.wait_ge(tr_free, n0 + 1)
                    one(0, tiles=(0,))
                    one(1, tiles=(0,))
                    turn(0, 1)
                    pe.wait_ge(tr_free, n0 + 2)
                    one(0, tiles=(1,))
                    turn(1, 0)
                    turn(1, 1)
                    one(1, tiles=(1,))
                for j in range(2 if head else 0, n_units - tail):
                    if before:
                        before(j)
                    one(j)
                    if after:
                        after(j)
                for t in range(TT if tail else 0):
                    for j in range(n_units - tail, n_units):
                        if before and t == 0:
                            before(j)
                        one(j, tiles=(t,))

            def transposes(n, parts, parity=None):
                if not (isinstance(n, int) and n < 2):
                    pe.wait_ge(tr_free, n - 1)
                dst = trb[n % 2 if parity is None else parity]
                for q, src in enumerate(parts):
                    ins = nc.tensor.transpose(dst[:, q * P:(q + 1) * P], src, ident[:])
                ins.then_inc(tr_ready, 1)

            def turned(n0, arrived, by_tile):
                def turn(c, t):
                    arrived(2 * c + t)
                    transposes(n0 + 2 * c + t, [xres[:, t, (4 * c + q) * P:(4 * c + q + 1) * P] for q in range(4)])

                def before(j):
                    if j == 0:
                        turn(0, 0)
                        turn(0, 1)
                    if j % 2 == 0:
                        pe.wait_ge(tr_free, n0 + j + 2)
                    elif j < 6:
                        turn((j + 1) // 2, 0)
                        turn((j + 1) // 2, 1)
                return dict(before=before, head=(turn, n0) if by_tile else None)

            def normalised(y0):
                return lambda n: pe.wait_ge(y_ready, y0 + n + 1)

            def attention_step(n0, units, s, scores, values):
                N = len(units)
                if s < N:
                    n = n0 + s
                    if s >= 2:
                        pe.wait_ge(ex_ready, n - 1)
                    scores(units[s], scb[n % 2], (units[s][2] + 1) * P)
                if 2 <= s < N + 2:
                    n = n0 + s - 2
                    kind, j, t = units[s - 2]
                    pe.wait_ge(pr_ready, n + 1)
                    if s >= 3:
                        pe.wait_ge(pt_copied, n)
                    for g in range(2):
                        for k in range(t + 1):
                            q = g * (t + 1) + k
                            ins = nc.tensor.transpose(trb[0][:, q * P:(q + 1) * P],
                                                      p_sb[:, n % 2, g, k * P:(k + 1) * P], ident[:])
                    ins.then_inc(pt_ready, 1)
                if 3 <= s < N + 3:
                    n = n0 + s - 3
                    kind, j, t = units[s - 3]
                    pe.wait_ge(pt_copied, n + 1)
                    if s >= 4:
                        pe.wait_ge(o_lo, n)
                    for g in range(2):
                        for k in range(t + 1):
                            ins = mm(trb[1][:, g * P:(g + 1) * P], values(units[s - 3], g, k),
                                     pT[:, n % 2, g * (t + 1) + k, :], start=k == 0, stop=k == t)
                    ins.then_inc(o_ready, 1)

            pe.wait_ge(consts, 1)

            def x_arrived(n):
                pe.wait_ge(x0_in if n == 0 else x_in[n // 2], 16)

            for b in range(2):
                block_of(cols_unit, UNIT0["e_u"] + b * UPB, BLOCK0["e_u"] + b,
                         **(turned(TR0["x"], x_arrived, False) if b == 0 else {}))
            pe.wait_ge(wf_split, 1)
            for k in range(KD):
                mm(scb[0][:, 0:T], wfh[:, k, :], xTh[:, k, :], start=k == 0, stop=False)
                mm(scb[0][:, 0:T], wfl[:, k, :], xTh[:, k, :], start=False, stop=False)
                ins = mm(scb[0][:, 0:T], wfh[:, k, :], xTl[:, k, :], start=False, stop=k == KD - 1)
            ins.then_inc(f_ready, 1)

            def f_turned(j):
                if j == 0:
                    pe.wait_ge(f_copied, 1)
                    for t in range(TT):
                        ins = nc.tensor.transpose(scb[1][:, t * P:(t + 1) * P], fT[:, t * P:(t + 1) * P], ident[:])
                    ins.then_inc(f_ready, 1)

            def cumulative(j):
                if j == 2:
                    pe.wait_ge(consts, 2)
                    pe.wait_ge(f_log, 1)
                    lf = fz[:, 6, :].rearrange("p (t h) -> p t h", t=TT)
                    mm(scb[1][:, 0:8], tri[:, 0:P], lf[:, 0, :], start=True, stop=True)
                    mm(scb[1][:, 8:16], tri[:, P:T], lf[:, 0, :], start=True, stop=False)
                    mm(scb[1][:, 8:16], tri[:, 0:P], lf[:, 1, :], start=False, stop=True).then_inc(c_ready, 1)

            for b, after in enumerate((f_turned, cumulative)):
                block_of(cols_unit, UNIT0["e_q"] + b * UPB, BLOCK0["e_q"] + b, after=after)

            def gates(n):
                pe.wait_ge(conv_done, n + 1)
                if n == 0:
                    pe.wait_ge(c_done, 1)
                if n >= 2:
                    pe.wait_ge(gates_free, n - 1)
                mm(scb[n % 2][:, 0:T], rw[:, n, :], uc[:, n, :], start=True, stop=True)
                mm(scb[n % 2][:, T:2 * T], iw[:, n, :], uc[:, n, :], start=True, stop=True).then_inc(gates_ready, 1)

            block_of(cols_unit, UNIT0["e_k"], BLOCK0["e_k"], after=gates)
            block_of(cols_unit, UNIT0["e_k"] + UPB, BLOCK0["e_k"] + 1)
            for b in range(2):
                block_of(rows_unit, UNIT0["e_v"] + b * UPB, BLOCK0["e_v"] + b)

            def fox_scores(unit, bank_, W):
                kind, j, t = unit
                for g in range(2):
                    h = 2 * j + g
                    o = bank_[:, g * T:g * T + W]
                    mm(o, qT[:, h, t * P:(t + 1) * P], kT[:, h, 0:W], start=True, stop=False)
                    if t == 1:
                        mm(bank_[:, g * T + P:g * T + T], nlf[:, 1, h, :], tri[:, 0:P], start=False, stop=False,
                           skip_group_check=True)
                    ins = mm(o, nlf[:, 0, h, :], tri[:, 0:W], start=False, stop=True)
                ins.then_inc(sc_ready, 1)

            def fox_values(unit, g, k):
                h = 2 * unit[1] + g
                return vt[:, k, h * P:(h + 1) * P]

            def fox_after(b):
                def after(j):
                    if b * UPB + j in FOX_AFTER:
                        s = FOX_AFTER.index(b * UPB + j)
                        if s == 0:
                            pe.wait_ge(f_rep, 1)
                            pe.wait_ge(gates_free, 8)
                            pe.wait_ge(acc_free[BLOCK0["e_v"] % 2], uses(BLOCK0["e_v"]) + 1)
                            pe.wait_ge(acc_free[1 - BLOCK0["e_v"] % 2], uses(BLOCK0["e_v"]) + 1)
                        attention_step(0, FOX, s, fox_scores, fox_values)
                return after

            for b in range(2):
                block_of(cols_unit, UNIT0["e_g"] + b * UPB, BLOCK0["e_g"] + b, after=fox_after(b))

            def e_out_ready(j):
                if j == 0:
                    pe.wait_ge(rg_lo, 1)
                if j == 2:
                    pe.wait_ge(o_lo, len(FOX))
                if j == 6:
                    pe.wait_ge(rg_lo, 2)

            with pe.Fori(0, 2) as i:
                for b in range(2):
                    block_of(rows_unit, UNIT0["e_out"] + b * UPB, BLOCK0["e_out"] + b, i=i, per_u=2 * UPB, per_b=2,
                             before=e_out_ready if b == 0 else None, first_tile=tile0_done, tail=SLOTS,
                             src=lambda j: ((eTh[E_OUT_K[j] // 8], eTl[E_OUT_K[j] // 8]), E_OUT_K[j] % 8))

            def ffn(l, y0):
                u0, b0, t0 = UNIT0[f"gu{l}"], BLOCK0[f"gu{l}"], TR0[f"gu{l}"]

                def hidden(i):
                    for t in range(TT):
                        if t == 0:
                            pe.wait_ge(h0_ready, i + (l * FFN_BLOCKS + 1))
                        else:
                            pe.wait_ge(acc_free[1], i + uses(b0 + 1) + 1)
                        transposes(i * 2 + (t0 + t), [hbuf[:, t, q * P:(q + 1) * P] for q in range(4)],
                                   (t0 + t) % 2)

                def body(i, first):
                    block_of(rows_unit, u0, b0, i=i, per_u=2 * UPB, per_b=2,
                             **(turned(TR0[f"ln{2 * l}"], normalised(y0), True) if first else
                                dict(after=lambda j: hidden(i - 1) if j == 1 else None)))
                    block_of(rows_unit, u0 + UPB, b0 + 1, i=i, per_u=2 * UPB, per_b=2, first_tile=up0_done)

                body(0, True)
                with pe.Fori(1, FFN_BLOCKS) as i:
                    body(i, False)
                hidden(FFN_BLOCKS - 1)
                pe.wait_ge(tr_free, t0 + 2 * FFN_BLOCKS - 2)

                def last_hidden(j):
                    if j == DOWN_UNITS - 2:
                        pe.wait_ge(tr_free, t0 + 2 * FFN_BLOCKS)

                with pe.Fori(0, 2) as i:
                    for b in range(2):
                        block_of(rows_unit, UNIT0[f"down{l}"] + b * DOWN_UNITS, BLOCK0[f"down{l}"] + b,
                                 n_units=DOWN_UNITS, i=i, per_u=2 * DOWN_UNITS, per_b=2,
                                 before=last_hidden, src=lambda j: ((hTh, hTl), j * UK), first_tile=tile0_done,
                                 tail=SLOTS)

            ffn(0, 0)

            def compressed(j):
                m = j - 4
                if 0 <= m < 3:
                    b = BLOCK0["o_cq"]
                    pe.wait_ge(acc_free[b % 2], uses(b) + 1)
                    if m == 2:
                        pe.wait_ge(c_norm, 1)
                    transposes(TR0["rms"] + m, [
                        cqs[:, t, k * P:(k + 1) * P] if k < 4 else ckvs[:, t, (k - 4) * P:(k - 3) * P]
                        for k in (2 * m, 2 * m + 1) for t in range(TT)])

            for name, width in (("o_ckv", KV_RANK + ROPE), ("o_cq", QR_RANK), ("o_kv", 2 * SWA_KV * SWA_DH)):
                block_of(rows_unit, UNIT0[name], BLOCK0[name], width=width,
                         **(turned(TR0["ln1"], normalised(8), True) if name == "o_ckv" else {}),
                         after=compressed if name == "o_kv" else None)
            pe.wait_ge(tr_free, TR0["rms"] + 2)
            b = BLOCK0["qb_nope"]
            open_block(b)
            for k in range(QR_RANK // P):
                u = at(UNIT0["qb_nope"] + k)
                unit_ready(u)
                for h in range(MLA_H):
                    if (k, h) == (0, 4):
                        open_block(b + 1)
                    wh, wl = (w[:, u[0], h * P:(h + 1) * P] for w in (whi, wlo))
                    o = acc[(b + h // 4) % 2][h % 4 // 2][:, (h % 2) * T:(h % 2 + 1) * T]
                    mm(o, wh, cTh[:, k, :], start=k == 0 and h % 2 == 0, stop=False, skip_group_check=True)
                    mm(o, wl, cTh[:, k, :], start=False, stop=False, skip_group_check=True)
                    ins = mm(o, wh, cTl[:, k, :], start=False, stop=k == QR_RANK // P - 1, skip_group_check=True)
                ins.then_inc(w_used, 1)
            b = BLOCK0["o_kv"]
            pe.wait_ge(acc_free[b % 2], uses(b) + 1)
            transposes(TR0["kswa"], [kvs[:, t, v * P:(v + 1) * P] for v in range(2) for t in range(TT)])
            b = BLOCK0["qb_rope"]
            open_block(b)
            for k in range(QR_RANK // P):
                rows_unit(at(UNIT0["qb_rope"] + k), b % 2, k, k == 0, k == QR_RANK // P - 1, src=(cTh, cTl), kts=1)
            pe.wait_ge(tr_free, TR0["rms"] + 3)
            for b in range(4):
                u, blk = at(UNIT0["kvb"] + b), BLOCK0["kvb"] + b
                open_block(blk)
                unit_ready(u)
                s = u[0]
                for g in range(2):
                    for k in range(UK):
                        wh, wl = (w[:, s, k * COLS + g * T:k * COLS + g * T + P] for w in (whi, wlo))
                        xh, xl = cTh[:, 4 + k, :], cTl[:, 4 + k, :]
                        o = acc[blk % 2][0][:, g * T:(g + 1) * T]
                        mm(o, wh, xh, start=k == 0, stop=False)
                        mm(o, wl, xh, start=False, stop=False)
                        mm(o, wh, xl, start=False, stop=k == UK - 1)
                for t in range(TT):
                    for k in range(UK):
                        wh, wl = (w[:, s, k * COLS:(k + 1) * COLS].rearrange("p (g n) -> p g n", g=2)[:, :, P:T]
                                  for w in (whi, wlo))
                        xh, xl = (a[:, 4 + k, t * P:(t + 1) * P] for a in (cTh, cTl))
                        o = acc[blk % 2][1][:, t * T:(t + 1) * T].rearrange("p (g n) -> p g n", g=2)
                        mm(o, xh, wh, start=k == 0, stop=False)
                        mm(o, xh, wl, start=False, stop=False)
                        ins = mm(o, xl, wh, start=False, stop=k == UK - 1)
                ins.then_inc(w_used, 1)

            def rope_turned():
                pe.wait_ge(rope_out, 1)
                for m in range(3):
                    transposes(TR0["rope"] + m, [qro[:, t, 2 * c:2 * c + 2, :].rearrange("p a b -> p (a b)")
                                                 for c in range(2 * m, min(2 * m + 2, 5)) for t in range(TT)])

            def odd_scores(unit, bank_, W):
                kind, j, t = unit
                mask = wmr if (kind, t) == ("swa", 1) else bmr
                both = bank_[:].rearrange("p (g k) -> p g k", g=2)[:, :, 0:W]
                mm(both, identr[:], mask[:, :, T - W:T], start=True, stop=False, skip_group_check=True)
                for g in range(2):
                    o = bank_[:, g * T:g * T + W]
                    if kind == "swa":
                        kv = 2 * j // (SWA_Q // SWA_KV)
                        ins = mm(o, qT[:, j, t * P:(t + 1) * P], kz[:, kv, g, 0:W], start=False, stop=True,
                                 skip_group_check=True)
                    else:
                        h = 2 * j + g
                        mm(o, qnT[:, h, t * P:(t + 1) * P], knT[:, h, 0:W], start=False, stop=False,
                           skip_group_check=True)
                        ins = mm(o, qrT[:, j, t * P:(t + 1) * P], krz[:, g, 0:W], start=False, stop=True,
                                 skip_group_check=True)
                ins.then_inc(sc_ready, 1)

            def odd_values(unit, g, k):
                kind, j, t = unit
                if kind == "swa":
                    return vd[:, k, 2 * j // (SWA_Q // SWA_KV), :]
                return vm[:, k, 2 * j + g, :]

            def odd_step(s):
                if s == 0:
                    pe.wait_ge(tr_free, TR0["rope"] + 3)
                    pe.wait_ge(masks_r, 1)
                    for p in range(2):
                        pe.wait_ge(acc_free[p], uses(BLOCK0["o_q"] + p))
                if s == 8:
                    b = BLOCK0["o_q"]
                    pe.wait_ge(acc_free[b % 2], uses(b) + 1)
                if s == 16:
                    b = BLOCK0["o_q"] + 1
                    pe.wait_ge(acc_free[b % 2], uses(b) + 1)
                attention_step(len(FOX), ODD, s, odd_scores, odd_values)

            def after_query_unit(b):
                return lambda j: rope_turned() if (b, j) == (0, 0) else odd_step(b * UPB + j - 1)

            for b in range(2):
                block_of(cols_unit, UNIT0["o_q"] + b * UPB, BLOCK0["o_q"] + b, after=after_query_unit(b))

            b0 = BLOCK0["o_out"]
            steps = 2 * UPB - 1
            for j, (b, k) in enumerate(O_OUT_HEAD):
                if k == 8:
                    open_block(b0 + b)
                if j == 0:
                    pe.wait_ge(o_lo, len(FOX) + 8)
                if j == 8:
                    pe.wait_ge(o_lo, len(FOX) + 16)
                if j == 12:
                    pe.wait_ge(o_lo, len(FOX) + len(ODD))
                src, k0 = ((mTh, mTl), k - 8) if k >= 8 else ((sTh, sTl), k) if k < 4 else ((xTh, xTl), k)
                rows_unit(at(UNIT0["o_out"] + j), (b0 + b) % 2, k0, k == 8, k == 6, src=src, first_tile=tile0_done)
                if steps < ODD_STEPS:
                    odd_step(steps)
                    steps += 1
            for b in range(2, 4):
                block_of(rows_unit, UNIT0["o_out"] + b * UPB, b0 + b, first_tile=tile0_done, tail=SLOTS,
                         src=lambda j: ((mTh, mTl), j * UK - 8) if j >= 4 else ((sTh, sTl), j * UK) if j < 2
                         else ((xTh, xTl), j * UK))
            assert steps == ODD_STEPS, steps
            ffn(1, 16)

        @block.scalar
        def _(act):
            chain = [0]
            activate = nc.scalar.activation

            def link(ins):
                chain[0] += 1
                ins.then_inc(av, 1)
                act.wait_ge(av, chain[0])

            def high(u, span=UNIT):
                slot, rounds = u
                act.wait_ge(w_in[slot], rounds * 16 + 16)
                if not (isinstance(rounds, int) and rounds == 0):
                    act.wait_ge(w_used, number(u) - (SLOTS - 1))
                activate(whi[:, slot, 0:span], raw[:, slot, 0:span], ACT.Copy).then_inc(w_hi, 1)

            def ahead(u0, j, i=0, per=0):
                if not (isinstance(i, int) and i * per + u0 + j + SLOTS >= UNITS):
                    high(at(u0 + j + SLOTS, i, per), span_of(u0 + j + SLOTS, i, per))

            def split_out(n, dst, parity=None):
                act.wait_ge(tr_ready, n + 1)
                activate(dst, trb[n % 2 if parity is None else parity][:].rearrange("p (k t) -> p k t", k=4),
                         ACT.Copy).then_inc(tr_hi, 1)

            def stream_high(n0, c, t):
                split_out(n0 + 2 * c + t, xTh[:, 4 * c:4 * c + 4, t * P:(t + 1) * P])

            def first_block(n0, u0):
                for c in range(4):
                    for t in range(TT):
                        stream_high(n0, c, t)
                    if c < 2:
                        high(at(2 * c))
                        high(at(2 * c + 1))
                    for j in AHEAD_OF_CHUNK[c]:
                        if j == 6:
                            forget_high()
                        ahead(u0, j)

            def ln_root(l, t):
                act.wait_ge(ln_var, 2 * l + t + 1)
                activate(lnv[:, 1, t:t + 1], lnv[:, 0, t:t + 1], ACT.Sqrt).then_inc(ln_sd, 1)

            def ln_block(l, n0, last0, u0):
                activate(lnv[:, 3, 0:1], ident[:, 0:1], ACT.Sqrt)
                ln_root(l, 0)
                for j in range(SLOTS - 1):
                    ahead(last0, j)
                stream_high(n0, 0, 0)
                ln_root(l, 1)
                ahead(last0, SLOTS - 1)
                stream_high(n0, 0, 1)
                for c in range(1, 4):
                    for t in range(TT):
                        stream_high(n0, c, t)
                    for j in AHEAD_OF_CHUNK[c]:
                        ahead(u0, j)

            act.wait_ge(consts, 1)
            activate(identr[:], ident[:], ACT.Copy)

            def read_cols(b, dst, func=ACT.Copy, scale=1.0):
                act.wait_ge(w_used, BLOCK_END[b])
                for k in range(2):
                    ins = activate(dst(k), acc[b % 2][k][:].rearrange("p (c t) -> p c t", c=2), func, scale=scale)
                ins.then_inc(acc_free[b % 2], 1)

            def forget_high():
                act.wait_ge(wf_in, 16)
                act.wait_ge(consts, 2)
                activate(wfh[:, :, 0:FOX_HEADS], wf[:], ACT.Copy).then_inc(wf_hi, 1)

            for b in range(2):
                if b == 0:
                    first_block(TR0["x"], UNIT0["e_u"])
                else:
                    for j in range(UPB):
                        ahead(UNIT0["e_u"] + b * UPB, j)
                read_cols(BLOCK0["e_u"] + b, lambda k: uT[:, 4 * b + 2 * k:4 * b + 2 * k + 2, CONV - 1:])
            for b in range(2):
                for j in range(UPB):
                    ahead(UNIT0["e_q"] + b * UPB, j)
                    if b == 0 and j == 1:
                        act.wait_ge(f_neg, 1)
                        activate(fz[:, 2, :], fz[:, 1, :], ACT.Exp).then_inc(f_exp, 1)
                    if b == 0 and j == 3:
                        act.wait_ge(lam_x, 1)
                        activate(lz[:, 2, :], lz[:, 1, :], ACT.Exp).then_inc(lam_e, 1)
                    if b == 1 and j == 2:
                        act.wait_ge(f_log, 1)
                        activate(nlf[:].rearrange("p t h q -> p (t h) q"),
                                 fz[:, 6, :].unsqueeze(2).broadcast_to([P, TT * FOX_HEADS, P]),
                                 ACT.Copy, scale=-1.0).then_inc(f_rep, 1)
                read_cols(BLOCK0["e_q"] + b, lambda k: qT[:, 4 * b + 2 * k:4 * b + 2 * k + 2, :], scale=SCALES["fox"])
            for b in range(2):
                for j in range(UPB):
                    ahead(UNIT0["e_k"] + b * UPB, j)
                    if b == 0:
                        act.wait_ge(gates_ready, j + 1)
                        activate(rt[:, j, :], scb[j % 2][:, 0:T], ACT.Sigmoid, bias=cols[:, 1, j:j + 1])
                        activate(it[:, j, :], scb[j % 2][:, T:2 * T], ACT.Sigmoid,
                                 bias=cols[:, 2, j:j + 1]).then_inc(gates_free, 1)
                    if b == 1 and j < 4:
                        if j == 0:
                            act.wait_ge(lam_done, 1)
                            act.wait_ge(gates_free, 8)
                            act.wait_ge(conv_done, 8)
                            act.wait_ge(c_done, 1)
                        for n in (2 * j, 2 * j + 1):
                            ins = activate(gT[:, n, :], rt[:, n, :], ACT.Tanh, scale=clam[:, 0, n:n + 1])
                        ins.then_inc(rg_t, 1)
                    if b == 1 and j >= 4:
                        for n in (2 * j - 8, 2 * j - 7):
                            ins = activate(uT[:, n, 0:T], rt[:, n, :], ACT.Exp, scale=clam[:, 1, n:n + 1])
                        if j == 7:
                            ins.then_inc(rg_at, 1)
                read_cols(BLOCK0["e_k"] + b, lambda k: kT[:, 4 * b + 2 * k:4 * b + 2 * k + 2, :])
            for b in range(2):
                for j in range(UPB):
                    ahead(UNIT0["e_v"] + b * UPB, j)
                    if b == 1 and j == 1:
                        act.wait_ge(rg_var, 1)
                        activate(gT[:], gT[:], ACT.Sqrt).then_inc(rg_sq, 1)
                blk = BLOCK0["e_v"] + b
                act.wait_ge(w_used, BLOCK_END[blk])
                for t in range(TT):
                    ins = activate(vt[:, t, b * COLS:(b + 1) * COLS], acc[blk % 2][t][:], ACT.Copy)
                ins.then_inc(acc_free[blk % 2], 1)

            def attention_step(n0, units, s):
                N = len(units)
                if 2 <= s < N + 2:
                    n = n0 + s - 2
                    kind, j, t = units[s - 2]
                    act.wait_ge(pt_ready, n + 1)
                    if s >= 4:
                        act.wait_ge(o_ready, n - 1)
                    W = 2 * (t + 1) * P
                    activate(pT[:, n % 2, 0:2 * (t + 1), :].rearrange("p a b -> p (a b)"),
                             trb[0][:, 0:W], ACT.Copy).then_inc(pt_copied, 1)
                if 3 <= s < N + 3:
                    n = n0 + s - 3
                    act.wait_ge(o_ready, n + 1)
                    t = units[s - 3][2]
                    for rows, hi, lo, k0, k1, cols_ in out_parts(units[s - 3]):
                        ins = activate(hi[rows, k0:k1, t * P:(t + 1) * P],
                                       trb[1][rows, cols_].rearrange("p (a b) -> p a b", b=P), ACT.Copy)
                    ins.then_inc(o_hi, 1)
                if s < N:
                    n = n0 + s
                    kind, j, t = units[s]
                    act.wait_ge(nm_ready, n + 1)
                    if s >= 2:
                        act.wait_ge(pt_ready, n - 1)
                    W = (t + 1) * P
                    for g in range(2):
                        if kind == "swa":
                            h = 2 * j + g
                            activate(es[:, n % 2, g:g + 1], sinks[:, h:h + 1], ACT.Exp, bias=nm[:, n % 2, g:g + 1])
                        src = s_sb[:, n % 2, g, 0:W] if kind == "fox" else scb[n % 2][:, g * T:g * T + W]
                        ins = activate(p_sb[:, n % 2, g, 0:W], src, ACT.Exp,
                                       bias=nm[:, n % 2, g:g + 1], accum_out=lsum[:, n % 2, g:g + 1])
                    ins.then_inc(ex_ready, 1)

            for b in range(2):
                for j in range(UPB):
                    if b * UPB + j in FOX_AFTER:
                        attention_step(0, FOX, FOX_AFTER.index(b * UPB + j))
                    ahead(UNIT0["e_g"] + b * UPB, j)
                read_cols(BLOCK0["e_g"] + b, lambda k: gT[:, 4 * b + 2 * k:4 * b + 2 * k + 2, :],
                          ACT.Gelu_apprx_tanh)
                act.wait_ge(rg_out, b + 1)
                activate(eTh[1][:, 4 * b:4 * b + 4, :], gT[:, 4 * b:4 * b + 4, :], ACT.Copy).then_inc(rg_hi, 1)

            for j in range(4 * UPB - SLOTS):
                ahead(UNIT0["e_out"], j)

            def ffn(l):
                u0, b0, t0 = UNIT0[f"gu{l}"], BLOCK0[f"gu{l}"], TR0[f"gu{l}"]

                def hidden(i):
                    for t in range(TT):
                        split_out(i * 2 + (t0 + t), hTh[:, bass.ds(i * 4, 4), t * P:(t + 1) * P],
                                  (t0 + t) % 2)

                def body(i, first):
                    if first:
                        ln_block(2 * l, TR0[f"ln{2 * l}"], u0 - SLOTS, u0)
                    else:
                        for j in range(UPB):
                            ahead(u0, j, i, 2 * UPB)
                            if j == 2:
                                hidden(i - 1)
                    act.wait_ge(w_used, i * (2 * UPB) + BLOCK_END[b0])
                    act.wait_ge(acc_free[1], i + uses(b0 + 1))
                    for t in range(TT):
                        ins = activate(sg[:, t, :], acc[0][t][:], ACT.Silu)
                    ins.then_inc(acc_free[0], 1)
                    for j in range(UPB, 2 * UPB):
                        ahead(u0, j, i, 2 * UPB)

                body(0, True)
                with act.Fori(1, FFN_BLOCKS) as i:
                    body(i, False)
                hidden(FFN_BLOCKS - 1)
                d0 = UNIT0[f"down{l}"]
                for j in range(4 * DOWN_UNITS - SLOTS):
                    ahead(d0, j)

            ffn(0)

            ln_block(1, TR0["ln1"], UNIT0["o_ckv"] - SLOTS, UNIT0["o_ckv"])
            b = BLOCK0["o_ckv"]
            act.wait_ge(w_used, BLOCK_END[b])
            for t in range(TT):
                src = acc[b % 2][t]
                activate(ckvs[:, t, :], src[:, 0:KV_RANK], ACT.Copy)
                activate(p_sb[:, 1, t, :], src[:, 0:KV_RANK], ACT.Square, accum_out=rms[:, 0, 2 + t:3 + t])
                for c in range(2):
                    ins = activate(qr[:, t, 8 + c, :], src[:, KV_RANK:KV_RANK + ROPE], ACT.Copy)
            ins.then_inc(acc_free[b % 2], 1)
            for j in range(UPB - 1):
                ahead(UNIT0["o_cq"], j)
                if j == 3:
                    act.wait_ge(trig_arg, 1)
                    activate(trig[:, 4:6, :, :], trig[:, 2:4, :, :], ACT.Sin).then_inc(trig_done, 1)
                if j == 4:
                    act.wait_ge(consts, 3)
                    activate(bmr[:], bmask[:], ACT.Copy)
                    activate(wmr[:], wmask[:], ACT.Copy).then_inc(masks_r, 1)
                if j == 5:
                    activate(lnv[:, 3, 0:1], ident[:, 0:1], ACT.Sqrt)
            b = BLOCK0["o_cq"]
            act.wait_ge(w_used, BLOCK_END[b])
            act.wait_ge(masks_r, 1)
            for t, scratch in enumerate((p_sb, s_sb)):
                ins = activate(scratch[:, 0, :, :].rearrange("p a b -> p (a b)"), acc[b % 2][t][:], ACT.Square,
                               accum_out=rms[:, 0, t:t + 1])
            ins.then_inc(sq_done, 1)
            act.wait_ge(rms_var, 1)
            activate(rms[:, 2, :], rms[:, 1, :], ACT.Sqrt).then_inc(rms_sd, 1)
            ahead(UNIT0["o_cq"], UPB - 1)
            for j in range(UPB - 1):
                m = j - 4
                if m >= 0:
                    n = TR0["rms"] + m
                    act.wait_ge(tr_ready, n + 1)
                    for k in range(2):
                        ins = activate(cTh[:, 2 * m + k, :], trb[n % 2][:, k * T:(k + 1) * T], ACT.Copy,
                                       scale=qkg[:, 2 * m + k:2 * m + k + 1])
                    ins.then_inc(tr_hi, 1)
                if j < UPB - 2:
                    ahead(UNIT0["o_kv"], j)
            b = BLOCK0["o_kv"]
            act.wait_ge(w_used, BLOCK_END[b])
            for t in range(TT):
                src = acc[b % 2][t]
                activate(kvs[:, t, 0:P], src[:, 0:P], ACT.Copy)
                activate(kvs[:, t, P:P + 64], src[:, 64:P], ACT.Copy)
                activate(kvs[:, t, P + 64:2 * P], src[:, 0:64], ACT.Copy)
                for half in range(2):
                    ins = activate(vd[:, t, :, half * 64:(half + 1) * 64],
                                   src[:, P:2 * P].rearrange("p (v d) -> p v d", v=2), ACT.Copy)
            ins.then_inc(acc_free[b % 2], 1)
            ahead(UNIT0["o_kv"], UPB - 2)
            ahead(UNIT0["o_kv"], UPB - 1)
            for j in range(3):
                ahead(UNIT0["qb_nope"], j)
            for b in range(2):
                read_cols(BLOCK0["qb_nope"] + b, lambda k: qnT[:, 4 * b + 2 * k:4 * b + 2 * k + 2, :],
                          scale=SCALES["mla"])
            ahead(UNIT0["qb_nope"], 3)
            for j in range(3):
                ahead(UNIT0["qb_rope"], j)
            b = BLOCK0["qb_rope"]
            act.wait_ge(w_used, BLOCK_END[b])
            for t in range(TT):
                ins = activate(qr[:, t, 0:8, :], acc[b % 2][t][:].rearrange("p (h d) -> p h d", d=ROPE), ACT.Copy,
                               scale=SCALES["mla"])
            ins.then_inc(acc_free[b % 2], 1)
            ahead(UNIT0["qb_rope"], 3)
            for b in range(4):
                ahead(UNIT0["kvb"], b)
                blk = BLOCK0["kvb"] + b
                act.wait_ge(w_used, BLOCK_END[blk])
                activate(knT[:, 2 * b:2 * b + 2, :], acc[blk % 2][0][:].rearrange("p (g t) -> p g t", g=2), ACT.Copy)
                activate(vm[:, :, 2 * b:2 * b + 2, :].rearrange("p t g d -> p t (g d)"),
                         acc[blk % 2][1][:].rearrange("p (t d) -> p t d", t=2), ACT.Copy).then_inc(acc_free[blk % 2], 1)
            for b in range(2):
                for j in range(UPB):
                    if b * UPB + j >= 1:
                        attention_step(len(FOX), ODD, b * UPB + j - 1)
                    ahead(UNIT0["o_q"] + b * UPB, j)
                read_cols(BLOCK0["o_q"] + b, lambda k: qT[:, 4 * b + 2 * k:4 * b + 2 * k + 2, :], scale=SCALES["swa"])
            for j in range(4 * UPB - SLOTS):
                if 2 * UPB - 1 + j < ODD_STEPS:
                    attention_step(len(FOX), ODD, 2 * UPB - 1 + j)
                ahead(UNIT0["o_out"], j)
            ffn(1)
            activate(lnv[:, 3, 0:1], ident[:, 0:1], ACT.Sqrt)
            ln_root(3, 0)
            ln_root(3, 1)

        @block.vector
        def _(dve):
            chain = [0]
            v = nc.vector

            def link(ins):
                chain[0] += 1
                ins.then_inc(dv, 1)
                dve.wait_ge(dv, chain[0])

            def low(u, span=UNIT):
                slot = u[0]
                dve.wait_ge(w_hi, number(u) + 1)
                v.tensor_tensor(wlo[:, slot, 0:span], raw[:, slot, 0:span], whi[:, slot, 0:span].bitcast(F32),
                                ALU.subtract).then_inc(w_lo, 1)

            def ahead(u0, j, i=0, per=0):
                if not (isinstance(i, int) and i * per + u0 + j + SLOTS >= UNITS):
                    low(at(u0 + j + SLOTS, i, per), span_of(u0 + j + SLOTS, i, per))

            def rest_out(parity, h, hi, dst):
                dve.wait_ge(tr_hi, h + 1)
                v.tensor_tensor(dst, trb[parity][:].rearrange("p (k t) -> p k t", k=4),
                                hi.bitcast(F32), ALU.subtract).then_inc(tr_free, 1)

            def stream_low(n0, h0, n):
                t, c = n % 2, n // 2
                at_ = (slice(None), slice(4 * c, 4 * c + 4), slice(t * P, (t + 1) * P))
                rest_out((n0 + n) % 2, h0 + n, xTh[at_], xTl[at_])

            def log1p_of(e, y, q, s, out_):
                link(v.tensor_scalar(y, e, 2.0, None, ALU.add))
                link(v.reciprocal(y, y))
                link(v.tensor_tensor(s, e, y, ALU.mult))
                link(v.tensor_tensor(q, s, s, ALU.mult))
                link(v.tensor_scalar(y, q, 1.0 / (2 * LOG1P_TERMS + 1), None, ALU.mult))
                for k in range(LOG1P_TERMS - 1, 0, -1):
                    link(v.scalar_tensor_tensor(out=y, in0=y, scalar=1.0 / (2 * k + 1), in1=q,
                                                op0=ALU.add, op1=ALU.mult))
                link(v.scalar_tensor_tensor(out=y, in0=y, scalar=1.0, in1=s, op0=ALU.add, op1=ALU.mult))
                link(v.tensor_scalar(out_, y, 2.0, None, ALU.mult))

            def first_block(n0, h0, u0):
                for c in range(4):
                    stream_low(n0, h0, 2 * c)
                    stream_low(n0, h0, 2 * c + 1)
                    if c < 2:
                        low(at(2 * c))
                        low(at(2 * c + 1))
                    for j in AHEAD_OF_CHUNK[c]:
                        if j == 6:
                            forget_low()
                        ahead(u0, j)

            def conv(n):
                link(v.tensor_scalar(uc[:, n, :], uT[:, n, 0:T], cw[:, 0, n:n + 1], cols[:, 0, n:n + 1],
                                     ALU.mult, ALU.add))
                for k in range(1, CONV):
                    ins = v.scalar_tensor_tensor(out=uc[:, n, :], in0=uT[:, n, k:k + T], scalar=cw[:, k, n:n + 1],
                                                 in1=uc[:, n, :], op0=ALU.mult, op1=ALU.add)
                    if k < CONV - 1:
                        link(ins)
                ins.then_inc(conv_done, 1)

            def forget_low():
                dve.wait_ge(wf_hi, 1)
                v.tensor_tensor(wfl[:, :, 0:FOX_HEADS], wf[:], wfh[:, :, 0:FOX_HEADS].bitcast(F32),
                                ALU.subtract).then_inc(wf_split, 1)

            first_block(TR0["x"], HI0["x"], UNIT0["e_u"])
            for j in range(UPB):
                ahead(UNIT0["e_u"] + UPB, j)
                if j == 3:
                    dve.wait_ge(acc_free[0], uses(BLOCK0["e_u"]) + 1)
                    dve.wait_ge(ev_in, 11 * 16)
                    dve.wait_ge(consts, 2)
                if j >= 4:
                    conv(j - 4)
            for b in range(2):
                for j in range(UPB):
                    if b == 0 and j == 0:
                        dve.wait_ge(f_ready, 1)
                        v.tensor_copy(fT[:], scb[0][:, 0:T]).then_inc(f_copied, 1)
                    ahead(UNIT0["e_q"] + b * UPB, j)
                    if b == 0 and j == 1:
                        dve.wait_ge(f_ready, 2)
                        for t in range(TT):
                            ins = v.tensor_tensor(fz[:, 0, t * 8:t * 8 + 8], scb[1][:, t * P:t * P + 8], fb[:], ALU.add)
                        link(ins)
                        link(v.tensor_scalar(fz[:, 1, :], fz[:, 0, :], -1.0, None, ALU.mult))
                        v.tensor_tensor(fz[:, 1, :], fz[:, 1, :], fz[:, 0, :], ALU.min).then_inc(f_neg, 1)
                        link(v.tensor_scalar(lz[:, 0, :], cols[:, 3, :], -1.0, None, ALU.mult))
                        v.tensor_tensor(lz[:, 1, :], lz[:, 0, :], cols[:, 3, :], ALU.min).then_inc(lam_x, 1)
                    if b == 0 and j == 4:
                        dve.wait_ge(f_exp, 1)
                        log1p_of(fz[:, 2, :], fz[:, 3, :], fz[:, 4, :], fz[:, 5, :], fz[:, 1, :])
                        v.scalar_tensor_tensor(out=fz[:, 6, :], in0=fz[:, 0, :], scalar=0.0, in1=fz[:, 1, :],
                                               op0=ALU.min, op1=ALU.subtract).then_inc(f_log, 1)
                    if b == 0 and j == 6:
                        dve.wait_ge(lam_e, 1)
                        log1p_of(lz[:, 2, :], lz[:, 3, :], lz[:, 4, :], lz[:, 5, :], lz[:, 1, :])
                        link(v.scalar_tensor_tensor(out=lz[:, 3, :], in0=lz[:, 0, :], scalar=0.0, in1=lz[:, 1, :],
                                                    op0=ALU.max, op1=ALU.add))
                        v.tensor_scalar(clam[:, 0, :], lz[:, 3, :], LRU_C, None, ALU.mult)
                        v.tensor_scalar(clam[:, 1, :], lz[:, 3, :], -LRU_C, None, ALU.mult).then_inc(lam_done, 1)
                    if b == 1:
                        if j == 0:
                            dve.wait_ge(acc_free[1], uses(BLOCK0["e_u"]) + 1)
                        if j < 4:
                            conv(j + 4)
                        if j == 4:
                            dve.wait_ge(c_ready, 1)
                            v.tensor_copy(cq[:].rearrange("p t h -> p (t h)"), scb[1][:, 0:16]).then_inc(c_done, 1)
            def decayed(m):
                n = m // 2
                if m % 2 == 0:
                    dve.wait_ge(rg_t, n // 2 + 1)
                    link(v.tensor_scalar(rgd[:, n, :], gT[:, n, :], 1.0, None, ALU.add))
                    link(v.reciprocal(rgd[:, n, :], rgd[:, n, :]))
                else:
                    link(v.scalar_tensor_tensor(out=gT[:, n, :], in0=gT[:, n, :], scalar=2.0, in1=rgd[:, n, :],
                                                op0=ALU.mult, op1=ALU.mult))
                    ins = v.tensor_scalar(gT[:, n, :], gT[:, n, :], 1e-34, None, ALU.max)
                    if n == 7:
                        ins.then_inc(rg_var, 1)

            for b in range(2):
                for j in range(UPB):
                    ahead(UNIT0["e_k"] + b * UPB, j)
                    if b == 1 and j >= 1:
                        decayed(j - 1)
            for b in range(2):
                for j in range(UPB):
                    ahead(UNIT0["e_v"] + b * UPB, j)
                    n = b * UPB + j
                    if n < 9:
                        decayed(n + UPB - 1)
                    if n == 8:
                        link(v.tensor_tensor(it[:], it[:], uc[:], ALU.mult))
                    if n == 9:
                        dve.wait_ge(rg_at, 1)
                        dve.wait_ge(rg_sq, 1)
                        link(v.tensor_tensor(it[:], it[:], gT[:], ALU.mult))
                    if 10 <= n < 14:
                        for m in (2 * n - 20, 2 * n - 19):
                            ins = v.tensor_tensor_scan(rt[:, m, :], uT[:, m, 0:T], it[:, m, :], 0.0, ALU.mult, ALU.add)
                        if n == 13:
                            ins.then_inc(rg_h, 1)

            def attention_step(n0, units, s, scores):
                N = len(units)
                if s < N:
                    n = n0 + s
                    kind, j, t = units[s]
                    W = (t + 1) * P
                    dve.wait_ge(sc_ready, n + 1)
                    if s >= 2:
                        dve.wait_ge(ex_ready, n - 1)
                    link(v.tensor_reduce(mx[:, n % 2, :], scores(units[s], n, W), AX.X, ALU.max))
                    if kind == "swa":
                        link(v.tensor_tensor(mx[:, n % 2, :], mx[:, n % 2, :], sinks[:, 2 * j:2 * j + 2], ALU.max))
                    v.tensor_scalar(nm[:, n % 2, :], mx[:, n % 2, :], -1.0, None, ALU.mult).then_inc(nm_ready, 1)
                if 1 <= s < N + 1:
                    n = n0 + s - 1
                    kind, j, t = units[s - 1]
                    W = (t + 1) * P
                    dve.wait_ge(ex_ready, n + 1)
                    if kind == "swa":
                        link(v.tensor_tensor(lsum[:, n % 2, :], lsum[:, n % 2, :], es[:, n % 2, :], ALU.add))
                    link(v.reciprocal(rl[:, n % 2, :], lsum[:, n % 2, :]))
                    probs = p_sb[:, n % 2, :, 0:W]
                    v.tensor_tensor(probs, probs, rl[:, n % 2, :].unsqueeze(2).broadcast_to([P, 2, W]),
                                    ALU.mult).then_inc(pr_ready, 1)
                if s >= 3:
                    n = n0 + s - 3
                    t = units[s - 3][2]
                    dve.wait_ge(o_hi, n + 1)
                    for rows, hi, lo, k0, k1, cols_ in out_parts(units[s - 3]):
                        ins = v.tensor_tensor(lo[rows, k0:k1, t * P:(t + 1) * P],
                                              trb[1][rows, cols_].rearrange("p (a b) -> p a b", b=P),
                                              hi[rows, k0:k1, t * P:(t + 1) * P].bitcast(F32), ALU.subtract)
                    ins.then_inc(o_lo, 1)

            def fox_masked(unit, n, W):
                kind, j, t = unit
                for g in range(2):
                    h = 2 * j + g
                    ins = v.scalar_tensor_tensor(out=s_sb[:, n % 2, g, 0:W], in0=scb[n % 2][:, g * T:g * T + W],
                                                 scalar=cq[:, t, h:h + 1], in1=cmask[:, T - W:T],
                                                 op0=ALU.add, op1=ALU.add)
                link(ins)
                return s_sb[:, n % 2, :, 0:W]

            def odd_masked(unit, n, W):
                return scb[n % 2][:].rearrange("p (g k) -> p g k", g=2)[:, :, 0:W]

            for b in range(2):
                for j in range(UPB):
                    if b * UPB + j in FOX_AFTER:
                        attention_step(0, FOX, FOX_AFTER.index(b * UPB + j), fox_masked)
                    ahead(UNIT0["e_g"] + b * UPB, j)
                blk = BLOCK0["e_g"] + b
                part = (slice(None), slice(4 * b, 4 * b + 4), slice(None))
                if b == 0:
                    dve.wait_ge(rg_h, 1)
                dve.wait_ge(acc_free[blk % 2], uses(blk) + 1)
                v.tensor_tensor(gT[part], rt[part], gT[part], ALU.mult).then_inc(rg_out, 1)
                dve.wait_ge(rg_hi, b + 1)
                v.tensor_tensor(eTl[1][part], gT[part], eTh[1][part].bitcast(F32), ALU.subtract).then_inc(rg_lo, 1)

            def residual(b, c, phase, t):
                pair, cs = b % 2, slice(c * COLS, (c + 1) * COLS)
                if t == 0:
                    dve.wait_ge(tile0_done, 4 * phase + c + 1)
                else:
                    dve.wait_ge(w_used, BLOCK_END[b])
                done, count = (res0_done, 4 * phase + c + 1) if t == 0 else (acc_free[pair], uses(b) + 1)
                v.scalar_tensor_tensor(out=xres[:, t, cs], in0=xres[:, t, cs], scalar=ALPHA, in1=acc[pair][t][:],
                                       op0=ALU.mult, op1=ALU.add).then_inc(done, 1)
                dve.wait_ge(done, count)
                v.bn_stats(stats[:, t, c, :], xres[:, t, cs]).then_inc(stats_done[t], 1)

            def residual_block(u0, b, c, phase, n_units, ln=None):
                for j in range(n_units - SLOTS):
                    ahead(u0, j)
                residual(b, c, phase, 0)
                if ln:
                    ln.moments(0)
                    ln.affine(0)
                    if ln.l == 3:
                        return
                for j in range(n_units - SLOTS, n_units - (3 if ln else 1)):
                    ahead(u0, j)
                residual(b, c, phase, 1)
                if not ln:
                    ahead(u0, n_units - 1)

            class LayerNorm:

                def __init__(self, l, order):
                    self.l, self.order, self.rooted = l, order, [False, False]

                def moments(self, t):
                    dve.wait_ge(stats_done[t], 4 * (self.l + 1))
                    link(v.bn_aggr(mv[:, t, :], stats[:, t, :, :].rearrange("p a b -> p (a b)")))
                    v.tensor_scalar(lnv[:, 0, t:t + 1], mv[:, t, 1:2], LN_EPS, None, ALU.add).then_inc(ln_var, 1)

                def affine(self, n):
                    t, c = self.order(n)
                    cs = slice(c * COLS, (c + 1) * COLS)
                    if n == 0:
                        dve.wait_ge(gb_in, 32 * (self.l + 1))
                    link(v.scalar_tensor_tensor(out=xres[:, t, cs], in0=xres[:, t, cs], scalar=mv[:, t, 0:1],
                                                in1=gb[:, 0, cs], op0=ALU.subtract, op1=ALU.mult))
                    if not self.rooted[t]:
                        self.rooted[t] = True
                        dve.wait_ge(ln_sd, 2 * self.l + t + 1)
                        link(v.reciprocal(lnv[:, 2, t:t + 1], lnv[:, 1, t:t + 1]))
                    v.scalar_tensor_tensor(out=xres[:, t, cs], in0=xres[:, t, cs], scalar=lnv[:, 2, t:t + 1],
                                           in1=gb[:, 1, cs], op0=ALU.mult, op1=ALU.add).then_inc(y_ready, 1)

            def ln_block(ln, n0, h0, u0):
                stream_low(n0, h0, 0)
                ln.moments(1)
                ahead(u0, -3)
                ln.affine(1)
                ahead(u0, -2)
                stream_low(n0, h0, 1)
                ln.affine(2)
                ln.affine(3)
                ahead(u0, -1)
                stream_low(n0, h0, 2)
                stream_low(n0, h0, 3)
                ln.affine(4)
                ln.affine(5)
                ahead(u0, 0)
                stream_low(n0, h0, 4)
                stream_low(n0, h0, 5)
                ahead(u0, 1)
                ln.affine(6)
                ln.affine(7)
                ahead(u0, 2)
                stream_low(n0, h0, 6)
                stream_low(n0, h0, 7)
                for j in range(3, UPB):
                    ahead(u0, j)

            def by_columns(n):
                return n % 2, n // 2

            def by_rows(n):
                return n // 4, n % 4

            norms = [LayerNorm(l, by_columns if l < 3 else by_rows) for l in range(4)]
            for c in range(4):
                residual_block(UNIT0["e_out"] + c * UPB, BLOCK0["e_out"] + c, c, 0, UPB, norms[0] if c == 3 else None)

            def ffn(l):
                u0, b0, t0, h0 = UNIT0[f"gu{l}"], BLOCK0[f"gu{l}"], TR0[f"gu{l}"], HI0[f"gu{l}"]

                def hidden(i):
                    for t in range(TT):
                        at_ = (slice(None), bass.ds(i * 4, 4), slice(t * P, (t + 1) * P))
                        rest_out((t0 + t) % 2, i * 2 + (h0 + t), hTh[at_], hTl[at_])

                def body(i, first):
                    if first:
                        ln_block(norms[2 * l], TR0[f"ln{2 * l}"], HI0[f"ln{2 * l}"], u0)
                    else:
                        for j in range(UPB):
                            ahead(u0, j, i, 2 * UPB)
                            if j == 2:
                                hidden(i - 1)
                    for j in range(UPB, 2 * UPB - 1):
                        ahead(u0, j, i, 2 * UPB)
                    dve.wait_ge(acc_free[0], i + uses(b0) + 1)
                    if not first:
                        dve.wait_ge(tr_ready, i * 2 + t0)
                    for t, done in enumerate((h0_ready, acc_free[1])):
                        if t == 0:
                            dve.wait_ge(up0_done, i + (l * FFN_BLOCKS + 1))
                        else:
                            dve.wait_ge(w_used, i * (2 * UPB) + BLOCK_END[b0 + 1])
                        v.tensor_tensor(hbuf[:, t, :], sg[:, t, :], acc[1][t][:], ALU.mult).then_inc(done, 1)
                    ahead(u0, 2 * UPB - 1, i, 2 * UPB)

                body(0, True)
                with dve.Fori(1, FFN_BLOCKS) as i:
                    body(i, False)
                hidden(FFN_BLOCKS - 1)
                d0, b0 = UNIT0[f"down{l}"], BLOCK0[f"down{l}"]

                for c in range(4):
                    residual_block(d0 + c * DOWN_UNITS, b0 + c, c, 1 + 2 * l, DOWN_UNITS,
                                   norms[1 + 2 * l] if c == 3 else None)

            ffn(0)

            ln_block(norms[1], TR0["ln1"], HI0["ln1"], UNIT0["o_ckv"])
            for j in range(UPB - 1):
                ahead(UNIT0["o_cq"], j)
                if j == 0:
                    dve.wait_ge(od_in, 4 * 16)
                    dve.wait_ge(consts, 3)
                    link(v.tensor_copy(pos[:], pos_i[:]))
                    for t in range(TT):
                        ins = v.tensor_scalar(trig[:, 0, t, :], invf[:], pos[:, t:t + 1], None, ALU.mult)
                    link(ins)
                    rnd = 1.5 * 2.0 ** 23
                    c1 = 6.28125
                    c2 = 2 * math.pi - c1
                    link(v.tensor_scalar(trig[:, 1], trig[:, 0], 1.0 / (2 * math.pi), rnd, ALU.mult, ALU.add))
                    link(v.tensor_scalar(trig[:, 1], trig[:, 1], -rnd, None, ALU.add))
                    link(v.scalar_tensor_tensor(out=trig[:, 2], in0=trig[:, 1], scalar=-c1, in1=trig[:, 0],
                                                op0=ALU.mult, op1=ALU.add))
                    link(v.scalar_tensor_tensor(out=trig[:, 2], in0=trig[:, 1], scalar=-c2, in1=trig[:, 2],
                                                op0=ALU.mult, op1=ALU.add))
                if j == 1:
                    link(v.tensor_scalar(trig[:, 3], trig[:, 2], math.pi / 2, None, ALU.add))
                    link(v.tensor_scalar(trig[:, 1], trig[:, 3], math.pi, -2 * math.pi, ALU.is_gt, ALU.mult))
                    link(v.tensor_tensor(trig[:, 3], trig[:, 3], trig[:, 1], ALU.add))
                    pi = 3.1415925
                    v.tensor_scalar(trig[:, 2:4], trig[:, 2:4], pi, -pi, ALU.min, ALU.max).then_inc(trig_arg, 1)
            dve.wait_ge(sq_done, 1)
            link(v.tensor_scalar(rms[:, 1, 0:2], rms[:, 0, 0:2], 1.0 / QR_RANK, RMS_EPS, ALU.mult, ALU.add))
            v.tensor_scalar(rms[:, 1, 2:4], rms[:, 0, 2:4], 1.0 / KV_RANK, RMS_EPS, ALU.mult,
                            ALU.add).then_inc(rms_var, 1)
            dve.wait_ge(rms_sd, 1)
            link(v.reciprocal(rms[:, 3, :], rms[:, 2, :]))
            b = BLOCK0["o_cq"]
            for t in range(TT):
                ins = v.tensor_scalar(cqs[:, t, :], acc[b % 2][t][:], rms[:, 3, t:t + 1], None, ALU.mult)
            ins.then_inc(acc_free[b % 2], 1)
            ahead(UNIT0["o_cq"], UPB - 1)
            for t in range(TT):
                ins = v.tensor_scalar(ckvs[:, t, :], ckvs[:, t, :], rms[:, 3, 2 + t:3 + t], None, ALU.mult)
            ins.then_inc(c_norm, 1)
            for j in range(UPB):
                m = j - 4
                if 0 <= m < 3:
                    n = TR0["rms"] + m
                    dve.wait_ge(tr_hi, HI0["rms"] + m + 1)
                    for k in range(2):
                        ins = v.scalar_tensor_tensor(out=cTl[:, 2 * m + k, :], in0=trb[n % 2][:, k * T:(k + 1) * T],
                                                     scalar=qkg[:, 2 * m + k:2 * m + k + 1],
                                                     in1=cTh[:, 2 * m + k, :].bitcast(F32),
                                                     op0=ALU.mult, op1=ALU.subtract)
                    ins.then_inc(tr_free, 1)
                ahead(UNIT0["o_kv"], j)
            for j in range(4):
                ahead(UNIT0["qb_nope"], j)
            dve.wait_ge(tr_ready, TR0["kswa"] + 1)
            for h in range(SWA_KV):
                bank_ = trb[TR0["kswa"] % 2]
                v.tensor_copy(kz[0:64, h, 0, :], bank_[0:64, h * T:(h + 1) * T])
                ins = v.tensor_copy(kz[64:P, 1 - h, 1, :], bank_[64:P, h * T:(h + 1) * T])
            ins.then_inc(tr_free, 1)
            for j in range(4):
                ahead(UNIT0["qb_rope"], j)
            b = BLOCK0["qb_rope"]
            dve.wait_ge(acc_free[b % 2], uses(b) + 1)
            dve.wait_ge(trig_done, 1)
            H = ROPE // 2
            for t in range(TT):
                sin, cos = (trig[:, f, t, :].unsqueeze(1).broadcast_to([P, 10, H]) for f in (4, 5))
                x1, x2, y1, y2 = (a[:, t, :, c * H:(c + 1) * H] for a in (qr, qro) for c in range(2))
                v.tensor_tensor(y1, x1, cos, ALU.mult)
                link(v.tensor_tensor(rtmp[:], x2, sin, ALU.mult))
                link(v.tensor_tensor(y1, y1, rtmp[:], ALU.subtract))
                v.tensor_tensor(y2, x2, cos, ALU.mult)
                link(v.tensor_tensor(rtmp[:], x1, sin, ALU.mult))
                ins = v.tensor_tensor(y2, y2, rtmp[:], ALU.add)
                if t == 0:
                    link(ins)
                    ahead(UNIT0["kvb"], 0)
            ins.then_inc(rope_out, 1)
            for j in range(1, 4):
                ahead(UNIT0["kvb"], j)
            for b in range(2):
                for j in range(UPB):
                    if (b, j) == (0, 0):
                        for m in range(3):
                            n = TR0["rope"] + m
                            dve.wait_ge(tr_ready, n + 1)
                            if m < 2:
                                ins = v.tensor_copy(qrT[:, 2 * m:2 * m + 2, :].rearrange("p a b -> p (a b)"),
                                                    trb[n % 2][:])
                            else:
                                for g in range(2):
                                    rows = slice(g * 64, (g + 1) * 64)
                                    ins = v.tensor_copy(krz[rows, g, :], trb[n % 2][rows, 0:T])
                            ins.then_inc(tr_free, 1)
                    else:
                        attention_step(len(FOX), ODD, b * UPB + j - 1, odd_masked)
                    ahead(UNIT0["o_q"] + b * UPB, j)
            b0 = BLOCK0["o_out"]
            for j in range(2 * UPB):
                if 2 * UPB - 1 + j < ODD_STEPS:
                    attention_step(len(FOX), ODD, 2 * UPB - 1 + j, odd_masked)
                if j + 1 in (14, 16):
                    c = j // 15
                    residual(b0 + c, c, 2, 0)
                    residual(b0 + c, c, 2, 1)
                ahead(UNIT0["o_out"], j)
            for c in (2, 3):
                residual_block(UNIT0["o_out"] + c * UPB, b0 + c, c, 2, UPB, norms[2] if c == 3 else None)
            ffn(1)
            for n in range(1, 4):
                norms[3].affine(n)
            residual(BLOCK0["down1"] + 3, 3, 3, 1)
            norms[3].moments(1)
            for n in range(4, 8):
                norms[3].affine(n)


_INS = ['x', 'positions', 'ev_w_in', 'ev_forget_bias', 'ev_conv_w', 'ev_conv_b', 'ev_rgate_w', 'ev_rgate_b',
        'ev_igate_w', 'ev_igate_b', 'ev_lru_lambda', 'ev_w_out', 'od_w_in', 'od_sinks', 'od_q_norm', 'od_w_qb',
        'od_kv_norm', 'od_w_kvb', 'od_w_out', 'ln_mix_g', 'ln_mix_b', 'ffn_w_gate', 'ffn_w_up', 'ffn_w_down',
        'ln_ffn_g', 'ln_ffn_b']
_OUTS = [((1, 256, 2048), 'float32')]


def kernel(**inputs):
    import numpy as _np
    import concourse.bacc as _bacc
    from concourse import mybir as _mybir
    from concourse.bass_utils import run_bass_kernel_spmd as _run

    nc = _bacc.Bacc("TRN2", target_bir_lowering=False, num_devices=1)
    arrays, args = {}, []
    for name in _INS:
        a = _np.ascontiguousarray(inputs[name])
        arrays[f"in_{name}_dram"] = a
        args.append(nc.dram_tensor(f"in_{name}_dram", a.shape, _mybir.dt.from_np(a.dtype), kind="ExternalInput").ap())
    for i, (shape, dtype) in enumerate(_OUTS):
        dt = _mybir.dt.from_np(_np.dtype(dtype))
        args.append(nc.dram_tensor(f"out_{i}_dram", shape, dt, kind="ExternalOutput").ap())
    hybrid_trunk_kernel(nc, *args)
    r = _run(nc, [arrays], core_ids=[0])
    got = tuple(r.results[0][f"out_{i}_dram"] for i in range(len(_OUTS)))
    return got[0]
```
